# Optimizing a Trainium2 kernel written in Bass

```python
import math
import jax, jax.numpy as jnp
from jax import lax
import numpy as np

D_MODEL = 1024
BATCH = 1
SEQ = 128
DEPTH = 2
DEC_BATCH = 1
DEC_SEQ = 256
PAST_LEN = 128

GRID_W = 64
N_EVEN = (DEPTH + 1) // 2
N_ODD = DEPTH // 2
A_HEADS = 4
A_HD = 64
B_HEADS = 8
B_HD = 64
NA_ROWS = 8
NA_COLS = 16
NA_KCB = 2 * NA_COLS
C_HEADS = 4
C_DK = 128
C_DV = 128
C_CHUNK = 64
D_RNN = 512
D_BLOCKS = 8
D_BW = D_RNN // D_BLOCKS
RG_C = 8.0
CONV_W = 4
FF_DENSE = 2816
N_EXPERTS = 8
TOP_K = 2
FF_EXPERT = 2048
ROPE_BASE = 10000.0
EPS = 1e-6
Q_BLOCK = 128
NEG_INF = -1e30
A_W = A_HEADS * 2 * A_HD
B_W = B_HEADS * B_HD
C_W = C_HEADS * C_DK
IN_EVEN = 3 * A_W + 3 * B_W
MIX_EVEN = A_W + B_W
IN_ODD = 4 * C_W + 4 * C_HEADS + 2 * D_RNN
MIX_ODD = C_W + D_RNN
F32 = jnp.float32

kernel_name = 'hybrid_flow_trunk_step'

def rmsnorm(x, g):
    xf = x.astype(F32)
    y = xf * lax.rsqrt(jnp.mean(xf * xf, axis=-1, keepdims=True) + EPS)
    return (y * g.astype(F32)).astype(x.dtype)

def adaln(cvec, w, b):
    return jnp.split(jax.nn.silu(cvec) @ w + b, 6, axis=-1)

def sublayer(x, shift, scale, gate, g_pre, g_post, fn):
    h = rmsnorm(x, g_pre) * (1 + scale[:, None]) + shift[:, None]
    out, aux = fn(h)
    return x + gate[:, None] * rmsnorm(out, g_post), aux

def rope_2d(x):
    S, d = x.shape[1], x.shape[-1]
    half = d // 2
    t = jnp.arange(S)
    pos = jnp.stack([t // GRID_W, t % GRID_W], axis=-1).astype(F32)
    freqs = ROPE_BASE ** (-jnp.arange(0, half, 2, dtype=F32) / half)
    ang = pos[:, :, None] * freqs
    cos = jnp.cos(ang)[None, :, None]
    sin = jnp.sin(ang)[None, :, None]
    xr = x.astype(F32).reshape(x.shape[:-1] + (2, 2, half // 2))
    x1, x2 = xr[..., 0, :], xr[..., 1, :]
    out = jnp.stack([x1 * cos - x2 * sin, x1 * sin + x2 * cos], axis=-2)
    return out.reshape(x.shape).astype(x.dtype)

def map_query_blocks(fn, q):
    B, S = q.shape[:2]
    nb = S // Q_BLOCK
    qb = jnp.moveaxis(q.reshape((B, nb, Q_BLOCK) + q.shape[2:]), 1, 0)
    out = jnp.moveaxis(lax.map(fn, qb), 0, 1)
    return out.reshape((B, S) + out.shape[3:])

def diff_attention(q, k, v, lam_vec, subln_g, lam_init):
    B, S = q.shape[:2]
    lv = lam_vec.astype(F32)
    lam = jnp.exp(jnp.sum(lv[0] * lv[1])) - jnp.exp(jnp.sum(lv[2] * lv[3])) + lam_init

    def block(qb):
        s = jnp.einsum('bqhmd,bkhmd->bhmqk', qb, k).astype(F32) * (A_HD ** -0.5)
        p = jax.nn.softmax(s, axis=-1)
        p = p[:, :, 0] - lam * p[:, :, 1]
        return jnp.einsum('bhqk,bkhe->bqhe', p.astype(v.dtype), v)

    o = map_query_blocks(block, q)
    o = rmsnorm(o, subln_g) * (1.0 - lam_init)
    return o.reshape(B, S, A_W)

def dense_attention(q, k, v):
    B, S = q.shape[:2]

    def block(qb):
        s = jnp.einsum('bqhd,bkhd->bhqk', qb, k).astype(F32) * (B_HD ** -0.5)
        p = jax.nn.softmax(s, axis=-1)
        return jnp.einsum('bhqk,bkhd->bqhd', p.astype(v.dtype), v)

    return map_query_blocks(block, q).reshape(B, S, B_W)

def neighbourhood_attention(q, k, v, k_ctx, v_ctx, rpb):
    B, S, H, d = q.shape
    rows = S // GRID_W
    kr = min(NA_ROWS, rows)
    ncb = GRID_W // NA_COLS
    r = np.arange(rows)
    row_idx = np.clip(r - kr // 2, 0, rows - kr)[:, None] + np.arange(kr)
    jb = np.arange(ncb)
    col_idx = np.clip(jb * NA_COLS - NA_COLS // 2, 0, GRID_W - NA_KCB)[:, None] + np.arange(NA_KCB)
    qcol = jb[:, None] * NA_COLS + np.arange(NA_COLS)
    cstart = np.clip(qcol - NA_COLS // 2, 0, GRID_W - NA_COLS)
    kc = col_idx[:, None, :]
    valid = (kc >= cstart[..., None]) & (kc < cstart[..., None] + NA_COLS)
    dr = row_idx - r[:, None] + NA_ROWS - 1
    dc = np.clip(kc - qcol[..., None] + NA_COLS - 1, 0, 2 * NA_COLS - 2)
    bias = rpb.astype(F32)[:, dr[:, None, None, :, None], dc[None, :, :, None, :]]
    nw = kr * NA_KCB
    bias = jnp.where(valid[None, None, :, :, None, :], bias, NEG_INF).reshape(H, rows, ncb, NA_COLS, nw)
    ri = row_idx[:, None, :, None]
    ci = col_idx[None, :, None, :]
    kw = k.reshape(B, rows, GRID_W, H, d)[:, ri, ci].reshape(B, rows, ncb, nw, H, d)
    vw = v.reshape(B, rows, GRID_W, H, d)[:, ri, ci].reshape(B, rows, ncb, nw, H, d)
    qg = q.reshape(B, rows, ncb, NA_COLS, H, d)
    scale = d ** -0.5
    s_win = jnp.einsum('brjqhd,brjkhd->bhrjqk', qg, kw).astype(F32) * scale + bias[None]
    s_ctx = jnp.einsum('brjqhd,bchd->bhrjqc', qg, k_ctx).astype(F32) * scale
    p = jax.nn.softmax(jnp.concatenate([s_win, s_ctx], axis=-1), axis=-1).astype(v.dtype)
    o = (jnp.einsum('bhrjqk,brjkhd->brjqhd', p[..., :nw], vw)
         + jnp.einsum('bhrjqc,bchd->brjqhd', p[..., nw:], v_ctx))
    return o.reshape(B, S, B_W)

def even_project(h, w_in):
    B, S, _ = h.shape
    qa, ka, va, qb, kb, vb = jnp.split(
        h @ w_in, [A_W, 2 * A_W, 3 * A_W, 3 * A_W + B_W, 3 * A_W + 2 * B_W], axis=-1)
    return (qa.reshape(B, S, A_HEADS, 2, A_HD), ka.reshape(B, S, A_HEADS, 2, A_HD),
            va.reshape(B, S, A_HEADS, 2 * A_HD), qb.reshape(B, S, B_HEADS, B_HD),
            kb.reshape(B, S, B_HEADS, B_HD), vb.reshape(B, S, B_HEADS, B_HD))

def even_mixer_context(h, w_in, w_out, lam_vec, subln_g, lam_init):
    B, S, _ = h.shape
    qa, ka, va, qb, kb, vb = even_project(h, w_in)
    oa = diff_attention(qa, ka, va, lam_vec, subln_g, lam_init)
    ob = dense_attention(qb, kb, vb)
    out = jnp.concatenate([oa, ob], axis=-1) @ w_out
    return out, (ka.reshape(B, S, A_HEADS, 2 * A_HD), va, kb, vb)

def even_mixer_latent(h, ak, av, bk, bv, rpb, w_in, w_out, lam_vec, subln_g, lam_init):
    B, S, _ = h.shape
    qa, ka, va, qb, kb, vb = even_project(h, w_in)
    qa = rope_2d(qa.reshape(B, S, 2 * A_HEADS, A_HD)).reshape(qa.shape)
    ka = rope_2d(ka.reshape(B, S, 2 * A_HEADS, A_HD)).reshape(ka.shape)
    L = ak.shape[1]
    k_all = jnp.concatenate([ka, ak.reshape(B, L, A_HEADS, 2, A_HD).astype(ka.dtype)], axis=1)
    v_all = jnp.concatenate([va, av.astype(va.dtype)], axis=1)
    oa = diff_attention(qa, k_all, v_all, lam_vec, subln_g, lam_init)
    ob = neighbourhood_attention(qb, kb, vb, bk.astype(kb.dtype), bv.astype(vb.dtype), rpb)
    out = jnp.concatenate([oa, ob], axis=-1) @ w_out
    return out, None

def conv_centred(x, w):
    C = x.shape[-1]
    left = (CONV_W - 1) // 2
    right = CONV_W - 1 - left
    return lax.conv_general_dilated(
        x, w.astype(x.dtype)[:, None, :], window_strides=(1,), padding=[(left, right)],
        dimension_numbers=('NWC', 'WIO', 'NWC'), feature_group_count=C)

def mlstm_chunked(q, k, v, i_pre, f_pre, C0, n0, m0):
    B, H, S, _ = q.shape
    L = C_CHUNK
    nc = S // L

    def to_chunks(a):
        return jnp.moveaxis(a.astype(F32).reshape((B, H, nc, L) + a.shape[3:]), 2, 0)

    xs = (to_chunks(q * (C_DK ** -0.5)), to_chunks(k), to_chunks(v), to_chunks(i_pre),
          to_chunks(jax.nn.log_sigmoid(f_pre.astype(F32))))
    causal = jnp.tril(jnp.ones((L, L), dtype=bool))

    def step(carry, chunk):
        C, n, m = carry
        qb, kb, vb, ib, lfb = chunk
        b = jnp.cumsum(lfb, axis=-1)
        dlog = jnp.where(causal, b[..., :, None] - b[..., None, :] + ib[..., None, :], -jnp.inf)
        inter = b + m[..., None]
        m_t = jnp.maximum(inter, jnp.max(dlog, axis=-1))
        w_in = jnp.exp(dlog - m_t[..., None])
        w_st = jnp.exp(inter - m_t)
        s = jnp.einsum('bhtd,bhsd->bhts', qb, kb) * w_in
        num = w_st[..., None] * jnp.einsum('bhtd,bhde->bhte', qb, C) + jnp.einsum('bhts,bhse->bhte', s, vb)
        nq = w_st * jnp.einsum('bhtd,bhd->bht', qb, n) + jnp.sum(s, axis=-1)
        h = num / jnp.maximum(jnp.abs(nq), jnp.exp(-m_t))[..., None]
        b_last = b[..., -1]
        wlog = b_last[..., None] - b + ib
        m_new = jnp.maximum(b_last + m, jnp.max(wlog, axis=-1))
        ws = jnp.exp(wlog - m_new[..., None])
        wc = jnp.exp(b_last + m - m_new)
        C_new = wc[..., None, None] * C + jnp.einsum('bhs,bhsd,bhse->bhde', ws, kb, vb)
        n_new = wc[..., None] * n + jnp.einsum('bhs,bhsd->bhd', ws, kb)
        return (C_new, n_new, m_new), h

    (C, n, m), hs = lax.scan(step, (C0.astype(F32), n0.astype(F32), m0.astype(F32)), xs)
    return jnp.moveaxis(hs, 0, 2).reshape(B, H, S, C_DV), (C, n, m)

def combine_linear(left, right):
    a1, b1 = left
    a2, b2 = right
    return a1 * a2, a2 * b1 + b2

def rglru(x, wa, ba, wx, bx, lam, h0):
    B, S, _ = x.shape
    x = x.astype(F32)
    xb = x.reshape(B, S, D_BLOCKS, D_BW)
    r = jax.nn.sigmoid(jnp.einsum('bsnd,nde->bsne', xb, wa).reshape(B, S, D_RNN) + ba)
    ig = jax.nn.sigmoid(jnp.einsum('bsnd,nde->bsne', xb, wx).reshape(B, S, D_RNN) + bx)
    log_a = -RG_C * r * jax.nn.softplus(-lam.astype(F32))
    a = jnp.exp(log_a)
    u = jnp.sqrt(-jnp.expm1(2.0 * log_a)) * (ig * x)
    u = u.at[:, 0].add(a[:, 0] * h0.astype(F32))
    _, hs = lax.associative_scan(combine_linear, (a, u), axis=1)
    return hs, hs[:, -1]

def zero_states(B):
    return (jnp.zeros((B, 2, C_HEADS, C_DK, C_DV), F32), jnp.zeros((B, 2, C_HEADS, C_DK), F32),
            jnp.zeros((B, 2, C_HEADS), F32), jnp.zeros((B, 2, D_RNN), F32))

def odd_mixer(h, st_C, st_n, st_m, st_h, w_in, gate_b, conv_c, conv_d, conv_d_b,
              rg_wa, rg_ba, rg_wx, rg_bx, rg_lam, norm_g, w_out):
    B, S, _ = h.shape
    qk, v, o, gates, xd, gd = jnp.split(
        h @ w_in, [2 * C_W, 3 * C_W, 4 * C_W, 4 * C_W + 4 * C_HEADS, 4 * C_W + 4 * C_HEADS + D_RNN], axis=-1)
    q, k = jnp.split(jax.nn.silu(conv_centred(qk, conv_c)), 2, axis=-1)

    def heads(a):
        return a.reshape(B, S, C_HEADS, -1).transpose(0, 2, 1, 3)

    q, k, v = heads(q), heads(k), heads(v)
    g = (gates + gate_b).reshape(B, S, 4, C_HEADS).transpose(2, 0, 3, 1)
    hf, (Cf, nf, mf) = mlstm_chunked(q, k, v, g[0], g[1], st_C[:, 0], st_n[:, 0], st_m[:, 0])
    hb, (Cb, nb, mb) = mlstm_chunked(jnp.flip(q, 2), jnp.flip(k, 2), jnp.flip(v, 2), jnp.flip(g[2], 2),
                                     jnp.flip(g[3], 2), st_C[:, 1], st_n[:, 1], st_m[:, 1])
    hc = rmsnorm(hf + jnp.flip(hb, 2), norm_g)
    hc = hc.transpose(0, 2, 1, 3).reshape(B, S, C_W) * jax.nn.sigmoid(o)
    xc = conv_centred(xd, conv_d) + conv_d_b
    rf, hfin_f = rglru(xc, rg_wa[0], rg_ba[0], rg_wx[0], rg_bx[0], rg_lam[0], st_h[:, 0])
    rb, hfin_b = rglru(jnp.flip(xc, 1), rg_wa[1], rg_ba[1], rg_wx[1], rg_bx[1], rg_lam[1], st_h[:, 1])
    hd = (rf + jnp.flip(rb, 1)) * jax.nn.gelu(gd)
    out = (jnp.concatenate([hc, hd], axis=-1) @ w_out).astype(h.dtype)
    states = (jnp.stack([Cf, Cb], axis=1), jnp.stack([nf, nb], axis=1),
              jnp.stack([mf, mb], axis=1), jnp.stack([hfin_f, hfin_b], axis=1))
    return out, states

def swiglu(x, w1, w3, w2):
    return (jax.nn.silu(x @ w1) * (x @ w3)) @ w2

def moe_swiglu(h, router_w, router_b, w1, w3, w2):
    B, S, D = h.shape
    t = h.reshape(B * S, D)
    logits = (t @ router_w + router_b).astype(F32)
    top_v, top_i = lax.top_k(logits, TOP_K)
    gate = jax.nn.softmax(top_v, axis=-1)
    dense_gate = jnp.sum(jax.nn.one_hot(top_i, N_EXPERTS, dtype=F32) * gate[..., None], axis=1).astype(t.dtype)
    out = jnp.zeros_like(t)
    for e in range(N_EXPERTS):
        out = out + dense_gate[:, e:e + 1] * swiglu(t, w1[e], w3[e], w2[e])
    return out.reshape(B, S, D)

def setup_inputs(seed: int = 0) -> dict:
    key = jax.random.key(seed)
    ks = iter(jax.random.split(key, 64))

    def nrm(shape, scale=1.0):
        return jax.random.normal(next(ks), shape, F32) * scale

    def gain(shape):
        return 1.0 + nrm(shape, 0.05)

    u = jax.random.uniform(next(ks), (N_ODD, 2, D_RNN), F32, 0.9, 0.999)
    s = u ** (1.0 / RG_C)
    rg_lam = jnp.log(s) - jnp.log1p(-s)
    gate_offset = jnp.array([0.0, 4.0, 0.0, 4.0], F32)[:, None]
    c_gate_b = (nrm((N_ODD, 4, C_HEADS), 0.1) + gate_offset).reshape(N_ODD, 4 * C_HEADS)
    return {
        'x_prompt': nrm((BATCH, SEQ, D_MODEL)),
        'x_sample': nrm((DEC_BATCH, DEC_SEQ, D_MODEL)),
        'c': nrm((DEC_BATCH, D_MODEL)),
        'cache_a_k': nrm((DEC_BATCH, N_EVEN, PAST_LEN, A_HEADS, 2 * A_HD)),
        'cache_a_v': nrm((DEC_BATCH, N_EVEN, PAST_LEN, A_HEADS, 2 * A_HD)),
        'cache_b_k': nrm((DEC_BATCH, N_EVEN, PAST_LEN, B_HEADS, B_HD)),
        'cache_b_v': nrm((DEC_BATCH, N_EVEN, PAST_LEN, B_HEADS, B_HD)),
        'state_c_C': nrm((DEC_BATCH, N_ODD, 2, C_HEADS, C_DK, C_DV), 0.5),
        'state_c_n': nrm((DEC_BATCH, N_ODD, 2, C_HEADS, C_DK), 0.5),
        'state_c_m': nrm((DEC_BATCH, N_ODD, 2, C_HEADS)),
        'state_d_h': nrm((DEC_BATCH, N_ODD, 2, D_RNN), 0.5),
        'c_ctx': nrm((D_MODEL,)),
        'mod_w': nrm((DEPTH, D_MODEL, 6 * D_MODEL), 0.5 * D_MODEL ** -0.5),
        'mod_b': nrm((DEPTH, 6 * D_MODEL), 0.02),
        'norm_g': gain((DEPTH, 4, D_MODEL)),
        'w_in_even': nrm((N_EVEN, D_MODEL, IN_EVEN), D_MODEL ** -0.5),
        'w_out_even': nrm((N_EVEN, MIX_EVEN, D_MODEL), MIX_EVEN ** -0.5),
        'a_lam': nrm((N_EVEN, 4, A_HD), 0.1),
        'a_subln_g': gain((N_EVEN, 2 * A_HD)),
        'b_rpb': nrm((N_EVEN, B_HEADS, 2 * NA_ROWS - 1, 2 * NA_COLS - 1), 0.5),
        'ff_w1': nrm((N_EVEN, D_MODEL, FF_DENSE), D_MODEL ** -0.5),
        'ff_w3': nrm((N_EVEN, D_MODEL, FF_DENSE), D_MODEL ** -0.5),
        'ff_w2': nrm((N_EVEN, FF_DENSE, D_MODEL), FF_DENSE ** -0.5),
        'w_in_odd': nrm((N_ODD, D_MODEL, IN_ODD), D_MODEL ** -0.5),
        'c_gate_b': c_gate_b,
        'conv_c': nrm((N_ODD, CONV_W, 2 * C_W), 0.5),
        'conv_d': nrm((N_ODD, CONV_W, D_RNN), 0.5),
        'conv_d_b': nrm((N_ODD, D_RNN), 0.02),
        'rg_wa': nrm((N_ODD, 2, D_BLOCKS, D_BW, D_BW), D_BW ** -0.5),
        'rg_ba': nrm((N_ODD, 2, D_RNN), 0.1),
        'rg_wx': nrm((N_ODD, 2, D_BLOCKS, D_BW, D_BW), D_BW ** -0.5),
        'rg_bx': nrm((N_ODD, 2, D_RNN), 0.1),
        'rg_lam': rg_lam,
        'c_norm_g': gain((N_ODD, C_DV)),
        'w_out_odd': nrm((N_ODD, MIX_ODD, D_MODEL), MIX_ODD ** -0.5),
        'router_w': nrm((N_ODD, D_MODEL, N_EXPERTS), D_MODEL ** -0.5),
        'router_b': nrm((N_ODD, N_EXPERTS), 0.01),
        'moe_w1': nrm((N_ODD, N_EXPERTS, D_MODEL, FF_EXPERT), D_MODEL ** -0.5),
        'moe_w3': nrm((N_ODD, N_EXPERTS, D_MODEL, FF_EXPERT), D_MODEL ** -0.5),
        'moe_w2': nrm((N_ODD, N_EXPERTS, FF_EXPERT, D_MODEL), FF_EXPERT ** -0.5),
    }

def reference(x_prompt, x_sample, c, cache_a_k, cache_a_v, cache_b_k, cache_b_v,
              state_c_C, state_c_n, state_c_m, state_d_h, c_ctx, mod_w, mod_b, norm_g,
              w_in_even, w_out_even, a_lam, a_subln_g, b_rpb, ff_w1, ff_w3, ff_w2,
              w_in_odd, c_gate_b, conv_c, conv_d, conv_d_b, rg_wa, rg_ba, rg_wx, rg_bx, rg_lam,
              c_norm_g, w_out_odd, router_w, router_b, moe_w1, moe_w3, moe_w2):
    y_p = x_prompt
    y_s = x_sample
    new_a_k, new_a_v, new_b_k, new_b_v = [], [], [], []
    new_c_C, new_c_n, new_c_m, new_d_h = [], [], [], []
    for l in range(DEPTH):
        mp = adaln(c_ctx[None], mod_w[l], mod_b[l])
        ms = adaln(c, mod_w[l], mod_b[l])
        g = norm_g[l]
        if l % 2 == 0:
            e = l // 2
            lam_init = 0.8 - 0.6 * math.exp(-0.3 * l)
            ew = (w_in_even[e], w_out_even[e], a_lam[e], a_subln_g[e], lam_init)
            y_p, kv = sublayer(y_p, mp[0], mp[1], mp[2], g[0], g[1],
                               lambda h: even_mixer_context(h, *ew))
            y_s, _ = sublayer(y_s, ms[0], ms[1], ms[2], g[0], g[1],
                              lambda h: even_mixer_latent(h, cache_a_k[:, e], cache_a_v[:, e], cache_b_k[:, e],
                                                          cache_b_v[:, e], b_rpb[e], *ew))
            new_a_k.append(kv[0])
            new_a_v.append(kv[1])
            new_b_k.append(kv[2])
            new_b_v.append(kv[3])
            ffn = lambda h: (swiglu(h, ff_w1[e], ff_w3[e], ff_w2[e]), None)
        else:
            j = l // 2
            ow = (w_in_odd[j], c_gate_b[j], conv_c[j], conv_d[j], conv_d_b[j], rg_wa[j], rg_ba[j],
                  rg_wx[j], rg_bx[j], rg_lam[j], c_norm_g[j], w_out_odd[j])
            y_p, st = sublayer(y_p, mp[0], mp[1], mp[2], g[0], g[1],
                               lambda h: odd_mixer(h, *zero_states(h.shape[0]), *ow))
            y_s, _ = sublayer(y_s, ms[0], ms[1], ms[2], g[0], g[1],
                              lambda h: odd_mixer(h, state_c_C[:, j], state_c_n[:, j], state_c_m[:, j],
                                                  state_d_h[:, j], *ow))
            new_c_C.append(st[0])
            new_c_n.append(st[1])
            new_c_m.append(st[2])
            new_d_h.append(st[3])
            ffn = lambda h: (moe_swiglu(h, router_w[j], router_b[j], moe_w1[j], moe_w3[j], moe_w2[j]), None)
        y_p, _ = sublayer(y_p, mp[3], mp[4], mp[5], g[2], g[3], ffn)
        y_s, _ = sublayer(y_s, ms[3], ms[4], ms[5], g[2], g[3], ffn)
    new_a_k = jnp.stack(new_a_k, axis=1)
    new_a_v = jnp.stack(new_a_v, axis=1)
    new_b_k = jnp.stack(new_b_k, axis=1)
    new_b_v = jnp.stack(new_b_v, axis=1)
    new_c_C = jnp.stack(new_c_C, axis=1)
    new_c_n = jnp.stack(new_c_n, axis=1)
    new_c_m = jnp.stack(new_c_m, axis=1)
    new_d_h = jnp.stack(new_d_h, axis=1)
    return (y_p, y_s, new_a_k, new_a_v, new_b_k, new_b_v, new_c_C, new_c_n, new_c_m, new_d_h)


_drawn_inputs = setup_inputs


def setup_inputs(seed=0):
    import zlib

    import numpy as np

    out = dict(_drawn_inputs(seed))
    spreads = {}
    factors = {'state_c_C': 4.305,
     'state_c_n': 8.0,
     'state_c_m': 5.218,
     'rg_ba': 3.219,
     'c_norm_g': 14.798,
     'router_b': 3.938,
     'state_d_h': 4.644}
    for name, (base, spread) in spreads.items():
        noise = np.random.default_rng([zlib.crc32(name.encode()), seed]).standard_normal(out[name].shape)
        drawn = base * np.exp(spread * noise) if base else spread * noise
        out[name] = __import__('jax').numpy.asarray(drawn.astype(out[name].dtype))
    for name, factor in factors.items():
        out[name] = (out[name] * factor).astype(out[name].dtype)
    return out
```

```python
import math
from contextlib import ExitStack

import numpy as np
import concourse.bass as bass
from concourse import mybir

F32 = mybir.dt.float32
I32 = mybir.dt.int32
ALU = mybir.AluOpType
ACT = mybir.ActivationFunctionType
AX = mybir.AxisListType

P = 128
D = 1024
KD = D // P
NT = 3
T = NT * P
CONDS = 2
GRID_W = 64
A_HEADS, B_HEADS, HD = 4, 8, 64
C_HEADS = 4
FF = 2816
KF = FF // P
E_FF = 2048
KE = E_FF // P
N_EXP = 8
EPS = 1e-6
NEG = -1e30
LAM_INIT = 0.8 - 0.6 * math.exp(-0.3 * 0)
C_SCALE = 128 ** -0.5
RING = 3
MAX_ITEMS = (2 * T) // P + N_EXP - 1
SEG = (1, 132, 260)
PAD = 390
NPAD = 387

C_ID, C_ONE, C_ROT, C_COS, C_SIN, C_MF, C_MB = 0, 128, 384, 512, 768, 1024, 1152
C_SEL, C_CUM, C_TIE, C_IOTA, C_W = 1280, 2304, 2432, 2496, 2624
C_N = C_W + MAX_ITEMS * N_EXP


def shape_constants():
    c = np.zeros((P, C_N), np.float32)
    i = np.arange(P)
    c[:, C_ID:C_ID + P] = np.eye(P)
    c[:, C_ONE:C_ONE + 256] = 1.0
    j = (i // 16) % 2
    rot = np.zeros((P, P), np.float32)
    for m in range(P):
        if j[m] == 0:
            rot[m + 16, m] = -1.0
        else:
            rot[m - 16, m] = 1.0
    c[:, C_ROT:C_ROT + P] = rot
    t = np.arange(256)
    pos = np.stack([t // GRID_W, t % GRID_W]).astype(np.float32)
    freq = (10000.0 ** (-np.arange(0, 32, 2, dtype=np.float32) / 32)).astype(np.float32)
    ang = (pos[(i % 64) // 32] * freq[i % 16][:, None]).astype(np.float32)
    c[:, C_COS:C_COS + 256] = np.cos(ang)
    c[:, C_SIN:C_SIN + 256] = np.sin(ang)
    c[:, C_MF:C_MF + P] = np.where(i[None] >= i[:, None], 0.0, NEG)
    c[:, C_MB:C_MB + P] = np.where(i[None] <= i[:, None], 0.0, NEG)
    for u in range(8):
        c[32 * (u // 4) + u % 4, C_SEL + u * P:C_SEL + (u + 1) * P] = 1.0
    c[:, C_CUM:C_CUM + P] = i[:, None] < i[None]
    e = np.arange(N_EXP)
    c[:, C_TIE:C_TIE + 64] = (e[None] < e[:, None]).astype(np.float32).reshape(-1)
    c[:, C_IOTA:C_IOTA + P] = i[None]
    c[:, C_W:C_N] = np.repeat(np.arange(MAX_ITEMS), N_EXP)[None]
    return c


def trunk_step(nc, I, O, dbg=None, stop=99):
    with ExitStack() as ctx:
        def sb(name, shape, dt=F32):
            return ctx.enter_context(nc.sbuf_tensor(name, shape, dt))

        def sem(name):
            return ctx.enter_context(nc.semaphore(name))

        bank = [ctx.enter_context(nc.psum_tensor(f"bank{i}", [P, 512], F32)) for i in range(8)]

        ring = sb("ring", [P, RING, 4096])
        x = sb("x", [P, NT, D])
        xn = sb("xn", [P, NT, D])
        ht = sb("ht", [P, KD, T])
        gb = sb("gb", [P, CONDS, D])
        cst = sb("cst", [P, C_N])
        rowt = sb("rowt", [P, 3, P])
        cols = sb("cols", [P, 3 * P])
        sc = sb("sc", [P, KD, CONDS])
        modc = sb("modc", [P, 2, 48, CONDS])
        acol = sb("acol", [P, 4, KD, CONDS])
        gcol = sb("gcol", [P, 4, KD, CONDS])
        ss = sb("ss", [P, 4, 3])
        sd = sb("sd", [P, 4, 3])
        rs = sb("rs", [P, 4, 3])
        ss2 = sb("ss2", [P, 4, 6])
        ssum = sb("ssum", [P, 4, 3])
        sd2 = sb("sd2", [P, 4, 3])
        rs2 = sb("rs2", [P, 4, 3])
        epsc = sb("epsc", [P, 1])
        hn = sb("hn", [P, 2, 3, 12])
        jk = sb("jk", [P, 2, 512])
        arena = sb("arena", [P, 20800])
        at_f = [0]

        def carve(n, at=None):
            o = at_f[0] if at is None else at
            if at is None:
                at_f[0] += n
            assert o + n <= 20800, (o, n)
            return arena[:, o:o + n]

        shear = nc.dram_tensor("shear", [B_HEADS, GRID_W, 7, GRID_W], F32, kind="Internal").ap()
        ident = cst[:, C_ID:C_ID + P]
        ones = cst[:, C_ONE:C_ONE + P]

        qat = carve(1536).rearrange("p (h t) -> p h t", h=4)
        kat = carve(2048).rearrange("p (h t) -> p h t", h=4)
        va = carve(2048).rearrange("p (t e) -> p t e", t=4)
        qbt = carve(1536).rearrange("p (h t) -> p h t", h=4)
        kbt = carve(2048).rearrange("p (h t) -> p h t", h=4)
        vb = carve(2048).rearrange("p (t e) -> p t e", t=4)
        bias = carve(6144).rearrange("p (q h k) -> p q h k", q=2, h=8)
        kcache = jk
        SQ0 = at_f[0]
        prob = carve(1536).rearrange("p (s k) -> p s k", s=4)
        pts = carve(768).rearrange("p (s k) -> p s k", s=2)
        ropec = pts[:, 0, 0:256], pts[:, 1, 0:256]
        ropes = kcache[:, 0, 0:256], kcache[:, 0, 256:512]
        knew = ht[:, 0:3, :].rearrange("p a b -> p (a b)")[:, 0:1024].rearrange("p (a e) -> p a e", a=2)
        heads = xn
        alam = sb("alam", [P, 256])
        lamc = sb("lamc", [P, 6])
        subg = sb("subg", [P, 2, P])
        nmx = sb("nmx", [P, 48])
        lsum = sb("lsum", [P, 48])
        rl = sb("rl", [P, 48])

        at_f[0] = 0
        actt = carve(KF * T).rearrange("p (f t) -> p f t", f=KF)
        silt = carve(2 * T).rearrange("p (s t) -> p s t", s=2)

        at_f[0] = 0
        qkin = carve(8 * PAD).rearrange("p (n t) -> p n t", n=8)
        qkc = carve(8 * PAD).rearrange("p (n t) -> p n t", n=8)
        gd = carve(4 * T).rearrange("p (n t) -> p n t", n=4)
        c0 = carve(8 * 129).rearrange("p (u e) -> p u e", u=8)
        shared = at_f[0]
        xdin = carve(4 * PAD).rearrange("p (n t) -> p n t", n=4)
        xc = carve(4 * PAD).rearrange("p (n t) -> p n t", n=4)
        rgb = [carve(4 * PAD).rearrange("p (n t) -> p n t", n=4) for _ in range(4)]
        wrg = carve(16 * P).rearrange("p (d g n m) -> p d g n m", d=2, g=2, n=4)
        hfw = xdin
        at_f[0] = shared
        vaug = carve(NT * 4 * 129).rearrange("p (t h e) -> p t h e", t=NT, h=4)
        sigo = carve(NT * 512).rearrange("p (t e) -> p t e", t=NT)
        rows = carve(4 * T)[0:36, :].rearrange("p (k t) -> p k t", k=4)
        rwork = carve(7 * T)[0:36, :].rearrange("p (k t) -> p k t", k=7)
        rowsall = arena[0:36, shared + NT * 4 * 129 + NT * 512:shared + NT * 4 * 129 + NT * 512 + 11 * T]
        SQ1 = at_f[0]
        wt = carve(2 * 512).rearrange("p (s k) -> p s k", s=2)
        sw = carve(2 * 512).rearrange("p (s k) -> p s k", s=2)
        ktok = carve(512).rearrange("p (h e) -> p h e", h=4)
        kws = carve(2 * P).rearrange("p (s e) -> p s e", s=2)
        inter = carve(2 * 258).rearrange("p (s e) -> p s e", s=2)
        num = carve(258)
        colr = carve(9 * 36).rearrange("p (k r) -> p k r", k=9)
        den = sb("den", [P, 2, 3])
        cout = sb("cout", [P, 2, 129])
        wg = sb("wg", [P, KD, 16])
        wgp = sb("wgp", [P, KD, 2, 36])
        gbias = sb("gbias", [36, 2])
        m0 = sb("m0", [36, 1])
        sp = sb("sp", [P, 6, 8])
        fincols = sb("fincols", [P, 16])
        finrows = sb("finrows", [8, 2, P])

        at_f[0] = 0
        htok = xn
        yacc = carve(NT * D).rearrange("p (t d) -> p t d", t=NT)
        xg = carve(D).rearrange("p (k s) -> p k s", k=KD)
        act_e = carve(KE * P).rearrange("p (f s) -> p f s", f=KE)
        sil_e = carve(2 * P).rearrange("p (b s) -> p b s", b=2)
        og = carve(D)
        onehot = carve(NT * P).rearrange("p (t s) -> p t s", t=NT)
        gated = carve(NT * P).rearrange("p (t s) -> p t s", t=NT)
        gtmp = carve(NT * P).rearrange("p (t s) -> p t s", t=NT)
        scat = carve(NT * P).rearrange("p (t s) -> p t s", t=NT)
        slot = carve(P)
        rw = sb("rw", [P, KD, N_EXP])
        rb = sb("rb", [P, N_EXP])
        lg = sb("lg", [P, NT, N_EXP])
        cmp = sb("cmp", [P, 2, 64])
        rank = sb("rank", [P, NT, N_EXP])
        oh = sb("oh", [P, 3, NT, N_EXP])
        gp = sb("gp", [P, NT, N_EXP])
        tk = sb("tk", [P, 8, NT])
        nb = sb("nb", [P, 6, N_EXP])
        ewf = sb("ewf", [1, MAX_ITEMS * N_EXP])
        ew1 = sb("ew1", [1, MAX_ITEMS + 1])
        ewi = sb("ewi", [1, MAX_ITEMS + 1], I32)

        def vec(ap, pat, **kw):
            return ap.rearrange(pat, **kw)

        row_params = [
            ("c_ctx", 8, vec(I["c_ctx"], "(k p) -> k p", p=P)),
            ("c", 8, vec(I["c"], "b (k p) -> (b k) p", p=P)),
            ("mod_b", 96, vec(I["mod_b"], "l (k p) -> (l k) p", p=P)),
            ("norm_g", 64, vec(I["norm_g"], "l g (k p) -> (l g k) p", p=P)),
            ("conv_c", 32, vec(I["conv_c"], "o j (k p) -> (o j k) p", p=P)),
            ("conv_d", 16, vec(I["conv_d"], "o j (k p) -> (o j k) p", p=P)),
            ("conv_d_b", 4, vec(I["conv_d_b"], "o (k p) -> (o k) p", p=P)),
            ("rg_ba", 8, vec(I["rg_ba"], "o d (k p) -> (o d k) p", p=P)),
            ("rg_bx", 8, vec(I["rg_bx"], "o d (k p) -> (o d k) p", p=P)),
            ("rg_lam", 8, vec(I["rg_lam"], "o d (k p) -> (o d k) p", p=P)),
            ("state_d_h", 8, vec(I["state_d_h"], "b o d (k p) -> (b o d k) p", p=P)),
            ("state_c_n", 8, vec(I["state_c_n"], "b o d h k -> (b o d h) k")),
        ]
        col, row_dmas, at = {}, [], 0
        for name, n, src in row_params:
            col[name] = at
            done = 0
            while done < n:
                m = min(n - done, P - at % P)
                row_dmas.append((at // P, at % P, m, src[done:done + m, :]))
                done += m
                at += m
        n_rows = at
        last_rows = n_rows - 2 * P

        def cut(w, c0_, n):
            return w.rearrange("(k p) n -> p k n", p=P)[:, :, c0_:c0_ + n]

        def rows_cut(w, k0, n):
            return w.rearrange("(k p) n -> p k n", p=P)[:, k0:k0 + n, :]

        def mod_panel(m):
            return ("mod", m), [("k512", cut(I["mod_w"][m // 12], (m % 12) * 512, 512))]

        panels = [mod_panel(m) for m in range(6)]
        panels += [(("in0", j), [("k512", cut(I["w_in_even"][0], 512 * j, 512))]) for j in range(6)]
        panels += [mod_panel(m) for m in range(6, 24)]
        panels += [(("out0", j), [("k512", cut(I["w_out_even"][0], 512 * j, 512))]) for j in range(2)]
        panels += [(("up", j), [("lo256", cut(I["ff_w1"][0], 256 * j, 256)),
                                ("hi256", cut(I["ff_w3"][0], 256 * j, 256))]) for j in range(KF // 2)]
        panels += [(("down", j), [("rows", rows_cut(I["ff_w2"][0], 4 * j, min(4, KF - 4 * j)))])
                   for j in range((KF + 3) // 4)]
        for j, c_ in enumerate((2064, 2576, 0, 512, 1024, 1536)):
            panels.append((("in1", j), [("k512", cut(I["w_in_odd"][0], c_, 512))]))
        panels += [(("out1", j), [("k512", cut(I["w_out_odd"][0], 512 * j, 512))]) for j in range(2)]
        UP, DOWN = E_FF // 256, KE // 4
        ITEM = UP + DOWN
        number = {key: i for i, (key, _) in enumerate(panels)}
        NP0 = len(panels)
        landed = [0] * RING
        need = []
        for i, (_, parts) in enumerate(panels):
            landed[i % RING] += 16 * len(parts)
            need.append(landed[i % RING])
        slot_item = [0] * RING
        item_need = []
        for j in range(ITEM):
            slot_item[(NP0 + j) % RING] += 16 * (2 if j < UP else 1)
            item_need.append(landed[(NP0 + j) % RING] + slot_item[(NP0 + j) % RING])

        def place(i, where, n=4):
            r = ring[:, i % RING, :]
            if where == "rows":
                return r[:, 0:n * D].rearrange("p (k n) -> p k n", k=n)
            r = r.rearrange("p (k n) -> p k n", k=KD)
            return {"k512": r, "lo256": r[:, :, 0:256], "hi256": r[:, :, 256:512]}[where]

        x_in, cst_in, rows_in = sem("x_in"), sem("cst_in"), sem("rows_in")
        small_in, even_in, bias_in = sem("small_in"), sem("even_in"), sem("bias_in")
        odd_in, c0_in, wrg_in, router_in = sem("odd_in"), sem("c0_in"), sem("wrg_in"), sem("router_in")
        panel_in = [sem(f"panel_in{i}") for i in range(RING)]
        zeroed, masked = sem("zeroed"), sem("masked")
        rows_turned, cols_ready, sc_ready = sem("rows_turned"), sem("cols_ready"), sem("sc_ready")
        mod_done, mod_added, gains_ready = sem("mod_done"), sem("mod_added"), sem("gains_ready")
        x_ready, roots_ready, xn_ready = sem("x_ready"), sem("roots_ready"), sem("xn_ready")
        xn_turned, ht_act, ht_dve = sem("xn_turned"), sem("ht_act"), sem("ht_dve")
        gb_made, gb_kept = sem("gb_made"), sem("gb_kept")
        proj_done, proj_act, proj_dve = sem("proj_done"), sem("proj_act"), sem("proj_dve")
        aux_done, aux_kept = sem("aux_done"), sem("aux_kept")
        cos_part, rot_done, roped = sem("cos_part"), sem("rot_done"), sem("roped")
        lam_sums, lam_exps = sem("lam_sums"), sem("lam_exps")
        scores_done, max_ready, exp_done = sem("scores_done"), sem("max_ready"), sem("exp_done")
        probs_ready, probs_turned, pts_ready = sem("probs_ready"), sem("probs_turned"), sem("pts_ready")
        pv_done, o_kept = sem("pv_done"), sem("o_kept")
        hsq_ready, hsum_ready, hroot_ready, heads_ready = (
            sem("hsq_ready"), sem("hsum_ready"), sem("hroot_ready"), sem("heads_ready"))
        o_turned, ot_act, ot_dve = sem("o_turned"), sem("ot_act"), sem("ot_dve")
        out_done, sq2_ready, sum2_ready, root2_ready = (
            sem("out_done"), sem("sq2_ready"), sem("sum2_ready"), sem("root2_ready"))
        up_done, gate_done, silu_ready, prod_ready = (
            sem("up_done"), sem("gate_done"), sem("silu_ready"), sem("prod_ready"))
        act_step, dve_step, pool_step = sem("act_step"), sem("dve_step"), sem("pool_step")
        stored = sem("stored")
        xc_ready, rg_done, rg_act = sem("xc_ready"), sem("rg_done"), sem("rg_act")
        rg_exps, rg_ratio, rg_root, rg_free = sem("rg_exps"), sem("rg_ratio"), sem("rg_root"), sem("rg_free")
        sp_abs, sp_exp, wgp_ready = sem("sp_abs"), sem("sp_exp"), sem("wgp_ready")
        conv_ready, qk_ready = sem("conv_ready"), sem("qk_ready")
        gates_done, row_abs, row_exp, rows_m, rows_exp = (
            sem("gates_done"), sem("row_abs"), sem("row_exp"), sem("rows_m"), sem("rows_exp"))
        rows_turned2, colr_ready, ktok_done, ktok_kept = (
            sem("rows_turned2"), sem("colr_ready"), sem("ktok_done"), sem("ktok_kept"))
        vo_kept = sem("vo_kept")
        st_done, nm_done, wlog_ready, w_ready, sw_ready = (
            sem("st_done"), sem("nm_done"), sem("wlog_ready"), sem("w_ready"), sem("sw_ready"))
        kws_ready, mm_done, inter_kept, h_ready = sem("kws_ready"), sem("mm_done"), sem("inter_kept"), sem("h_ready")
        cout_kept, c_stored, fin_ready, fin_turned, fin_kept = (
            sem("cout_kept"), [sem("c_stored0"), sem("c_stored1")], sem("fin_ready"), sem("fin_turned"), sem("fin_kept"))
        logits_done, tok_turned, htok_ready = sem("logits_done"), sem("tok_turned"), sem("htok_ready")
        e1_in, e1_ready, sel_ready, pos_done, plan_ready = (
            sem("e1_in"), sem("e1_ready"), sem("sel_ready"), sem("pos_done"), sem("plan_ready"))
        item_step, yadd, rates_ready, down_done = sem("item_step"), sem("yadd"), sem("rates_ready"), sem("down_done")
        hot_ready, gath_done, xg_ready, gated_turned, scat_ready = (
            sem("hot_ready"), sem("gath_done"), sem("xg_ready"), sem("gated_turned"), sem("scat_ready"))
        eup_done, esilu_ready, eprod_ready = sem("eup_done"), sem("esilu_ready"), sem("eprod_ready")
        og_ready, scat_done, yacc_ready = (
            sem("og_ready"), sem("scat_done"), sem("yacc_ready"))

        shear_in = sem("shear_in")
        even_items = ([("qa", n, "A") for n in range(4)] + [("ka", n, "D") for n in range(4)] +
                      [("va", t, "A") for t in range(3)] + [("qb", n, "A") for n in range(4)] +
                      [("kb", n, "D") for n in range(4)] + [("vb", t, "A") for t in range(3)])
        odd_items = ([("xd", n, "AD"[n % 2]) for n in range(4)] + [("gd", n, "A") for n in range(4)] +
                     [("rg0", n, "A") for n in range(8)] + [("q", n, "AD"[n % 2]) for n in range(4)] +
                     [("rg1", n, "A") for n in range(8)] + [("k", n, "AD"[n % 2]) for n in range(4)] +
                     [("v", t, "A") for t in range(3)] + [("o", t, "A") for t in range(3)])
        items = even_items + odd_items
        index = {it[:2]: i for i, it in enumerate(items)}

        def kept_by(i):
            out = []
            if "A" in items[i][2]:
                out.append((proj_act, sum("A" in it[2] for it in items[:i + 1])))
            if "D" in items[i][2]:
                out.append((proj_dve, sum("D" in it[2] for it in items[:i + 1])))
            return out

        def wait_kept(eng, i):
            for s_, v_ in kept_by(i):
                eng.wait_ge(s_, v_)

        units = [("a", h, t, 2 * (3 * h + t)) for h in range(A_HEADS) for t in range(NT)]
        units += [("b", h, t, 24 + 3 * h + t) for h in range(B_HEADS) for t in range(NT)]
        NU = len(units)

        def keys(t):
            return (0, P) if t == 0 else (P, 4 * P)

        def slots(u):
            k_, _, _, s_ = units[u]
            return (s_, s_ + 1) if k_ == "a" else (s_,)

        def mod_bank(m):
            return 5 if m < 6 and m % 2 else 7

        def mod_at(i):
            return 6 + i // 2 if i % 2 == 0 and i // 2 < 18 else None

        munits = [(h, d) for h in range(C_HEADS) for d in range(2)]
        blocks = {0: ((0, 0, 0), (1, 1, P), (1, 2, 2 * P), (2, 2, 3 * P)),
                  1: ((0, 0, 0), (1, 1, P), (2, 1, 2 * P), (2, 2, 3 * P))}
        ALOG, WST, ENM, WS = 0, 3, 5, 8

        OUT_BASE = {0: 0, 2: 6}
        N_DOWN0 = (KF + 3) // 4
        SCATTER = ((1, 0), (1, 1), (2, 0), (0, 0), (0, 1), (2, 1))
        SCAT_BANK = (2, 3, 4, 0, 1, 5)
        ITEM_STEPS = 15
        sq_even = arena[:, SQ0:SQ0 + NT * 512]
        sq_odd = arena[:, SQ1:SQ1 + NT * 512]

        def released(i):
            (what, j) = panels[i][0]
            if what == "mod":
                return mod_done, j + 1
            if what == "up":
                return up_done, 2 * (j + 1)
            if what == "down":
                return down_done, j + 1
            if what in ("out0", "out1"):
                return out_done, OUT_BASE[2 * int(what[3])] + 3 * (j + 1)
            last = [("qa", 3), ("ka", 3), ("va", 2), ("qb", 3), ("kb", 3), ("vb", 2)] if what == "in0" else \
                   [("xd", 3), ("gd", 3), ("q", 3), ("k", 3), ("v", 2), ("o", 2)]
            return proj_done, index[last[j]] + 1

        block = ctx.enter_context(nc.Block())

        @block.sync
        def _(sp_):
            sp_.dma_start(x[:, 0, :], I["x_prompt"][0]).then_inc(x_in, 16)
            sp_.dma_start(x[:, 1:3, :], I["x_sample"][0].rearrange("(t p) d -> p t d", p=P)).then_inc(x_in, 16)
            for i, (_, parts) in enumerate(panels):
                if i >= RING:
                    sp_.wait_ge(*released(i - RING))
                for where, src in parts:
                    sp_.dma_start(place(i, where, src.shape[1]), src).then_inc(panel_in[i % RING], 16)
            if stop < 4:
                sp_.wait_ge(x_ready, 3 * stop)
                sp_.dma_start(O[0][0], x[:, 0, :]).then_inc(stored, 16)
                sp_.dma_start(O[1][0].rearrange("(t p) d -> p t d", p=P), x[:, 1:3, :]).then_inc(stored, 16)
                return
            for i in range(NP0 - RING, NP0):
                sp_.wait_ge(*released(i))
            sp_.wait_ge(plan_ready, 1)
            n_work = sp_.value_load(ewi[0:1, MAX_ITEMS:MAX_ITEMS + 1], min_val=1, max_val=MAX_ITEMS)
            with sp_.Fori(0, n_work) as w:
                e = sp_.value_load(ewi[0:1, bass.ds(w, 1)], min_val=0, max_val=N_EXP - 1)
                for j in range(ITEM):
                    i = NP0 + j
                    if j < RING:
                        sp_.wait_ge(down_done, w * DOWN + (N_DOWN0 - RING + j + 1))
                    elif j < UP + RING:
                        sp_.wait_ge(eup_done, w * (2 * KE) + 4 * (j - RING + 1))
                    else:
                        sp_.wait_ge(down_done, w * DOWN + (N_DOWN0 + j - RING - UP + 1))
                    if j < UP:
                        for where, src in (("lo256", I["moe_w1"]), ("hi256", I["moe_w3"])):
                            s_ = src[0, bass.ds(e, 1)].rearrange("o (k p) n -> p (o k) n", p=P)
                            sp_.dma_start(place(i, where), s_[:, :, 256 * j:256 * j + 256])\
                               .then_inc(panel_in[i % RING], 16)
                    else:
                        s_ = I["moe_w2"][0, bass.ds(e, 1)].rearrange("o (k p) n -> p (o k) n", p=P)
                        sp_.dma_start(place(i, "rows"), s_[:, 4 * (j - UP):4 * (j - UP) + 4, :])\
                           .then_inc(panel_in[i % RING], 16)
            sp_.wait_ge(x_ready, 10)
            sp_.dma_start(O[0][0], x[:, 0, :]).then_inc(stored, 16)
            sp_.wait_ge(x_ready, 12)
            sp_.dma_start(O[1][0].rearrange("(t p) d -> p t d", p=P), x[:, 1:3, :]).then_inc(stored, 16)
            sp_.wait_ge(stored, 16 * (4 + 2 + 2 + 2))
            for c_ in c_stored:
                sp_.wait_ge(c_, 4 * 16)

        @block.gpsimd
        def _(pool):
            n = [0]

            def then(ins):
                n[0] += 1
                ins.then_inc(pool_step, 1)
                pool.wait_ge(pool_step, n[0])

            pool.memset(epsc[:, :], EPS).then_inc(zeroed, 1)
            pool.wait_ge(zeroed, 1)
            pool.memset(bias[:, :, :, 256:384], 0.0).then_inc(zeroed, 1)
            pool.wait_ge(zeroed, 2)
            pool.memset(wgp[:, :, :, :], 0.0).then_inc(zeroed, 1)
            pool.wait_ge(zeroed, 3)
            pool.memset(gbias[:, :], 0.0).then_inc(zeroed, 1)
            pool.wait_ge(zeroed, 4)
            pool.memset(m0[:, :], 0.0).then_inc(zeroed, 1)
            pool.wait_ge(zeroed, 5)
            pool.wait_ge(bias_in, 16 * 4)
            for half in range(2):
                v = bias[64 * half:64 * half + 64, :, :, 0:256].rearrange("p q h (r c) -> p (q h) r c", r=4)
                lo = v[:, :, :, 0:48]
                hi = v[:, :, :, 16:64]
                for qh in range(16):
                    then(pool.affine_select(out=lo[:, qh], in_=lo[:, qh], compare_op=ALU.is_ge, fill=NEG,
                                            base=8, pattern=[[0, 4], [1, 48]], channel_multiplier=-1))
                    ins = pool.affine_select(out=hi[:, qh], in_=hi[:, qh], compare_op=ALU.is_gt, fill=NEG,
                                             base=8 - 16, pattern=[[0, 4], [-1, 48]], channel_multiplier=1)
                    if qh < 15 or half == 0:
                        then(ins)
            ins.then_inc(masked, 1)
            pool.wait_ge(masked, 1)
            for j in range(8):
                src = qat if j < 4 else kat
                wait_kept(pool, index[("qa" if j < 4 else "ka", j % 4)])
                if j >= 2:
                    pool.wait_ge(roped, j - 1)
                pool.tensor_tensor(ropec[j % 2], src[:, j % 4, P:3 * P], cst[:, C_COS:C_COS + 256], ALU.mult)\
                    .then_inc(cos_part, 1)
                pool.wait_ge(cos_part, j + 1)
            if stop < 3:
                return
            pool.wait_ge(x_ready, 6)
            pool.memset(xdin[:, :, :], 0.0).then_inc(zeroed, 1)
            pool.wait_ge(zeroed, 6)
            pool.memset(qkin[:, :, :], 0.0).then_inc(zeroed, 1)
            pool.wait_ge(zeroed, 7)
            pool.memset(wrg[:, :, :, :, :], 0.0).then_inc(zeroed, 1)
            pool.wait_ge(zeroed, 8)
            pool.wait_ge(rg_free, 1)
            pool.memset(rowsall, 0.0).then_inc(zeroed, 1)
            pool.wait_ge(zeroed, 9)
            pool.memset(vaug[:, :, :, 128:129], 1.0).then_inc(zeroed, 1)
            pool.wait_ge(zeroed, 10)
            if stop < 4:
                return
            pool.wait_ge(x_ready, 9)
            pool.memset(yacc[:, :, :], 0.0).then_inc(zeroed, 1)
            pool.wait_ge(zeroed, 11)

        @block.scalar
        def _(act):
            n = [0]

            def then(ins):
                n[0] += 1
                ins.then_inc(act_step, 1)
                act.wait_ge(act_step, n[0])

            for t_, p_, m_, src in row_dmas:
                act.dma_start(rowt[p_:p_ + m_, t_, :], src).then_inc(rows_in, 16)
            act.dma_start(cst[:, :], I["shape_constants"]).then_inc(cst_in, 16)
            act.dma_start(alam[:, :], bass.AP(tensor=I["a_lam"].tensor, offset=0, ap=[[0, P], [1, 256]]))\
               .then_inc(small_in, 16)
            act.dma_start(subg[:, 0, :], bass.AP(tensor=I["a_subln_g"].tensor, offset=0, ap=[[0, P], [1, P]]))\
               .then_inc(small_in, 16)
            act.dma_start(subg[:, 1, :], bass.AP(tensor=I["c_norm_g"].tensor, offset=0, ap=[[0, P], [1, P]]))\
               .then_inc(small_in, 16)
            act.dma_start(kcache[:, 0, :], I["cache_a_k"][0, 0].rearrange("s h e -> s (h e)")).then_inc(even_in, 16)
            act.dma_start(kcache[:, 1, :], I["cache_b_k"][0, 0].rearrange("s h e -> s (h e)")).then_inc(even_in, 16)
            act.dma_start(va[:, 3, :], I["cache_a_v"][0, 0].rearrange("s h e -> s (h e)")).then_inc(even_in, 16)
            act.dma_start(vb[:, 3, :], I["cache_b_v"][0, 0].rearrange("s h e -> s (h e)")).then_inc(even_in, 16)
            for k_ in range(7):
                act.dma_start(shear[:, :, k_, :],
                              bass.AP(tensor=I["b_rpb"].tensor, offset=(k_ + 4) * 31 + 15,
                                      ap=[[465, B_HEADS], [-1, GRID_W], [1, GRID_W]])).then_inc(shear_in, 16)
            act.wait_ge(shear_in, 16 * 7)
            for q in range(2):
                for half in range(2):
                    k_ = 3 - (2 * q + half)
                    act.dma_start(
                        bias[64 * half:64 * half + 64, q, :, 0:256].rearrange("p h (r c) -> p h r c", r=4),
                        shear[:, :, k_:k_ + 4, :].rearrange("h c r k -> c h r k")).then_inc(bias_in, 16)
            act.dma_start(wg[:, :, :], cut(I["w_in_odd"][0], 2048, 16)).then_inc(odd_in, 16)
            act.dma_start(rw[:, :, :], I["router_w"][0].rearrange("(k p) e -> p k e", p=P)).then_inc(router_in, 16)
            act.dma_start(rb[:, :], bass.AP(tensor=I["router_b"].tensor, offset=0, ap=[[0, P], [1, N_EXP]]))\
               .then_inc(router_in, 16)
            act.wait_ge(zeroed, 5)
            for d in range(2):
                for g in range(2):
                    act.dma_start(gbias[32 * d:32 * d + 4, g:g + 1],
                                  bass.AP(tensor=I["c_gate_b"].tensor, offset=8 * d + 4 * g, ap=[[1, 4], [1, 1]]))\
                       .then_inc(odd_in, 16)
                act.dma_start(m0[32 * d:32 * d + 4, :],
                              bass.AP(tensor=I["state_c_m"].tensor, offset=4 * d, ap=[[1, 4], [1, 1]]))\
                   .then_inc(odd_in, 16)

            def norm_in(s):
                for t in range(NT):
                    if s == 0:
                        act.wait_ge(x_in, 32)
                    else:
                        act.wait_ge(x_ready, 3 * (s - 1) + t + 1)
                    ins = act.activation(xn[:, t, :], x[:, t, :], ACT.Square, accum_out=ss[:, s, t:t + 1])
                then(ins)
                act.activation(sd[:, s, :], ss[:, s, :], ACT.Sqrt, scale=1.0 / D, bias=epsc[:, :])\
                   .then_inc(roots_ready, 1)
                act.wait_ge(gains_ready, s + 1)
                for k in range(0, KD, 2):
                    act.wait_ge(xn_turned, 8 * s + k + 1)
                    for c_, (lo, hi) in enumerate(((0, P), (P, T))):
                        ins = act.activation(ht[:, k, lo:hi], bank[k % 4][:, lo:hi], ACT.Identity,
                                             scale=acol[:, s, k, c_:c_ + 1],
                                             bias=modc[:, s // 2, 24 * (s % 2) + k, c_:c_ + 1])
                    ins.then_inc(ht_act, 1)
                for c_ in range(CONDS):
                    act.wait_ge(gb_made, 2 * s + c_ + 1)
                    act.activation(gb[:, c_, 0:512], bank[4][:, :], ACT.Copy)
                    act.activation(gb[:, c_, 512:1024], bank[5][:, :], ACT.Copy).then_inc(gb_kept, 1)

            def norm_out(s):
                for n_ in range(2):
                    for t in range(NT):
                        if s in (0, 2):
                            act.wait_ge(out_done, OUT_BASE[s] + 3 * n_ + t + 1)
                        elif s == 1:
                            act.wait_ge(down_done, N_DOWN0)
                        src = yacc[:, t, 512 * n_:512 * n_ + 512] if s == 3 else bank[2 * t + n_][:, :]
                        ins = act.activation(xn[:, t, 512 * n_:512 * n_ + 512], src, ACT.Square,
                                             accum_out=ss2[:, s, 2 * t + n_:2 * t + n_ + 1])
                ins.then_inc(sq2_ready, 1)
                act.wait_ge(sum2_ready, s + 1)
                act.activation(sd2[:, s, :], ssum[:, s, :], ACT.Sqrt, scale=1.0 / D, bias=epsc[:, :])\
                   .then_inc(root2_ready, 1)

            def head_norm(m):
                for t in range(NT):
                    sq = (sq_even, sq_odd)[m]
                    ins = act.activation(sq[:, 512 * t:512 * t + 512], heads[:, t, 0:512], ACT.Square)
                ins.then_inc(hsq_ready, 1)
                act.wait_ge(hsum_ready, m + 1)
                act.activation(hn[:, m, 1, :], hn[:, m, 0, :], ACT.Sqrt, scale=1.0 / P, bias=epsc[:, :])\
                   .then_inc(hroot_ready, 1)

            def turned_heads(m):
                for k in range(0, 8 if m == 0 else 4, 2):
                    act.wait_ge(o_turned, (0 if m == 0 else 8) + k + 1)
                    act.activation(ht[:, k, :], bank[k % 4][:, 0:T], ACT.Copy).then_inc(ot_act, 1)

            act.wait_ge(cols_ready, 1)
            act.activation(sc[:, :, 0], cols[:, col["c_ctx"]:col["c_ctx"] + 8], ACT.Silu).then_inc(sc_ready, 1)
            act.activation(sc[:, :, 1], cols[:, col["c"]:col["c"] + 8], ACT.Silu).then_inc(sc_ready, 1)
            act.wait_ge(zeroed, 1)
            norm_in(0)
            act.wait_ge(lam_sums, 1)
            act.activation(lamc[:, 2:4], lamc[:, 0:2], ACT.Exp).then_inc(lam_exps, 1)

            def keep_aux(i, dst, n_):
                act.wait_ge(aux_done, i + 1)
                act.activation(dst, bank[6][:, 0:n_].rearrange("p (h t) -> p h t", h=4), ACT.Copy)\
                   .then_inc(aux_kept, 1)

            keep_aux(0, kat[:, :, 3 * P:4 * P], 512)
            keep_aux(1, kbt[:, :, 3 * P:4 * P], 512)
            for i, (what, t, _) in enumerate(even_items):
                if "A" not in even_items[i][2]:
                    continue
                act.wait_ge(proj_done, i + 1)
                src = bank[i % 4]
                if what in ("qa", "qb"):
                    dst = (qat if what == "qa" else qbt)[:, t, :]
                    act.activation(dst, src[:, 0:T], ACT.Copy, scale=HD ** -0.5).then_inc(proj_act, 1)
                else:
                    act.activation((va if what == "va" else vb)[:, t, :], src[:, :], ACT.Copy).then_inc(proj_act, 1)
            act.wait_ge(aux_done, 3)
            keep_aux(2, knew[:, 0, :].rearrange("p (h t) -> p h t", h=4), 512)
            keep_aux(3, knew[:, 1, :].rearrange("p (h t) -> p h t", h=4), 512)
            act.wait_ge(aux_kept, 4)
            act.dma_start(O[2][0, 0].rearrange("s h e -> s (h e)"), knew[:, 0, :]).then_inc(stored, 16)
            act.dma_start(O[4][0, 0].rearrange("s h e -> s (h e)"), knew[:, 1, :]).then_inc(stored, 16)
            wait_kept(act, index[("vb", 2)])
            act.dma_start(O[3][0, 0].rearrange("s h e -> s (h e)"), va[:, 0, :]).then_inc(stored, 16)
            act.dma_start(O[5][0, 0].rearrange("s h e -> s (h e)"), vb[:, 0, :]).then_inc(stored, 16)

            for i in range(NU + 1):
                if i < NU:
                    kind, h, t, _ = units[i]
                    nk = keys(t)[1] - keys(t)[0]
                    if i >= 2:
                        act.wait_ge(probs_turned, i - 1)
                    for j in slots(i):
                        act.wait_ge(max_ready, j + 1)
                        src = prob[:, j % 4, 0:nk] if kind == "b" and t > 0 else bank[j % 4][:, 0:nk]
                        act.activation(prob[:, j % 4, 0:nk], src, ACT.Exp, bias=nmx[:, j:j + 1],
                                       accum_out=lsum[:, j:j + 1]).then_inc(exp_done, 1)
                if i >= 1:
                    u = i - 1
                    nk = keys(units[u][2])[1] - keys(units[u][2])[0]
                    act.wait_ge(probs_turned, u + 1)
                    if u >= 2:
                        act.wait_ge(pv_done, u - 1)
                    act.activation(pts[:, u % 2, 0:nk], bank[4 + u % 2][:, 0:nk], ACT.Copy).then_inc(pts_ready, 1)
            act.wait_ge(o_kept, NU)
            head_norm(0)
            act.wait_ge(stored, 16 * 4)
            turned_heads(0)
            norm_out(0)
            if stop == 1:
                return

            norm_in(1)
            for f in range(KF):
                act.wait_ge(gate_done, f + 1)
                if f >= 2:
                    act.wait_ge(prod_ready, f - 1)
                act.activation(silt[:, f % 2, :], bank[6][:, 0:T], ACT.Silu).then_inc(silu_ready, 1)
            norm_out(1)
            if stop == 2:
                return

            act.wait_ge(x_ready, 6)
            act.wait_ge(zeroed, 8)
            for d in range(2):
                for g, w_ in enumerate((I["rg_wa"], I["rg_wx"])):
                    for b in range(2):
                        act.dma_start(wrg[64 * b:64 * b + 64, d, g, :, 64 * b:64 * b + 64],
                                      w_[0, d].rearrange("(n b) i o -> b i n o", b=2)[b]).then_inc(wrg_in, 16)
            act.dma_start(c0[:, :, 0:P], I["state_c_C"][0, 0].rearrange("d h k e -> k (d h) e")).then_inc(c0_in, 16)
            act.wait_ge(sp_abs, 1)
            act.activation(sp[:, 1, :], sp[:, 0, :], ACT.Exp, scale=-1.0).then_inc(sp_exp, 1)
            norm_in(2)

            def odd_item(i):
                what, m, engine = items[i]
                if engine != "A":
                    return
                act.wait_ge(proj_done, i + 1)
                src = bank[i % 4]
                if what in ("xd", "q", "k"):
                    dst = xdin[:, m, :] if what == "xd" else qkin[:, m + (4 if what == "k" else 0), :]
                    act.activation(dst[:, 1:1 + P], src[:, 0:P], ACT.Copy)
                    act.activation(dst[:, SEG[1]:SEG[1] + 256], src[:, P:T], ACT.Copy).then_inc(proj_act, 1)
                elif what == "gd":
                    act.activation(gd[:, m, :], src[:, 0:T], ACT.Gelu_apprx_tanh).then_inc(proj_act, 1)
                elif what in ("rg0", "rg1"):
                    d = int(what[2])
                    if d == 1 and m == 0:
                        act.wait_ge(rg_done, 1)
                    bc = col["rg_ba" if m < 4 else "rg_bx"] + 4 * d + m % 4
                    act.activation(rgb[m // 4][:, m % 4, 1:1 + NPAD], src[:, 0:NPAD], ACT.Sigmoid,
                                   bias=cols[:, bc:bc + 1]).then_inc(proj_act, 1)
                elif what == "v":
                    if m == 0:
                        act.wait_ge(rg_free, 1)
                    act.activation(vaug[:, m, :, 0:P], src[:, :].rearrange("p (h e) -> p h e", h=4), ACT.Copy)\
                       .then_inc(proj_act, 1)
                else:
                    act.activation(sigo[:, m, :], src[:, :], ACT.Sigmoid).then_inc(proj_act, 1)

            def rg_chain(d):
                act.wait_ge(rates_ready, 2)
                wait_kept(act, index[(f"rg{d}", 7)])
                for n_ in range(4):
                    c_ = 4 * d + n_
                    act.activation(rgb[2][:, n_, 1:1 + NPAD], rgb[0][:, n_, 1:1 + NPAD], ACT.Exp,
                                   scale=sp[:, 4, c_:c_ + 1]).then_inc(rg_exps, 1)
                act.wait_ge(rg_exps, 8 * d + 4)
                for n_ in range(4):
                    c_ = 4 * d + n_
                    act.activation(rgb[0][:, n_, 1:1 + NPAD], rgb[0][:, n_, 1:1 + NPAD], ACT.Tanh,
                                   scale=sp[:, 5, c_:c_ + 1]).then_inc(rg_exps, 1)
                act.wait_ge(rg_ratio, d + 1)
                act.activation(rgb[0][:, :, 1:1 + NPAD], rgb[0][:, :, 1:1 + NPAD], ACT.Sqrt, scale=2.0)\
                   .then_inc(rg_root, 1)

            act.wait_ge(zeroed, 8)
            for i in range(len(even_items), index[("rg0", 7)] + 1):
                odd_item(i)
            rg_chain(0)
            for i in range(index[("q", 0)], index[("rg1", 7)] + 1):
                odd_item(i)
            rg_chain(1)
            for i in range(index[("k", 0)], index[("k", 3)] + 1):
                odd_item(i)
            for n_ in range(8):
                act.wait_ge(conv_ready, n_ + 1)
                act.activation(qkc[:, n_, 1:1 + NPAD], qkc[:, n_, 1:1 + NPAD], ACT.Silu).then_inc(qk_ready, 1)
            for i in range(index[("v", 0)], index[("o", 2)] + 1):
                odd_item(i)
            act.wait_ge(row_abs, 1)
            act.activation(rwork[:, 2, :], rwork[:, 1, :], ACT.Exp, scale=-1.0).then_inc(row_exp, 1)
            act.wait_ge(rows_m, 1)
            act.activation(rows[:, 2, :], rwork[:, 2, :], ACT.Exp, scale=-1.0).then_inc(rows_exp, 1)
            act.activation(rows[:, 1, P:T], rwork[:, 6, P:T], ACT.Exp, bias=m0[:, :]).then_inc(rows_exp, 1)
            for d, last in ((0, P - 1), (1, 0)):
                pp = slice(32 * d, 32 * d + 4)
                act.activation(rows[pp, 3, 0:P], rows[pp, 0, 0:P], ACT.Exp, bias=rwork[pp, 6, last:last + 1])\
                   .then_inc(rows_exp, 1)
                act.dma_start(O[8][0, 0, d].rearrange("(h o) -> h o", o=1), rwork[pp, 2, last:last + 1])\
                   .then_inc(stored, 16)
            act.wait_ge(ktok_done, 1)
            act.activation(ktok[:, :, :], bank[7][:, :].rearrange("p (h e) -> p h e", h=4), ACT.Copy)\
               .then_inc(ktok_kept, 1)
            def mlstm_exp(u):
                act.wait_ge(wlog_ready, u + 1)
                act.activation(wt[:, u % 2, :], wt[:, u % 2, :], ACT.Exp).then_inc(w_ready, 1)

            mlstm_exp(0)
            for u, (h, d) in enumerate(munits):
                q, r = u % 2, 32 * d + h
                if u + 1 < 8:
                    mlstm_exp(u + 1)
                act.wait_ge(mm_done, u + 1)
                if u >= 2:
                    act.wait_ge(h_ready, u - 1)
                    act.wait_ge(c_stored[q], 16 * (u // 2))
                for t in range(1, NT):
                    act.activation(inter[:, q, 129 * (t - 1):129 * t], bank[6 + q][:, 129 * (t - 1):129 * t],
                                   ACT.Copy, scale=colr[:, WST + t - 1, r:r + 1]).then_inc(inter_kept, 1)
                act.activation(cout[:, q, :], bank[6 + q][:, 258:387], ACT.Copy).then_inc(cout_kept, 1)
                act.wait_ge(cout_kept, u + 1)
                act.dma_start(O[6][0, 0, d, h], cout[:, q, 0:P]).then_inc(c_stored[q], 16)
            act.wait_ge(h_ready, 8)
            head_norm(1)
            act.wait_ge(fin_turned, 1)
            act.activation(finrows[:, :, :], bank[7][0:8, 0:256].rearrange("p (a e) -> p a e", a=2), ACT.Copy)\
               .then_inc(fin_kept, 1)
            act.wait_ge(fin_kept, 1)
            act.dma_start(O[7][0, 0].rearrange("d h k -> (d h) k"), finrows[:, 0, :]).then_inc(stored, 16)
            act.dma_start(O[9][0, 0].rearrange("d (n k) -> (d n) k", k=P), finrows[:, 1, :]).then_inc(stored, 16)
            turned_heads(1)
            norm_out(2)
            if stop == 3:
                return

            norm_in(3)
            for j in range(6):
                act.wait_ge(tok_turned, j + 1)
                act.activation(htok[:, j // 2, 512 * (j % 2):512 * (j % 2) + 512], bank[j % 4][:, :], ACT.Copy)\
                   .then_inc(htok_ready, 1)
            act.wait_ge(e1_in, 1)
            act.activation(tk[:, 5, :], tk[:, 4, :], ACT.Exp).then_inc(e1_ready, 1)
            act.wait_ge(plan_ready, 1)
            n_work = act.value_load(ewi[0:1, MAX_ITEMS:MAX_ITEMS + 1], min_val=1, max_val=MAX_ITEMS)
            with act.Fori(0, n_work) as w:
                for b in range(2):
                    act.wait_ge(gath_done, w * 2 + (b + 1))
                    act.activation(xg[:, 4 * b:4 * b + 4, :],
                                   bank[6 + b][:, :].rearrange("p (k s) -> p k s", k=4), ACT.Copy)\
                       .then_inc(xg_ready, 1)
                for f in range(KE):
                    act.wait_ge(eup_done, w * (2 * KE) + (2 * f + 1))
                    if f >= 2:
                        act.wait_ge(eprod_ready, w * KE + (f - 1))
                    act.activation(sil_e[:, f % 2, :], bank[f % 2][:, 0:P], ACT.Silu).then_inc(esilu_ready, 1)
                for b in range(2):
                    act.wait_ge(down_done, w * DOWN + (N_DOWN0 + DOWN))
                    act.activation(og[:, 512 * b:512 * b + 512], bank[6 + b][:, :], ACT.Copy).then_inc(og_ready, 1)
            act.wait_ge(yacc_ready, 1)
            norm_out(3)

        @block.tensor
        def _(pe):
            def panel(key):
                i = number[key]
                pe.wait_ge(panel_in[i % RING], need[i])
                return i

            def mod_mm(m):
                if m >= 2:
                    pe.wait_ge(mod_added, m - 1 if m < 6 else m)
                i = panel(("mod", m))
                w = place(i, "k512")
                for n_ in range(4):
                    for k in range(KD):
                        ins = pe.matmul(bank[mod_bank(m)][:, 2 * n_:2 * n_ + 2], w[:, k, P * n_:P * n_ + P],
                                        sc[:, k, :], start=(k == 0), stop=(k == KD - 1))
                ins.then_inc(mod_done, 1)

            def norm_in(s):
                pe.wait_ge(xn_ready, 3 * (s + 1))
                for k in range(KD):
                    if k >= 4:
                        pe.wait_ge((ht_act, ht_dve)[k % 2], 4 * s + (k - 4) // 2 + 1)
                    for t in range(NT):
                        ins = pe.transpose(bank[k % 4][:, P * t:P * t + P], xn[:, t, P * k:P * k + P], ident)
                    ins.then_inc(xn_turned, 1)
                pe.wait_ge(gains_ready, s + 1)
                for c_ in range(CONDS):
                    if c_:
                        pe.wait_ge(gb_kept, 2 * s + 1)
                    for k in range(KD):
                        ins = pe.matmul(bank[4 + k // 4][:, P * (k % 4):P * (k % 4) + P],
                                        gcol[:, s, k, c_:c_ + 1].to_broadcast([P, P]), ident,
                                        start=True, stop=True)
                    ins.then_inc(gb_made, 1)
                pe.wait_ge(ht_act, 4 * (s + 1))
                pe.wait_ge(ht_dve, 4 * (s + 1))
                pe.wait_ge(gb_kept, 2 * (s + 1))

            def project(i, w, n0=None, t=None):
                if (i if i < len(even_items) else i - len(even_items)) >= 4:
                    wait_kept(pe, i - 4)
                for k in range(KD):
                    if t is None:
                        ins = pe.matmul(bank[i % 4][:, 0:T], w[:, k, n0:n0 + P], ht[:, k, :],
                                        start=(k == 0), stop=(k == KD - 1))
                    else:
                        ins = pe.matmul(bank[i % 4][:, :], ht[:, k, P * t:P * t + P], w[:, k, :],
                                        start=(k == 0), stop=(k == KD - 1))
                return ins

            def project_panel(key, what, by_token):
                i = panel(key)
                w = place(i, "k512")
                for m in range(3 if by_token else 4):
                    j = index[(what, m)]
                    ins = project(j, w, t=m) if by_token else project(j, w, n0=P * m)
                    ins.then_inc(proj_done, 1)

            def turn_heads(m):
                for k in range(8 if m == 0 else 4):
                    if k >= 4:
                        if k % 2 == 0:
                            pe.wait_ge(ot_act, k // 2 - 1)
                        else:
                            pe.wait_ge(ot_dve, k // 2 - 1)
                    for t in range(NT):
                        ins = pe.transpose(bank[k % 4][:, P * t:P * t + P], heads[:, t, P * k:P * k + P], ident)
                    ins.then_inc(o_turned, 1)
                pe.wait_ge(ot_act, 4 if m == 0 else 6)
                pe.wait_ge(ot_dve, 4 if m == 0 else 6)

            def out_proj(m):
                for j in range(2):
                    i = panel((f"out{m}", j))
                    w = place(i, "k512")
                    for t in range(NT):
                        for k in range(KD):
                            lhs = gd[:, k - 4, P * t:P * t + P] if m == 1 and k >= 4 else ht[:, k, P * t:P * t + P]
                            ins = pe.matmul(bank[2 * t + j][:, :], lhs, w[:, k, :], start=(k == 0), stop=(k == KD - 1))
                        ins.then_inc(out_done, 1)

            pe.wait_ge(cst_in, 16)
            pe.wait_ge(rows_in, 16 * len(row_dmas))
            for t_ in range(3):
                m_ = P if t_ < 2 else last_rows
                ins = pe.transpose(bank[6][:, P * t_:P * t_ + m_], rowt[0:m_, t_, :], ident[0:m_, 0:m_])
            ins.then_inc(rows_turned, 1)
            pe.wait_ge(sc_ready, 2)
            for m in range(6):
                mod_mm(m)
            norm_in(0)
            for a in range(2):
                pe.wait_ge(even_in, 64)
                if a:
                    pe.wait_ge(aux_kept, a)
                for h in range(4):
                    ins = pe.transpose(bank[6][:, P * h:P * h + P], kcache[:, a, P * h:P * h + P], ident)
                ins.then_inc(aux_done, 1)
            project_panel(("in0", 0), "qa", False)
            project_panel(("in0", 1), "ka", False)
            project_panel(("in0", 2), "va", True)
            for j in range(8):
                src = qat if j < 4 else kat
                if j == 0:
                    wait_kept(pe, index[("ka", 3)])
                    wait_kept(pe, index[("qa", 3)])
                if j >= 2:
                    pe.wait_ge(roped, j - 1)
                pe.matmul(bank[4 + j % 2][:, 0:256], cst[:, C_ROT:C_ROT + P], src[:, j % 4, P:3 * P],
                          start=True, stop=True).then_inc(rot_done, 1)
            project_panel(("in0", 3), "qb", False)
            project_panel(("in0", 4), "kb", False)
            project_panel(("in0", 5), "vb", True)
            for a in range(2):
                pe.wait_ge(aux_kept, a + 2)
                wait_kept(pe, index[("kb", 3)])
                for h in range(4):
                    ins = pe.transpose(bank[6][:, P * h:P * h + P], (kat, kbt)[a][:, h, 0:P], ident)
                ins.then_inc(aux_done, 1)
            wait_kept(pe, index[("vb", 2)])
            wait_kept(pe, index[("vb", 1)])
            pe.wait_ge(roped, 8)
            pe.wait_ge(aux_kept, 4)
            for i in range(NU + 2):
                if i < NU:
                    kind, h, t, _ = units[i]
                    k0, k1 = keys(t)
                    for j in slots(i):
                        if j >= 4:
                            pe.wait_ge(exp_done, j - 3)
                        if kind == "a":
                            pp = slice(64 * (j % 2), 64 * (j % 2) + 64)
                            q_, k_ = qat[pp, h, P * t:P * t + P], kat[pp, h, k0:k1]
                        else:
                            pp = slice(64 * (h % 2), 64 * (h % 2) + 64)
                            q_, k_ = qbt[pp, h // 2, P * t:P * t + P], kbt[pp, h // 2, k0:k1]
                        pe.matmul(bank[j % 4][:, 0:k1 - k0], q_, k_, start=True, stop=True).then_inc(scores_done, 1)
                m = mod_at(i)
                if m is not None:
                    mod_mm(m)
                if 1 <= i <= NU:
                    u = i - 1
                    k0, k1 = keys(units[u][2])
                    j = slots(u)[0]
                    if units[u][0] == "a":
                        pe.wait_ge(probs_ready, u + 1)
                    else:
                        pe.wait_ge(exp_done, j + 1)
                    if u >= 2:
                        pe.wait_ge(pts_ready, u - 1)
                    for b in range((k1 - k0) // P):
                        ins = pe.transpose(bank[4 + u % 2][:, P * b:P * b + P], prob[:, j % 4, P * b:P * b + P], ident)
                    ins.then_inc(probs_turned, 1)
                if i >= 2:
                    u = i - 2
                    kind, h, t, _ = units[u]
                    k0, k1 = keys(t)
                    nb_ = (k1 - k0) // P
                    e = P if kind == "a" else HD
                    pe.wait_ge(pts_ready, u + 1)
                    if u:
                        pe.wait_ge(o_kept, u)
                    for b in range(nb_):
                        v_ = (va if kind == "a" else vb)[:, k0 // P + b, e * h:e * h + e]
                        ins = pe.matmul(bank[6][:, 0:e], pts[:, u % 2, P * b:P * b + P], v_,
                                        start=(b == 0), stop=(b == nb_ - 1))
                    ins.then_inc(pv_done, 1)
            pe.wait_ge(heads_ready, 1)
            turn_heads(0)
            out_proj(0)
            if stop == 1:
                return

            norm_in(1)
            for f in range(KF):
                if f % 2 == 0:
                    i = panel(("up", f // 2))
                w = place(i, "k512")
                for g in range(2):
                    if f:
                        pe.wait_ge((silu_ready, prod_ready)[g], f)
                    for k in range(KD):
                        ins = pe.matmul(bank[6 + g][:, 0:T], w[:, k, 256 * g + P * (f % 2):256 * g + P * (f % 2) + P],
                                        ht[:, k, :], start=(k == 0), stop=(k == KD - 1))
                    ins.then_inc((gate_done, up_done)[g], 1)
            pe.wait_ge(gb_kept, 4)
            pe.wait_ge(prod_ready, KF)
            for f in range(KF):
                if f % 4 == 0:
                    i = panel(("down", f // 4))
                w = place(i, "rows")
                for t in range(NT):
                    for n_ in range(2):
                        ins = pe.matmul(bank[2 * t + n_][:, :], actt[:, f, P * t:P * t + P],
                                        w[:, f % 4, 512 * n_:512 * n_ + 512], start=(f == 0), stop=(f == KF - 1))
                if f == KF - 1 or f % 4 == 3:
                    ins.then_inc(down_done, 1)
            if stop == 2:
                return

            norm_in(2)
            project_panel(("in1", 0), "xd", False)
            project_panel(("in1", 1), "gd", False)

            def rg_mm(d):
                if d == 0:
                    pe.wait_ge(xc_ready, 4)
                    pe.wait_ge(wrg_in, 16 * 8)
                for m in range(8):
                    i = index[(f"rg{d}", m)]
                    wait_kept(pe, i - 4)
                    pe.matmul(bank[i % 4][:, 0:NPAD], wrg[:, d, m // 4, m % 4, :], xc[:, m % 4, 1:1 + NPAD],
                              start=True, stop=True).then_inc(proj_done, 1)

            rg_mm(0)
            project_panel(("in1", 2), "q", False)
            rg_mm(1)
            project_panel(("in1", 3), "k", False)
            pe.wait_ge(wgp_ready, 1)
            for g in range(2):
                for k in range(KD):
                    ins = pe.matmul(bank[4 + g][0:36, 0:T], wgp[:, k, g, :], ht[:, k, :],
                                    start=(k == 0), stop=(k == KD - 1))
            ins.then_inc(gates_done, 1)
            project_panel(("in1", 4), "v", True)
            project_panel(("in1", 5), "o", True)
            pe.wait_ge(qk_ready, 8)
            for h in range(4):
                ins = pe.transpose(bank[7][:, P * h:P * h + P], qkc[:, 4 + h, SEG[0]:SEG[0] + P], ident)
            ins.then_inc(ktok_done, 1)
            pe.wait_ge(rows_m, 1)
            pe.wait_ge(rows_exp, 4)
            turns = ([(0, t) for t in range(3)] + [(1, 1), (1, 2)] + [(2, t) for t in range(3)] + [(3, 0)])
            for j, (kind, t) in enumerate(turns):
                ins = pe.transpose(bank[6][:, 36 * j:36 * j + 36], rows[:, kind, P * t:P * t + P], ident[0:36, 0:36])
            ins.then_inc(rows_turned2, 1)
            pe.wait_ge(colr_ready, 1)
            pe.wait_ge(ktok_kept, 1)
            pe.wait_ge(c0_in, 16)
            wait_kept(pe, index[("o", 2)])
            wait_kept(pe, index[("o", 1)])
            pe.wait_ge(zeroed, 10)

            def mlstm_logs(u):
                h, d = munits[u]
                if d == 0:
                    if u:
                        pe.wait_ge(sw_ready, u)
                    for s_, dst in ((0, bank[0][:, 0:P]), (1, bank[0][:, P:T]), (2, bank[1][:, 0:256])):
                        q_ = qkc[:, h, SEG[0]:SEG[0] + P] if s_ == 0 else qkc[:, h, SEG[1]:SEG[1] + 256]
                        ins = pe.matmul(dst, qkc[:, 4 + h, SEG[s_]:SEG[s_] + P], q_, start=True, stop=True)
                    ins.then_inc(st_done, 1)
                if u >= 2:
                    pe.wait_ge(wlog_ready, u - 1)
                sel_ = C_SEL + (4 * d + h) * P
                pe.matmul(bank[2 + u % 2][:, 0:T], cst[0:36, sel_:sel_ + P], rwork[:, 6, :], start=True, stop=True)\
                  .then_inc(nm_done, 1)

            mlstm_logs(0)
            for u, (h, d) in enumerate(munits):
                q = u % 2
                pe.wait_ge(sw_ready, u + 1)
                if u + 1 < 8:
                    mlstm_logs(u + 1)
                pe.wait_ge(kws_ready, u + 1)
                if u >= 2:
                    pe.wait_ge(h_ready, u - 1)
                    pe.wait_ge(inter_kept, 2 * (u - 1))
                    pe.wait_ge(cout_kept, u - 1)
                for t in range(NT):
                    bl = [b for b in blocks[d] if b[1] == t]
                    for b, (s_, _, o_) in enumerate(bl):
                        pe.matmul(bank[4 + q][:, 129 * t:129 * t + 129], sw[:, q, o_:o_ + P], vaug[:, s_, h, :],
                                  start=(b == 0), stop=(b == len(bl) - 1))
                for t in range(1, NT):
                    pe.matmul(bank[6 + q][:, 129 * (t - 1):129 * t], qkc[:, h, SEG[t]:SEG[t] + P],
                              c0[:, 4 * d + h, :], start=True, stop=True)
                pe.matmul(bank[6 + q][:, 258:387], kws[:, q, :], vaug[:, 0, h, :], start=True, stop=True)\
                  .then_inc(mm_done, 1)
            pe.wait_ge(fin_ready, 8)
            pe.wait_ge(rg_free, 1)
            pe.wait_ge(cout_kept, 8)
            for a in range(2):
                ins = pe.transpose(bank[7][0:8, P * a:P * a + P], fincols[:, 8 * a:8 * a + 8], ident)
            ins.then_inc(fin_turned, 1)
            pe.wait_ge(heads_ready, 2)
            turn_heads(1)
            pe.wait_ge(rg_free, 1)
            out_proj(1)
            if stop == 3:
                return

            norm_in(3)
            pe.wait_ge(router_in, 32)
            for t in range(NT):
                for k in range(KD):
                    ins = pe.matmul(bank[6][:, 8 * t:8 * t + 8], ht[:, k, P * t:P * t + P], rw[:, k, :],
                                    start=(k == 0), stop=(k == KD - 1))
            ins.then_inc(logits_done, 1)
            for j in range(6):
                if j >= 4:
                    pe.wait_ge(htok_ready, j - 3)
                for k in range(4):
                    ins = pe.transpose(bank[j % 4][:, P * k:P * k + P],
                                       ht[:, 4 * (j % 2) + k, P * (j // 2):P * (j // 2) + P], ident)
                ins.then_inc(tok_turned, 1)
            pe.wait_ge(sel_ready, 1)
            for t in range(NT):
                for t2 in range(t + 1):
                    m_ = cst[:, C_CUM:C_CUM + P] if t2 == t else ones
                    pe.matmul(bank[7][:, 8 * t:8 * t + 8], m_, oh[:, 2, t2, :], start=(t2 == 0), stop=(t2 == t))
            for t in range(NT):
                ins = pe.matmul(bank[7][:, 24:32], ones, oh[:, 2, t, :], start=(t == 0), stop=(t == NT - 1))
            ins.then_inc(pos_done, 1)
            pe.wait_ge(htok_ready, 6)
            pe.wait_ge(plan_ready, 1)
            n_work = pe.value_load(ewi[0:1, MAX_ITEMS:MAX_ITEMS + 1], min_val=1, max_val=MAX_ITEMS)
            with pe.Fori(0, n_work) as w:
                pe.wait_ge(hot_ready, w + 1)
                for b in range(2):
                    for k in range(4):
                        for t in range(NT):
                            ins = pe.matmul(bank[6 + b][:, P * k:P * k + P],
                                            htok[:, t, 512 * b + P * k:512 * b + P * k + P], onehot[:, t, :],
                                            start=(t == 0), stop=(t == NT - 1))
                    ins.then_inc(gath_done, 1)
                pe.wait_ge(yadd, w * 6 + 1)
                for t in range(NT):
                    ins = pe.transpose(bank[4][:, P * t:P * t + P], gated[:, t, :], ident)
                ins.then_inc(gated_turned, 1)
                pe.wait_ge(xg_ready, w * 2 + 2)
                for f in range(KE):
                    j = f // 2
                    if f % 2 == 0:
                        pe.wait_ge(panel_in[(NP0 + j) % RING], w * slot_item[(NP0 + j) % RING] + item_need[j])
                    wp = place(NP0 + j, "k512")
                    for g in range(2):
                        dst = bank[2 * g + f % 2][:, 0:P]
                        if f >= 2 and g == 0:
                            pe.wait_ge(eprod_ready, w * KE + (f - 1))
                        for k in range(KD):
                            ins = pe.matmul(dst, wp[:, k, 256 * g + P * (f % 2):256 * g + P * (f % 2) + P],
                                            xg[:, k, :], start=(k == 0), stop=(k == KD - 1))
                        ins.then_inc(eup_done, 1)
                pe.wait_ge(eprod_ready, w * KE + KE)
                for jd in range(DOWN):
                    j = UP + jd
                    pe.wait_ge(panel_in[(NP0 + j) % RING], w * slot_item[(NP0 + j) % RING] + item_need[j])
                    wp = place(NP0 + j, "rows")
                    for k in range(4):
                        for b in range(2):
                            ins = pe.matmul(bank[6 + b][:, :], act_e[:, 4 * jd + k, :],
                                            wp[:, k, 512 * b:512 * b + 512],
                                            start=(jd == 0 and k == 0), stop=(jd == DOWN - 1 and k == 3))
                    ins.then_inc(down_done, 1)
                pe.wait_ge(scat_ready, w + 1)
                pe.wait_ge(og_ready, w * 2 + 2)
                for j, (t, b) in enumerate(SCATTER):
                    pe.matmul(bank[SCAT_BANK[j]][:, :], scat[:, t, :], og[:, 512 * b:512 * b + 512],
                              start=True, stop=True).then_inc(scat_done, 1)

        @block.vector
        def _(dve):
            n = [0]

            def then(ins):
                n[0] += 1
                ins.then_inc(dve_step, 1)
                dve.wait_ge(dve_step, n[0])

            def add_mod(m):
                dve.wait_ge(mod_done, m + 1)
                l, j = m // 12, m % 12
                b = cols[:, col["mod_b"] + 48 * l + 4 * j:col["mod_b"] + 48 * l + 4 * j + 4]
                dve.tensor_tensor(modc[:, l, 4 * j:4 * j + 4, :],
                                  bank[mod_bank(m)][:, 0:8].rearrange("p (n c) -> p n c", c=2),
                                  b.unsqueeze(2).to_broadcast([P, 4, 2]), ALU.add).then_inc(mod_added, 1)
                if m % 6 == 5:
                    gains(m // 6)

            def gains(s):
                l, h = s // 2, 24 * (s % 2)
                dve.wait_ge(mod_added, 6 * (s + 1))

                def g(r):
                    o = col["norm_g"] + 32 * l + 8 * (2 * (s % 2) + r)
                    return cols[:, o:o + 8].unsqueeze(2).to_broadcast([P, 8, 2])

                then(dve.scalar_tensor_tensor(out=acol[:, s, :, :], in0=modc[:, l, h + 8:h + 16, :], scalar=1.0,
                                              in1=g(0), op0=ALU.add, op1=ALU.mult))
                dve.tensor_tensor(gcol[:, s, :, :], modc[:, l, h + 16:h + 24, :], g(1), ALU.mult)\
                   .then_inc(gains_ready, 1)

            def norm_in(s):
                dve.wait_ge(roots_ready, s + 1)
                then(dve.reciprocal(rs[:, s, :], sd[:, s, :]))
                for t in range(NT):
                    dve.tensor_scalar(xn[:, t, :], x[:, t, :], rs[:, s, t:t + 1], None, ALU.mult)\
                       .then_inc(xn_ready, 1)
                for k in range(1, KD, 2):
                    dve.wait_ge(xn_turned, 8 * s + k + 1)
                    for c_, (lo, hi) in enumerate(((0, P), (P, T))):
                        ins = dve.tensor_scalar(ht[:, k, lo:hi], bank[k % 4][:, lo:hi], acol[:, s, k, c_:c_ + 1],
                                                modc[:, s // 2, 24 * (s % 2) + k, c_:c_ + 1], ALU.mult, ALU.add)
                    ins.then_inc(ht_dve, 1)

            def norm_out(s):
                dve.wait_ge(sq2_ready, s + 1)
                v = ss2[:, s, :].rearrange("p (t n) -> p n t", n=2)
                dve.tensor_tensor(ssum[:, s, :], v[:, 0, :], v[:, 1, :], ALU.add).then_inc(sum2_ready, 1)
                dve.wait_ge(root2_ready, s + 1)
                then(dve.reciprocal(rs2[:, s, :], sd2[:, s, :]))
                for t in range(NT):
                    if t:
                        dve.wait_ge(x_ready, 3 * s + t)
                    for n_ in range(2):
                        h = slice(512 * n_, 512 * n_ + 512)
                        src = yacc[:, t, h] if s == 3 else bank[2 * t + n_][:, :]
                        ins = dve.scalar_tensor_tensor(out=jk[:, n_, :], in0=src, scalar=rs2[:, s, t:t + 1],
                                                       in1=gb[:, min(t, 1), h], op0=ALU.mult, op1=ALU.mult)
                    then(ins)
                    for n_ in range(2):
                        h = slice(512 * n_, 512 * n_ + 512)
                        ins = dve.tensor_tensor(x[:, t, h], x[:, t, h], jk[:, n_, :], ALU.add)
                    ins.then_inc(x_ready, 1)

            def head_norm(m, sq, gate):
                dve.wait_ge(hsq_ready, m + 1)
                dve.tensor_reduce(hn[:, m, 0, :], sq.rearrange("p (u e) -> p u e", e=P), AX.X, ALU.add)\
                   .then_inc(hsum_ready, 1)
                dve.wait_ge(hroot_ready, m + 1)
                then(dve.reciprocal(hn[:, m, 2, :], hn[:, m, 1, :]))
                for t in range(NT):
                    for h in range(4):
                        v = heads[:, t, P * h:P * h + P]
                        ins = dve.scalar_tensor_tensor(out=v, in0=v, scalar=hn[:, m, 2, 4 * t + h:4 * t + h + 1],
                                                       in1=subg[:, m, :], op0=ALU.mult, op1=ALU.mult)
                if gate is not None:
                    then(ins)
                    for t in range(NT):
                        ins = dve.tensor_tensor(heads[:, t, 0:512], heads[:, t, 0:512], gate[:, t, :], ALU.mult)
                ins.then_inc(heads_ready, 1)

            def turned_heads(m):
                for k in range(1, 8 if m == 0 else 4, 2):
                    dve.wait_ge(o_turned, (0 if m == 0 else 8) + k + 1)
                    dve.tensor_copy(ht[:, k, :], bank[k % 4][:, 0:T]).then_inc(ot_dve, 1)

            dve.wait_ge(rows_turned, 1)
            dve.tensor_copy(cols[:, 0:n_rows], bank[6][:, 0:n_rows]).then_inc(cols_ready, 1)
            dve.wait_ge(cols_ready, 1)
            for m in range(6):
                add_mod(m)
            norm_in(0)

            dve.wait_ge(small_in, 48)
            dve.tensor_tensor_reduce(prob[:, 0, 0:64], alam[:, 0:64], alam[:, 64:128], 1.0, 0.0, ALU.mult, ALU.add,
                                     lamc[:, 0:1])
            dve.tensor_tensor_reduce(prob[:, 0, 64:128], alam[:, 128:192], alam[:, 192:256], 1.0, 0.0, ALU.mult,
                                     ALU.add, lamc[:, 1:2]).then_inc(lam_sums, 1)
            then(dve.tensor_scalar(subg[:, 0, :], subg[:, 0, :], 1.0 - LAM_INIT, None, ALU.mult))
            dve.wait_ge(lam_exps, 1)
            then(dve.tensor_tensor(lamc[:, 4:5], lamc[:, 3:4], lamc[:, 2:3], ALU.subtract))
            then(dve.tensor_scalar(lamc[:, 5:6], lamc[:, 4:5], -LAM_INIT, None, ALU.add))

            def even_item(i):
                what, t, _ = items[i]
                dve.wait_ge(proj_done, i + 1)
                dve.tensor_copy((kat if what == "ka" else kbt)[:, t, 0:T], bank[i % 4][:, 0:T]).then_inc(proj_dve, 1)

            for t in range(4):
                even_item(index[("ka", t)])
            dve.wait_ge(aux_done, 1)
            for j in range(8):
                dst = (qat if j < 4 else kat)[:, j % 4, P:3 * P]
                dve.wait_ge(rot_done, j + 1)
                if j >= 2:
                    dve.wait_ge(roped, j - 1)
                then(dve.tensor_tensor(ropes[j % 2], bank[4 + j % 2][:, 0:256], cst[:, C_SIN:C_SIN + 256], ALU.mult))
                dve.wait_ge(cos_part, j + 1)
                dve.tensor_tensor(dst, ropec[j % 2], ropes[j % 2], ALU.add).then_inc(roped, 1)
            for t in range(4):
                even_item(index[("kb", t)])

            for i in range(NU + 2):
                if i < NU:
                    kind, h, t, _ = units[i]
                    nk = keys(t)[1] - keys(t)[0]
                    for j in slots(i):
                        dve.wait_ge(scores_done, j + 1)
                        if kind == "b" and t > 0:
                            if h == 0 and t == 1:
                                dve.wait_ge(masked, 1)
                            dve.wait_ge(probs_turned, i - 1)
                            then(dve.tensor_tensor_reduce(prob[:, j % 4, 0:nk], bank[j % 4][:, 0:nk],
                                                          bias[:, t - 1, h, :], 1.0, -3.0e38, ALU.add, ALU.max,
                                                          rl[:, j:j + 1]))
                            dve.tensor_scalar(nmx[:, j:j + 1], rl[:, j:j + 1], -1.0, None, ALU.mult)\
                               .then_inc(max_ready, 1)
                        else:
                            dve.tensor_reduce(nmx[:, j:j + 1], bank[j % 4][:, 0:nk], AX.X, ALU.max, negate=True)\
                               .then_inc(max_ready, 1)
                m = mod_at(i)
                if m is not None:
                    add_mod(m)
                if 1 <= i <= NU:
                    u = i - 1
                    j = slots(u)[0]
                    nk = keys(units[u][2])[1] - keys(units[u][2])[0]
                    dve.wait_ge(exp_done, slots(u)[-1] + 1)
                    if units[u][0] == "a":
                        then(dve.reciprocal(rl[:, j:j + 2], lsum[:, j:j + 2]))
                        then(dve.tensor_scalar(rl[:, j + 1:j + 2], rl[:, j + 1:j + 2], lamc[:, 5:6], None, ALU.mult))
                        then(dve.tensor_scalar(prob[:, (j + 1) % 4, 0:nk], prob[:, (j + 1) % 4, 0:nk],
                                               rl[:, j + 1:j + 2], None, ALU.mult))
                        dve.scalar_tensor_tensor(out=prob[:, j % 4, 0:nk], in0=prob[:, j % 4, 0:nk],
                                                 scalar=rl[:, j:j + 1], in1=prob[:, (j + 1) % 4, 0:nk],
                                                 op0=ALU.mult, op1=ALU.add).then_inc(probs_ready, 1)
                    else:
                        then(dve.reciprocal(rl[:, j:j + 1], lsum[:, j:j + 1]))
                if i >= 2:
                    u = i - 2
                    kind, h, t, j = units[u]
                    dve.wait_ge(pv_done, u + 1)
                    if kind == "a":
                        dve.tensor_copy(heads[:, t, P * h:P * h + P], bank[6][:, 0:P])\
                           .then_inc(o_kept, 1)
                    else:
                        dve.tensor_scalar(heads[:, t, 512 + HD * h:512 + HD * h + HD],
                                          bank[6][:, 0:HD], rl[:, j:j + 1], None, ALU.mult)\
                           .then_inc(o_kept, 1)
            head_norm(0, sq_even, None)
            dve.wait_ge(stored, 16 * 4)
            turned_heads(0)
            norm_out(0)
            if stop == 1:
                return

            norm_in(1)
            for f in range(KF):
                dve.wait_ge(up_done, f + 1)
                dve.wait_ge(silu_ready, f + 1)
                dve.tensor_tensor(actt[:, f, :], silt[:, f % 2, :], bank[7][:, 0:T], ALU.mult).then_inc(prod_ready, 1)
            norm_out(1)
            if stop == 2:
                return

            def log1p_of(e, z, z2, acc, out):
                then(dve.tensor_scalar(z, e, 2.0, None, ALU.add))
                then(dve.reciprocal(z, z))
                then(dve.tensor_tensor(z, z, e, ALU.mult))
                then(dve.tensor_tensor(z2, z, z, ALU.mult))
                then(dve.tensor_scalar(acc, z2, 1.0 / 15, None, ALU.mult))
                for c_ in (13, 11, 9, 7, 5, 3):
                    then(dve.scalar_tensor_tensor(out=acc, in0=acc, scalar=1.0 / c_, in1=z2, op0=ALU.add, op1=ALU.mult))
                then(dve.scalar_tensor_tensor(out=acc, in0=acc, scalar=1.0, in1=z, op0=ALU.add, op1=ALU.mult))
                then(dve.tensor_scalar(out, acc, 2.0, None, ALU.mult))

            lam_ = cols[:, col["rg_lam"]:col["rg_lam"] + 8]
            dve.scalar_tensor_tensor(out=sp[:, 0, :], in0=lam_, scalar=-1.0, in1=lam_, op0=ALU.mult, op1=ALU.max)\
               .then_inc(sp_abs, 1)
            dve.wait_ge(sp_exp, 1)
            log1p_of(sp[:, 1, :], sp[:, 2, :], sp[:, 3, :], sp[:, 4, :], sp[:, 0, :])
            then(dve.tensor_scalar(sp[:, 2, :], lam_, -1.0, 0.0, ALU.mult, ALU.max))
            then(dve.tensor_tensor(sp[:, 3, :], sp[:, 0, :], sp[:, 2, :], ALU.add))
            dve.tensor_scalar(sp[:, 4, :], sp[:, 3, :], -8.0, None, ALU.mult).then_inc(rates_ready, 1)
            dve.tensor_scalar(sp[:, 5, :], sp[:, 3, :], 8.0, None, ALU.mult).then_inc(rates_ready, 1)
            dve.wait_ge(odd_in, 16 * 7)
            dve.wait_ge(zeroed, 5)
            for d in range(2):
                for g in range(2):
                    o = 8 * d + 4 * g
                    dve.tensor_copy(wgp[:, :, g, 32 * d:32 * d + 4], wg[:, :, o:o + 4]).then_inc(wgp_ready, 1)
            dve.tensor_copy(c0[:, :, P:P + 1], cols[:, col["state_c_n"]:col["state_c_n"] + 8].unsqueeze(2))\
               .then_inc(wgp_ready, 1)
            norm_in(2)
            dve.wait_ge(zeroed, 8)

            def odd_item(i):
                what, m, engine = items[i]
                if engine != "D":
                    return
                dve.wait_ge(proj_done, i + 1)
                dst = xdin[:, m, :] if what == "xd" else qkin[:, m + (4 if what == "k" else 0), :]
                dve.tensor_copy(dst[:, 1:1 + P], bank[i % 4][:, 0:P])
                dve.tensor_copy(dst[:, SEG[1]:SEG[1] + 256], bank[i % 4][:, P:T]).then_inc(proj_dve, 1)

            def conv(dst, src, w0, step, b):
                def tap(j):
                    return cols[:, w0 + step * j:w0 + step * j + 1]
                then(dve.tensor_scalar(dst[:, 1:1 + NPAD], src[:, 0:NPAD], tap(0), b, ALU.mult, ALU.add))
                for j in range(1, 4):
                    ins = dve.scalar_tensor_tensor(out=dst[:, 1:1 + NPAD - (j > 2)], in0=src[:, j:j + NPAD - (j > 2)],
                                                   scalar=tap(j), in1=dst[:, 1:1 + NPAD - (j > 2)],
                                                   op0=ALU.mult, op1=ALU.add)
                    if j < 3:
                        then(ins)
                return ins

            for m in range(4):
                odd_item(index[("xd", m)])
            for m in range(4):
                wait_kept(dve, index[("xd", m)])
                conv(xc[:, m, :], xdin[:, m, :], col["conv_d"] + m, 4,
                     cols[:, col["conv_d_b"] + m:col["conv_d_b"] + m + 1]).then_inc(xc_ready, 1)

            def rg_chain(d):
                a_, u_, tmp = rgb[2][:, :, 1:1 + NPAD], rgb[1][:, :, 1:1 + NPAD], rgb[3][:, :, 1:1 + NPAD]
                th = rgb[0][:, :, 1:1 + NPAD]
                dve.wait_ge(xc_ready, 4)
                wait_kept(dve, index[(f"rg{d}", 7)])
                then(dve.tensor_tensor(u_, u_, xc[:, :, 1:1 + NPAD], ALU.mult))
                dve.wait_ge(rg_exps, 8 * (d + 1))
                then(dve.tensor_scalar(tmp, th, 1.0, None, ALU.add))
                then(dve.reciprocal(tmp, tmp))
                dve.tensor_tensor(th, th, tmp, ALU.mult).then_inc(rg_ratio, 1)
                dve.wait_ge(rg_root, d + 1)
                then(dve.tensor_tensor(u_, u_, th, ALU.mult))
                out = hfw if d == 0 else rgb[3]
                for m in range(4):
                    for c_, w in ((SEG[0], P), (SEG[1], 256)):
                        init = cols[:, col["state_d_h"] + 4 * d + m:col["state_d_h"] + 4 * d + m + 1] if w == 256 else 0.0
                        fwd = slice(c_, c_ + w)
                        sl = fwd if d == 0 else slice(c_ + w - 1, c_ - 1, -1)
                        ins = dve.tensor_tensor_scan(out[:, m, sl], rgb[2][:, m, sl], rgb[1][:, m, sl], init,
                                                     ALU.mult, ALU.add)
                then(ins)
                last = SEG[0] + P - 1 if d == 0 else SEG[0]
                ins = dve.tensor_copy(fincols[:, 8 + 4 * d:12 + 4 * d].unsqueeze(2), out[:, :, last:last + 1])
                if d == 0:
                    ins.then_inc(rg_done, 1)
                    return
                then(ins)
                for c_, w, o in ((SEG[0], P, 0), (SEG[1], 256, P)):
                    then(dve.tensor_tensor(rgb[0][:, :, c_:c_ + w], hfw[:, :, c_:c_ + w], rgb[3][:, :, c_:c_ + w],
                                           ALU.add))
                    ins = dve.tensor_tensor(gd[:, :, o:o + w], gd[:, :, o:o + w], rgb[0][:, :, c_:c_ + w], ALU.mult)
                    if o == 0:
                        then(ins)
                ins.then_inc(rg_free, 1)

            wait_kept(dve, index[("gd", 3)])
            rg_chain(0)
            for m in range(4):
                odd_item(index[("q", m)])
            rg_chain(1)
            for m in range(4):
                odd_item(index[("k", m)])
            for m in range(8):
                i = index[("q" if m < 4 else "k", m % 4)]
                wait_kept(dve, i)
                conv(qkc[:, m, :], qkin[:, m, :], col["conv_c"] + m, 8, 0.0).then_inc(conv_ready, 1)

            dve.wait_ge(zeroed, 10)
            dve.wait_ge(gates_done, 1)
            ig, ff, t2, t3, lf, b_, nm = (rwork[:, k, :] for k in range(7))
            then(dve.tensor_scalar(ig, bank[4][0:36, 0:T], gbias[:, 0:1], None, ALU.add))
            then(dve.tensor_scalar(t3, bank[5][0:36, 0:T], gbias[:, 1:2], None, ALU.add))
            dve.scalar_tensor_tensor(out=ff, in0=t3, scalar=-1.0, in1=t3, op0=ALU.mult, op1=ALU.max)\
               .then_inc(row_abs, 1)
            dve.wait_ge(row_exp, 1)
            log1p_of(t2, ff, b_, nm, lf)
            then(dve.tensor_scalar(t3, t3, 0.0, None, ALU.min))
            then(dve.tensor_tensor(lf, t3, lf, ALU.subtract))

            def scan(out, src, op0, op1, first, init):
                for d in range(2):
                    pp = slice(32 * d, 32 * d + 4)
                    for lo, hi in ((0, P), (P, T)):
                        sl = slice(lo, hi) if d == 0 else slice(hi - 1, lo - 1 if lo else None, -1)
                        i0 = m0[pp, :] if init and lo else 0.0
                        f_ = cst[pp, C_ONE:C_ONE + hi - lo] if first is None else first[pp, sl]
                        ins = dve.tensor_tensor_scan(out[pp, sl], f_, src[pp, sl], i0, op0, op1)
                then(ins)

            then(dve.memset(b_, 0.0))
            scan(b_, lf, ALU.mult, ALU.add, None, False)
            then(dve.tensor_tensor(rows[:, 0, :], ig, b_, ALU.subtract))
            scan(nm, rows[:, 0, :], ALU.max, ALU.max, rows[:, 0, :], True)
            then(dve.tensor_tensor(t2, b_, nm, ALU.add))
            dve.tensor_scalar(nm, nm, -1.0, None, ALU.mult).then_inc(rows_m, 1)
            dve.wait_ge(rows_turned2, 1)
            then(dve.tensor_copy(colr[:, :, :], bank[6][:, 0:324].rearrange("p (k r) -> p k r", k=9)))
            dve.tensor_scalar(colr[:, WST:WST + 2, :], colr[:, WST:WST + 2, :], C_SCALE, None, ALU.mult)\
               .then_inc(colr_ready, 1)

            def mlstm_logs(u):
                h, d = munits[u]
                q, r = u % 2, 32 * d + h
                dve.wait_ge(nm_done, u + 1)
                for b, (s_, t, o_) in enumerate(blocks[d]):
                    src = bank[2 + q][:, P * t:P * t + P]
                    a_ = colr[:, ALOG + s_, r:r + 1]
                    mk = C_MF if d == 0 else C_MB
                    if s_ == t:
                        ins = dve.scalar_tensor_tensor(out=wt[:, q, o_:o_ + P], in0=src, scalar=a_,
                                                       in1=cst[:, mk:mk + P], op0=ALU.add, op1=ALU.min)
                    else:
                        ins = dve.tensor_scalar(wt[:, q, o_:o_ + P], src, a_, 0.0, ALU.add, ALU.min)
                ins.then_inc(wlog_ready, 1)

            dve.wait_ge(colr_ready, 1)
            dve.wait_ge(ktok_kept, 1)
            wait_kept(dve, index[("o", 2)])
            mlstm_logs(0)
            for u, (h, d) in enumerate(munits):
                q, r = u % 2, 32 * d + h
                dve.wait_ge(st_done, h + 1)
                dve.wait_ge(w_ready, u + 1)
                cut_ = 3 * P if d == 0 else 2 * P
                lo2 = P if d == 0 else 0
                dve.scalar_tensor_tensor(out=sw[:, q, 0:cut_], in0=bank[0][:, 0:cut_], scalar=C_SCALE,
                                         in1=wt[:, q, 0:cut_], op0=ALU.mult, op1=ALU.mult)
                dve.scalar_tensor_tensor(out=sw[:, q, cut_:512], in0=bank[1][:, lo2:256], scalar=C_SCALE,
                                         in1=wt[:, q, cut_:512], op0=ALU.mult, op1=ALU.mult).then_inc(sw_ready, 1)
                dve.tensor_scalar(kws[:, q, :], ktok[:, h, :], colr[:, WS, r:r + 1], None, ALU.mult)\
                   .then_inc(kws_ready, 1)
                if u + 1 < 8:
                    mlstm_logs(u + 1)
                dve.wait_ge(inter_kept, 2 * (u + 1))
                dve.wait_ge(cout_kept, u + 1)
                dve.tensor_copy(fincols[:, 4 * d + h:4 * d + h + 1], cout[:, q, P:P + 1]).then_inc(fin_ready, 1)
                then(dve.tensor_tensor(num[:, :], bank[4 + q][:, 129:387], inter[:, q, :], ALU.add))

                def row(t):
                    return bank[4 + q][:, 0:129] if t == 0 else num[:, 129 * (t - 1):129 * t]

                for t in range(NT):
                    ins = dve.tensor_scalar(den[:, 0, t:t + 1], row(t)[:, P:P + 1], -1.0, colr[:, ENM + t, r:r + 1],
                                            ALU.mult, ALU.max)
                then(ins)
                for t in range(NT):
                    ins = dve.tensor_tensor(den[:, 0, t:t + 1], den[:, 0, t:t + 1], row(t)[:, P:P + 1], ALU.max)
                then(ins)
                then(dve.reciprocal(den[:, 1, :], den[:, 0, :]))
                for t in range(NT):
                    dst = heads[:, t, P * h:P * h + P]
                    if d == 0:
                        ins = dve.tensor_scalar(dst, row(t)[:, 0:P], den[:, 1, t:t + 1], None, ALU.mult)
                    else:
                        ins = dve.scalar_tensor_tensor(out=dst, in0=row(t)[:, 0:P], scalar=den[:, 1, t:t + 1],
                                                       in1=dst, op0=ALU.mult, op1=ALU.add)
                ins.then_inc(h_ready, 1)
                if u < 7:
                    dve.wait_ge(h_ready, u + 1)
            dve.wait_ge(h_ready, 8)
            head_norm(1, sq_odd, sigo)
            turned_heads(1)
            norm_out(2)
            if stop == 3:
                return

            norm_in(3)
            dve.wait_ge(logits_done, 1)
            dve.wait_ge(router_in, 32)
            then(dve.tensor_tensor(lg[:, :, :], bank[6][:, 0:24].rearrange("p (t e) -> p t e", t=NT),
                                   rb[:, :].unsqueeze(1).to_broadcast([P, NT, N_EXP]), ALU.add))
            tie = cst[:, C_TIE:C_TIE + 64].rearrange("p (e j) -> p e j", e=N_EXP)
            for t in range(NT):
                lj = lg[:, t, :].unsqueeze(1).to_broadcast([P, N_EXP, N_EXP])
                le = lg[:, t, :].unsqueeze(2).to_broadcast([P, N_EXP, N_EXP])
                gt_, eq_ = (cmp[:, k, :].rearrange("p (e j) -> p e j", e=N_EXP) for k in range(2))
                then(dve.tensor_tensor(gt_, lj, le, ALU.is_gt))
                then(dve.tensor_tensor(eq_, lj, le, ALU.is_equal))
                then(dve.tensor_tensor(eq_, eq_, tie, ALU.mult))
                then(dve.tensor_tensor(gt_, gt_, eq_, ALU.add))
                then(dve.tensor_reduce(rank[:, t, :], gt_, AX.X, ALU.add))
            then(dve.tensor_scalar(oh[:, 0, :, :], rank[:, :, :], 0.0, None, ALU.is_equal))
            then(dve.tensor_scalar(oh[:, 1, :, :], rank[:, :, :], 1.0, None, ALU.is_equal))
            dve.tensor_tensor(oh[:, 2, :, :], oh[:, 0, :, :], oh[:, 1, :, :], ALU.add).then_inc(sel_ready, 1)

            def pick(dst, which, src):
                then(dve.tensor_tensor(rank[:, :, :], oh[:, which, :, :], src, ALU.mult))
                return dve.tensor_reduce(tk[:, dst, :], rank[:, :, :], AX.X, ALU.add)

            then(pick(0, 0, lg[:, :, :]))
            then(pick(1, 1, lg[:, :, :]))
            dve.tensor_tensor(tk[:, 4, :], tk[:, 1, :], tk[:, 0, :], ALU.subtract).then_inc(e1_in, 1)
            dve.wait_ge(e1_ready, 1)
            then(dve.tensor_scalar(tk[:, 7, :], tk[:, 5, :], 1.0, None, ALU.add))
            then(dve.reciprocal(tk[:, 6, :], tk[:, 7, :]))
            then(dve.tensor_tensor(tk[:, 7, :], tk[:, 5, :], tk[:, 6, :], ALU.mult))
            dve.wait_ge(pos_done, 1)
            cnt = bank[7][:, 24:32]
            then(dve.tensor_scalar(nb[:, 0, :], cnt, 0.0, None, ALU.is_gt))
            for j in range(1, NT):
                then(dve.scalar_tensor_tensor(out=nb[:, 0, :], in0=cnt, scalar=float(P * j), in1=nb[:, 0, :],
                                              op0=ALU.is_gt, op1=ALU.add))
            then(dve.tensor_tensor_scan(nb[:, 1, :], cst[:, C_ONE:C_ONE + N_EXP], nb[:, 0, :], 0.0, ALU.mult, ALU.add))
            then(dve.tensor_tensor(nb[:, 2, :], nb[:, 1, :], nb[:, 0, :], ALU.subtract))
            then(dve.tensor_scalar(nb[:, 3, :], nb[:, 2, :], float(P), None, ALU.mult))
            then(dve.tensor_tensor(gp[:, :, :], bank[7][:, 0:24].rearrange("p (t e) -> p t e", t=NT),
                                   nb[:, 3, :].unsqueeze(1).to_broadcast([P, NT, N_EXP]), ALU.add))
            then(pick(2, 0, gp[:, :, :]))
            then(pick(3, 1, gp[:, :, :]))
            wv = ewf[:, :].rearrange("p (w e) -> p w e", e=N_EXP)
            then(dve.tensor_tensor(wv, nb[0:1, 1, :].unsqueeze(1).to_broadcast([1, MAX_ITEMS, N_EXP]),
                                   cst[0:1, C_W:C_N].rearrange("p (w e) -> p w e", e=N_EXP), ALU.is_le))
            then(dve.tensor_reduce(ew1[:, 0:MAX_ITEMS], wv, AX.X, ALU.add))
            then(dve.tensor_scalar(ew1[:, 0:MAX_ITEMS], ew1[:, 0:MAX_ITEMS], float(N_EXP - 1), None, ALU.min))
            then(dve.tensor_copy(ew1[:, MAX_ITEMS:MAX_ITEMS + 1], nb[0:1, 1, N_EXP - 1:N_EXP]))
            dve.tensor_copy(ewi[:, :], ew1[:, :]).then_inc(plan_ready, 1)
            then(dve.tensor_copy(slot[:, :], cst[:, C_IOTA:C_IOTA + P]))

            def hot(step):
                for t in range(NT):
                    step(dve.tensor_scalar(onehot[:, t, :], slot[:, :], tk[:, 2, t:t + 1], None, ALU.is_equal), 0)
                    step(dve.tensor_scalar(gated[:, t, :], slot[:, :], tk[:, 2, t:t + 1], tk[:, 6, t:t + 1],
                                           ALU.is_equal, ALU.mult), 0)
                    step(dve.tensor_scalar(gtmp[:, t, :], slot[:, :], tk[:, 3, t:t + 1], tk[:, 7, t:t + 1],
                                           ALU.is_equal, ALU.mult), 1)
                for t in range(NT):
                    step(dve.scalar_tensor_tensor(out=onehot[:, t, :], in0=slot[:, :], scalar=tk[:, 3, t:t + 1],
                                                  in1=onehot[:, t, :], op0=ALU.is_equal, op1=ALU.add), 0)
                    ins = dve.tensor_tensor(gated[:, t, :], gated[:, t, :], gtmp[:, t, :], ALU.add)
                    if t < NT - 1:
                        step(ins, 0)
                ins.then_inc(hot_ready, 1)

            hot(lambda ins, w_: then(ins))
            dve.wait_ge(plan_ready, 1)
            n_work = dve.value_load(ewi[0:1, MAX_ITEMS:MAX_ITEMS + 1], min_val=1, max_val=MAX_ITEMS)
            dve.wait_ge(zeroed, 11)
            dve.memset(jk[:, 1, 0:1], 0.0).then_inc(yadd, 1)
            with dve.Fori(0, n_work) as w:
                c_ = [0]

                def chain(ins, w_=1):
                    c_[0] += 1
                    ins.then_inc(item_step, 1)
                    dve.wait_ge(item_step, w * ITEM_STEPS + c_[0])

                dve.wait_ge(gated_turned, w + 1)
                dve.tensor_copy(scat[:, :, :], bank[4][:, 0:T].rearrange("p (t s) -> p t s", t=NT))\
                   .then_inc(scat_ready, 1)
                for f in range(KE):
                    dve.wait_ge(eup_done, w * (2 * KE) + (2 * f + 2))
                    dve.wait_ge(esilu_ready, w * KE + (f + 1))
                    dve.tensor_tensor(act_e[:, f, :], sil_e[:, f % 2, :], bank[2 + f % 2][:, 0:P], ALU.mult)\
                       .then_inc(eprod_ready, 1)
                dve.wait_ge(hot_ready, w + 1)
                chain(dve.tensor_scalar(slot[:, :], slot[:, :], float(P), None, ALU.add))
                hot(chain)
                for j, (t, b) in enumerate(SCATTER):
                    dve.wait_ge(scat_done, w * 6 + (j + 1))
                    v = yacc[:, t, 512 * b:512 * b + 512]
                    dve.tensor_tensor(v, v, bank[SCAT_BANK[j]][:, :], ALU.add).then_inc(yadd, 1)
                assert c_[0] == ITEM_STEPS, c_[0]
            dve.memset(jk[:, 1, 0:1], 0.0).then_inc(yacc_ready, 1)
            norm_out(3)


_INS = ["x_prompt", "x_sample", "c", "cache_a_k", "cache_a_v", "cache_b_k", "cache_b_v", "state_c_C", "state_c_n",
        "state_c_m", "state_d_h", "c_ctx", "mod_w", "mod_b", "norm_g", "w_in_even", "w_out_even", "a_lam",
        "a_subln_g", "b_rpb", "ff_w1", "ff_w3", "ff_w2", "w_in_odd", "c_gate_b", "conv_c", "conv_d", "conv_d_b",
        "rg_wa", "rg_ba", "rg_wx", "rg_bx", "rg_lam", "c_norm_g", "w_out_odd", "router_w", "router_b",
        "moe_w1", "moe_w3", "moe_w2"]
_OUTS = [(1, 128, 1024), (1, 256, 1024), (1, 1, 128, 4, 128), (1, 1, 128, 4, 128), (1, 1, 128, 8, 64),
         (1, 1, 128, 8, 64), (1, 1, 2, 4, 128, 128), (1, 1, 2, 4, 128), (1, 1, 2, 4), (1, 1, 2, 512)]


def kernel(**inputs):
    import concourse.bacc as _bacc
    from concourse.bass_utils import run_bass_kernel_spmd as _run

    nc = _bacc.Bacc("TRN2", target_bir_lowering=False, num_devices=1)
    arrays, aps = {}, {}
    for name in _INS:
        a = np.ascontiguousarray(inputs[name])
        arrays[f"in_{name}_dram"] = a
        aps[name] = nc.dram_tensor(f"in_{name}_dram", a.shape, F32, kind="ExternalInput").ap()
    table = shape_constants()
    arrays["in_shape_constants_dram"] = table
    aps["shape_constants"] = nc.dram_tensor("in_shape_constants_dram", table.shape, F32, kind="ExternalInput").ap()
    outs = [nc.dram_tensor(f"out_{i}_dram", s, F32, kind="ExternalOutput").ap() for i, s in enumerate(_OUTS)]
    trunk_step(nc, aps, outs)
    r = _run(nc, [arrays], core_ids=[0])
    return tuple(r.results[0][f"out_{i}_dram"] for i in range(len(_OUTS)))
```

```python
import math
from contextlib import ExitStack

import numpy as np
import concourse.bass as bass
from concourse import mybir

F32 = mybir.dt.float32
I32 = mybir.dt.int32
F32R = mybir.dt.float32r
ALU = mybir.AluOpType
ACT = mybir.ActivationFunctionType
AX = mybir.AxisListType

P = 128
D = 1024
KD = D // P
NT = 3
T = NT * P
CONDS = 2
GRID_W = 64
A_HEADS, B_HEADS, HD = 4, 8, 64
C_HEADS = 4
FF = 2816
KF = FF // P
E_FF = 2048
KE = E_FF // P
N_EXP = 8
EPS = 1e-6
NEG = -1e30
LAM_INIT = 0.8 - 0.6 * math.exp(-0.3 * 0)
C_SCALE = 128 ** -0.5
RING = 3
E_RING = RING + 1
HALF = 2048
WHI = 4
USED0 = 8
MAX_ITEMS = (2 * T) // P + N_EXP - 1
SEG = (1, 132, 260)
PAD = 390
NPAD = 387

C_ID, C_ONE, C_ROT, C_COS, C_SIN, C_MF, C_MB = 0, 128, 384, 512, 768, 1024, 1152
C_SEL, C_CUM, C_TIE, C_IOTA, C_W = 1280, 2304, 2432, 2496, 2624
C_N = C_W + MAX_ITEMS * N_EXP


def shape_constants():
    c = np.zeros((P, C_N), np.float32)
    i = np.arange(P)
    c[:, C_ID:C_ID + P] = np.eye(P)
    c[:, C_ONE:C_ONE + 256] = 1.0
    j = (i // 16) % 2
    rot = np.zeros((P, P), np.float32)
    for m in range(P):
        if j[m] == 0:
            rot[m + 16, m] = -1.0
        else:
            rot[m - 16, m] = 1.0
    c[:, C_ROT:C_ROT + P] = rot
    t = np.arange(256)
    pos = np.stack([t // GRID_W, t % GRID_W]).astype(np.float32)
    freq = (10000.0 ** (-np.arange(0, 32, 2, dtype=np.float32) / 32)).astype(np.float32)
    ang = (pos[(i % 64) // 32] * freq[i % 16][:, None]).astype(np.float32)
    c[:, C_COS:C_COS + 256] = np.cos(ang)
    c[:, C_SIN:C_SIN + 256] = np.sin(ang)
    c[:, C_MF:C_MF + P] = np.where(i[None] >= i[:, None], 0.0, NEG)
    c[:, C_MB:C_MB + P] = np.where(i[None] <= i[:, None], 0.0, NEG)
    for u in range(8):
        c[32 * (u // 4) + u % 4, C_SEL + u * P:C_SEL + (u + 1) * P] = 1.0
    c[:, C_CUM:C_CUM + P] = i[:, None] < i[None]
    e = np.arange(N_EXP)
    c[:, C_TIE:C_TIE + 64] = (e[None] < e[:, None]).astype(np.float32).reshape(-1)
    c[:, C_IOTA:C_IOTA + P] = i[None]
    c[:, C_W:C_N] = np.repeat(np.arange(MAX_ITEMS), N_EXP)[None]
    return c


def trunk_step(nc, I, O):
    with ExitStack() as ctx:
        def sb(name, shape, dt=F32):
            return ctx.enter_context(nc.sbuf_tensor(name, shape, dt))

        def sem(name):
            return ctx.enter_context(nc.semaphore(name))

        bank = [ctx.enter_context(nc.psum_tensor(f"bank{i}", [P, 512], F32)) for i in range(8)]

        def shared_place():
            def names(end, dt):
                return [(f"ring{end}", [P, RING, 4096], dt), (f"xn{end}", [P, NT, D], dt),
                        (f"ht{end}", [P, KD, T], dt), (f"arena{end}", [P, 20800], dt)]

            with ExitStack() as first:
                parts = [first.enter_context(nc.sbuf_tensor(*a)) for a in names("_parts", F32R)]
            return [ctx.enter_context(nc.sbuf_tensor(*a)) for a in names("", F32)], parts

        (ring, xn, ht, arena), (ring_r, xn_r, ht_r, arena_r) = shared_place()
        x = sb("x", [P, NT, D])
        gb = sb("gb", [P, CONDS, D])
        cst = sb("cst", [P, C_N])
        rowt = sb("rowt", [P, 3, P])
        cols = sb("cols", [P, 3 * P])
        sc = sb("sc", [P, KD, 32])
        modc = sb("modc", [P, 2, 48, CONDS])
        acol = sb("acol", [P, 4, KD, CONDS])
        gcol = sb("gcol", [P, 4, KD, CONDS])
        ss = sb("ss", [P, 4, 3])
        sd = sb("sd", [P, 4, 3])
        rs = sb("rs", [P, 4, 3])
        ss2 = sb("ss2", [P, 4, 6])
        ssum = sb("ssum", [P, 4, 3])
        sd2 = sb("sd2", [P, 4, 3])
        rs2 = sb("rs2", [P, 4, 3])
        epsc = sb("epsc", [P, 1])
        hn = sb("hn", [P, 2, 3, 12])
        jk = sb("jk", [P, 2, 512])
        at_f = [0]

        def carve(n, at=None):
            o = at_f[0] if at is None else at
            if at is None:
                at_f[0] += n
            assert o + n <= 20800, (o, n)
            return arena[:, o:o + n]

        def carve_r(n):
            at_f[0] += n
            assert at_f[0] <= 20800, at_f[0]
            return arena_r[:, at_f[0] - n:at_f[0]]

        shear = nc.dram_tensor("shear", [B_HEADS, GRID_W, 7, GRID_W], F32, kind="Internal").ap()
        ident = cst[:, C_ID:C_ID + P]
        ones = cst[:, C_ONE:C_ONE + P]

        qat = carve(1536).rearrange("p (h t) -> p h t", h=4)
        kat = carve(2048).rearrange("p (h t) -> p h t", h=4)
        va = carve(2048).rearrange("p (t e) -> p t e", t=4)
        qbt = carve(1536).rearrange("p (h t) -> p h t", h=4)
        kbt = carve(2048).rearrange("p (h t) -> p h t", h=4)
        vb = carve(2048).rearrange("p (t e) -> p t e", t=4)
        bias = carve(6144).rearrange("p (q h k) -> p q h k", q=2, h=8)
        kcache = jk
        SQ0 = at_f[0]
        prob = carve(1536).rearrange("p (s k) -> p s k", s=4)
        pts = carve(768).rearrange("p (s k) -> p s k", s=2)
        ropec = pts[:, 0, 0:256], pts[:, 1, 0:256]
        ropes = kcache[:, 0, 0:256], kcache[:, 0, 256:512]
        knew = ht[:, 0:3, :].rearrange("p a b -> p (a b)")[:, 0:1024].rearrange("p (a e) -> p a e", a=2)
        heads = xn
        alam = sb("alam", [P, 256])
        lamc = sb("lamc", [P, 6])
        subg = sb("subg", [P, 2, P])
        nmx = sb("nmx", [P, 48])
        lsum = sb("lsum", [P, 48])
        rl = sb("rl", [P, 48])

        at_f[0] = 0
        actt = carve(KF * T).rearrange("p (f t) -> p f t", f=KF)
        silt = carve(2 * T).rearrange("p (s t) -> p s t", s=2)
        whi_dense = [carve_r(HALF) for _ in range(WHI)]
        hth = xn_r[:, :, :].rearrange("p a b -> p (a b)").rearrange("p (k t) -> p k t", k=KD)
        htl = ht_r[:, :, :]

        at_f[0] = 0
        qkin = carve(8 * PAD).rearrange("p (n t) -> p n t", n=8)
        qkc = carve(8 * PAD).rearrange("p (n t) -> p n t", n=8)
        gd = carve(4 * T).rearrange("p (n t) -> p n t", n=4)
        c0 = carve(8 * 129).rearrange("p (u e) -> p u e", u=8)
        shared = at_f[0]
        xdin = carve(4 * PAD).rearrange("p (n t) -> p n t", n=4)
        xc = carve(4 * PAD).rearrange("p (n t) -> p n t", n=4)
        rgb = [carve(4 * PAD).rearrange("p (n t) -> p n t", n=4) for _ in range(4)]
        wrg = carve(16 * P).rearrange("p (d g n m) -> p d g n m", d=2, g=2, n=4)
        hfw = xdin
        at_f[0] = shared
        vaug = carve(NT * 4 * 129).rearrange("p (t h e) -> p t h e", t=NT, h=4)
        sigo = carve(NT * 512).rearrange("p (t e) -> p t e", t=NT)
        rows = carve(4 * T)[0:36, :].rearrange("p (k t) -> p k t", k=4)
        rwork = carve(7 * T)[0:36, :].rearrange("p (k t) -> p k t", k=7)
        rowsall = arena[0:36, shared + NT * 4 * 129 + NT * 512:shared + NT * 4 * 129 + NT * 512 + 11 * T]
        SQ1 = at_f[0]
        wt = carve(2 * 512).rearrange("p (s k) -> p s k", s=2)
        sw = carve(2 * 512).rearrange("p (s k) -> p s k", s=2)
        ktok = carve(512).rearrange("p (h e) -> p h e", h=4)
        kws = carve(2 * P).rearrange("p (s e) -> p s e", s=2)
        inter = carve(2 * 258).rearrange("p (s e) -> p s e", s=2)
        num = carve(258)
        colr = carve(9 * 36).rearrange("p (k r) -> p k r", k=9)
        den = sb("den", [P, 2, 3])
        cout = sb("cout", [P, 2, 129])
        wg = sb("wg", [P, KD, 16])
        wgp = sb("wgp", [P, KD, 2, 36])
        gbias = sb("gbias", [36, 2])
        m0 = sb("m0", [36, 1])
        sp = sb("sp", [P, 6, 8])
        fincols = sb("fincols", [P, 16])
        finrows = sb("finrows", [8, 2, P])

        at_f[0] = 0
        htok = xn
        yacc = carve(NT * D).rearrange("p (t d) -> p t d", t=NT)
        xgh, xgl = (carve_r(D).rearrange("p (k s) -> p k s", k=KD) for _ in range(2))
        aeh, ael = (carve_r(KE * P).rearrange("p (f s) -> p f s", f=KE) for _ in range(2))
        a_tok = carve(2 * 256).rearrange("p (b f) -> p b f", b=2)
        sil_e = jk[:, 0, :].rearrange("p (b f) -> p b f", b=2)
        og = arena[:, NT * D:NT * D + D]
        ht_flat = ht[:, :, :].rearrange("p a b -> p (a b)")
        onehot, scat = (ht_flat[:, HALF + T * n_:HALF + T * n_ + T].rearrange("p (t s) -> p t s", t=NT)
                        for n_ in range(2))
        slot = ht_flat[:, HALF + 2 * T:HALF + 2 * T + P]
        gated = carve(NT * P).rearrange("p (t s) -> p t s", t=NT)
        gtmp = carve(NT * P).rearrange("p (t s) -> p t s", t=NT)
        ring_last = at_f[0]
        at_f[0] += 2 * HALF
        whi_moe = [carve_r(HALF) for _ in range(WHI - 1)]
        whi_moe.append(ht_r[:, :, :].rearrange("p a b -> p (a b)")[:, 0:HALF])
        rw = sb("rw", [P, KD, N_EXP])
        rb = sb("rb", [P, N_EXP])
        lg = sb("lg", [P, NT, N_EXP])
        cmp = sb("cmp", [P, 2, 64])
        rank = sb("rank", [P, NT, N_EXP])
        oh = sb("oh", [P, 3, NT, N_EXP])
        gp = sb("gp", [P, NT, N_EXP])
        tk = sb("tk", [P, 8, NT])
        nb = sb("nb", [P, 6, N_EXP])
        ewf = sb("ewf", [1, MAX_ITEMS * N_EXP])
        ew1 = sb("ew1", [1, MAX_ITEMS + 1])
        ewi = sb("ewi", [1, MAX_ITEMS + 1], I32)

        def vec(ap, pat, **kw):
            return ap.rearrange(pat, **kw)

        row_params = [
            ("c_ctx", 8, vec(I["c_ctx"], "(k p) -> k p", p=P)),
            ("c", 8, vec(I["c"], "b (k p) -> (b k) p", p=P)),
            ("mod_b", 96, vec(I["mod_b"], "l (k p) -> (l k) p", p=P)),
            ("norm_g", 64, vec(I["norm_g"], "l g (k p) -> (l g k) p", p=P)),
            ("conv_c", 32, vec(I["conv_c"], "o j (k p) -> (o j k) p", p=P)),
            ("conv_d", 16, vec(I["conv_d"], "o j (k p) -> (o j k) p", p=P)),
            ("conv_d_b", 4, vec(I["conv_d_b"], "o (k p) -> (o k) p", p=P)),
            ("rg_ba", 8, vec(I["rg_ba"], "o d (k p) -> (o d k) p", p=P)),
            ("rg_bx", 8, vec(I["rg_bx"], "o d (k p) -> (o d k) p", p=P)),
            ("rg_lam", 8, vec(I["rg_lam"], "o d (k p) -> (o d k) p", p=P)),
            ("state_d_h", 8, vec(I["state_d_h"], "b o d (k p) -> (b o d k) p", p=P)),
            ("state_c_n", 8, vec(I["state_c_n"], "b o d h k -> (b o d h) k")),
        ]
        col, row_dmas, at = {}, [], 0
        for name, n, src in row_params:
            col[name] = at
            done = 0
            while done < n:
                m = min(n - done, P - at % P)
                row_dmas.append((at // P, at % P, m, src[done:done + m, :]))
                done += m
                at += m
        n_rows = at
        last_rows = n_rows - 2 * P

        def cut(w, c0_, n):
            return w.rearrange("(k p) n -> p k n", p=P)[:, :, c0_:c0_ + n]

        def rows_cut(w, k0, n):
            return w.rearrange("(k p) n -> p k n", p=P)[:, k0:k0 + n, :]

        def mod_panel(m):
            return ("mod", m), [("k512", cut(I["mod_w"][m // 12], (m % 12) * 512, 512))]

        panels = [mod_panel(m) for m in range(6)]
        panels += [(("in0", j), [("k512", cut(I["w_in_even"][0], 512 * j, 512))]) for j in range(6)]
        panels += [mod_panel(m) for m in range(6, 24)]
        panels += [(("out0", j), [("k512", cut(I["w_out_even"][0], 512 * j, 512))]) for j in range(2)]
        panels += [(("up", j), [("lo256", cut(I["ff_w1"][0], 256 * j, 256)),
                                ("hi256", cut(I["ff_w3"][0], 256 * j, 256))]) for j in range(KF // 2)]
        panels += [(("down", j), [("rows", rows_cut(I["ff_w2"][0], 4 * j, min(4, KF - 4 * j)))])
                   for j in range((KF + 3) // 4)]
        for j, c_ in enumerate((2064, 2576, 0, 512, 1024, 1536)):
            panels.append((("in1", j), [("k512", cut(I["w_in_odd"][0], c_, 512))]))
        panels += [(("out1", j), [("k512", cut(I["w_out_odd"][0], 512 * j, 512))]) for j in range(2)]
        UP, DOWN = E_FF // 256, KE // 4
        ITEM = UP + DOWN
        number = {key: i for i, (key, _) in enumerate(panels)}
        NP0 = len(panels)
        landed = [0] * RING
        need = []
        for i, (_, parts) in enumerate(panels):
            landed[i % RING] += 16 * len(parts)
            need.append(landed[i % RING])
        slot_item = [0] * E_RING
        item_need = []
        for j in range(ITEM):
            slot_item[j % E_RING] += 16 * (2 if j < UP else 1)
            item_need.append(slot_item[j % E_RING])

        def place(i, where, n=4):
            r = ring[:, i % RING, :]
            if where == "rows":
                return r[:, 0:n * D].rearrange("p (k n) -> p k n", k=n)
            r = r.rearrange("p (k n) -> p k n", k=KD)
            return {"k512": r, "lo256": r[:, :, 0:256], "hi256": r[:, :, 256:512]}[where]

        def panel_half(i, h):
            return ring[:, i % RING, HALF * h:HALF * h + HALF]

        def low_half(i, h):
            return ring_r[:, i % RING, HALF * h:HALF * h + HALF]

        def parts_of(i, h, whi, k):
            return (whi[(2 * i + h) % WHI].rearrange("p (k n) -> p k n", k=k),
                    low_half(i, h).rearrange("p (k n) -> p k n", k=k))

        def e_panel(j, low=False):
            buf, big = (ring_r, arena_r) if low else (ring, arena)
            return buf[:, j % E_RING, :] if j % E_RING < RING else big[:, ring_last:ring_last + 2 * HALF]

        def e_half(j, h, low=False):
            return e_panel(j, low)[:, HALF * h:HALF * h + HALF]

        def e_parts(j, h, k):
            return (whi_moe[(2 * j + h) % WHI].rearrange("p (k n) -> p k n", k=k),
                    e_half(j, h, low=True).rearrange("p (k n) -> p k n", k=k))

        x_in, cst_in, rows_in = sem("x_in"), sem("cst_in"), sem("rows_in")
        small_in, even_in, bias_in = sem("small_in"), sem("even_in"), sem("bias_in")
        odd_in, c0_in, wrg_in, router_in = sem("odd_in"), sem("c0_in"), sem("wrg_in"), sem("router_in")
        panel_in = [sem(f"panel_in{i}") for i in range(RING)]
        e_panel_in = [sem(f"e_panel_in{i}") for i in range(E_RING)]
        zeroed, masked = sem("zeroed"), sem("masked")
        rows_turned, cols_ready, sc_ready = sem("rows_turned"), sem("cols_ready"), sem("sc_ready")
        sc_clear = sem("sc_clear")
        mod_kept, mod_turned = sem("mod_kept"), sem("mod_turned")
        mod_done, mod_added, gains_ready = sem("mod_done"), sem("mod_added"), sem("gains_ready")
        x_ready, roots_ready, xn_ready = sem("x_ready"), sem("roots_ready"), sem("xn_ready")
        xn_turned, ht_act, ht_dve = sem("xn_turned"), sem("ht_act"), sem("ht_dve")
        gb_made, gb_kept = sem("gb_made"), sem("gb_kept")
        proj_done, proj_act, proj_dve = sem("proj_done"), sem("proj_act"), sem("proj_dve")
        aux_done, aux_kept = sem("aux_done"), sem("aux_kept")
        cos_part, rot_done, roped = sem("cos_part"), sem("rot_done"), sem("roped")
        lam_sums, lam_exps = sem("lam_sums"), sem("lam_exps")
        scores_done, max_ready, exp_done = sem("scores_done"), sem("max_ready"), sem("exp_done")
        probs_ready, probs_turned, pts_ready = sem("probs_ready"), sem("probs_turned"), sem("pts_ready")
        pv_done, o_kept = sem("pv_done"), sem("o_kept")
        hsq_ready, hsum_ready, hroot_ready, heads_ready = (
            sem("hsq_ready"), sem("hsum_ready"), sem("hroot_ready"), sem("heads_ready"))
        o_turned, ot_act, ot_dve = sem("o_turned"), sem("ot_act"), sem("ot_dve")
        out_done, sq2_ready, sum2_ready, root2_ready = (
            sem("out_done"), sem("sq2_ready"), sem("sum2_ready"), sem("root2_ready"))
        up_done, gate_done, silu_ready, prod_ready = (
            sem("up_done"), sem("gate_done"), sem("silu_ready"), sem("prod_ready"))
        act_step, dve_step, pool_step = sem("act_step"), sem("dve_step"), sem("pool_step")
        stored = sem("stored")
        xc_ready, rg_done, rg_act = sem("xc_ready"), sem("rg_done"), sem("rg_act")
        rg_exps, rg_ratio, rg_root, rg_free = sem("rg_exps"), sem("rg_ratio"), sem("rg_root"), sem("rg_free")
        sp_abs, sp_exp, wgp_ready = sem("sp_abs"), sem("sp_exp"), sem("wgp_ready")
        conv_ready, qk_ready = sem("conv_ready"), sem("qk_ready")
        gates_done, row_abs, row_exp, rows_m, rows_exp = (
            sem("gates_done"), sem("row_abs"), sem("row_exp"), sem("rows_m"), sem("rows_exp"))
        rows_turned2, colr_ready, ktok_done, ktok_kept = (
            sem("rows_turned2"), sem("colr_ready"), sem("ktok_done"), sem("ktok_kept"))
        st_done, nm_done, wlog_ready, w_ready, sw_ready = (
            sem("st_done"), sem("nm_done"), sem("wlog_ready"), sem("w_ready"), sem("sw_ready"))
        kws_ready, mm_done, inter_kept, h_ready = sem("kws_ready"), sem("mm_done"), sem("inter_kept"), sem("h_ready")
        cout_kept, c_stored, fin_ready, fin_turned, fin_kept = (
            sem("cout_kept"), [sem("c_stored0"), sem("c_stored1")], sem("fin_ready"), sem("fin_turned"), sem("fin_kept"))
        logits_done, tok_turned, htok_ready = sem("logits_done"), sem("tok_turned"), sem("htok_ready")
        e1_in, e1_ready, sel_ready, pos_done, plan_ready = (
            sem("e1_in"), sem("e1_ready"), sem("sel_ready"), sem("pos_done"), sem("plan_ready"))
        item_step, yadd, rates_ready, down_done = sem("item_step"), sem("yadd"), sem("rates_ready"), sem("down_done")
        hot_ready, gath_done, gated_turned, scat_ready = (
            sem("hot_ready"), sem("gath_done"), sem("gated_turned"), sem("scat_ready"))
        whi_ready, wlo_ready, half_used = sem("whi_ready"), sem("wlo_ready"), sem("half_used")
        hth_ready, htl_ready = sem("hth_ready"), sem("htl_ready")
        xgh_ready, xgl_ready = sem("xgh_ready"), sem("xgl_ready")
        act_turned, aeh_ready, ael_ready = sem("act_turned"), sem("aeh_ready"), sem("ael_ready")
        esilu_ready, eprod_ready = sem("esilu_ready"), sem("eprod_ready")
        og_ready, scat_done, yacc_ready = (
            sem("og_ready"), sem("scat_done"), sem("yacc_ready"))

        shear_in, cst_rest_in = sem("shear_in"), sem("cst_rest_in")
        even_items = ([("qa", n, "A") for n in range(4)] + [("ka", n, "D") for n in range(4)] +
                      [("va", t, "A") for t in range(3)] + [("qb", n, "A") for n in range(4)] +
                      [("kb", n, "D") for n in range(4)] + [("vb", t, "A") for t in range(3)])
        odd_items = ([("xd", n, "AD"[n % 2]) for n in range(4)] + [("gd", n, "A") for n in range(4)] +
                     [("rg0", n, "A") for n in range(8)] + [("q", n, "AD"[n % 2]) for n in range(4)] +
                     [("rg1", n, "A") for n in range(8)] + [("k", n, "AD"[n % 2]) for n in range(4)] +
                     [("v", t, "A") for t in range(3)] + [("o", t, "A") for t in range(3)])
        items = even_items + odd_items
        index = {it[:2]: i for i, it in enumerate(items)}

        def kept_by(i):
            out = []
            if "A" in items[i][2]:
                out.append((proj_act, sum("A" in it[2] for it in items[:i + 1])))
            if "D" in items[i][2]:
                out.append((proj_dve, sum("D" in it[2] for it in items[:i + 1])))
            return out

        def wait_kept(eng, i):
            for s_, v_ in kept_by(i):
                eng.wait_ge(s_, v_)

        units = [("a", h, t, 2 * (3 * h + t)) for h in range(A_HEADS) for t in range(NT)]
        units += [("b", h, t, 24 + 3 * h + t) for h in range(B_HEADS) for t in range(NT)]
        NU = len(units)

        def keys(t):
            return (0, P) if t == 0 else (P, 4 * P)

        def slots(u):
            k_, _, _, s_ = units[u]
            return (s_, s_ + 1) if k_ == "a" else (s_,)

        def mod_bank(m):
            return 5 if m < 6 and m % 2 else 7

        def turn_bank(m):
            return 4 if m < 6 else 7

        def mod_row(m):
            return gb[:, m % 2, 0:512] if m < 6 else jk[:, m % 2, :]

        def mod_at(i):
            return 6 + i // 2 if i % 2 == 0 and i // 2 < 18 else None

        def turn_at(i):
            return 6 + i // 2 if i % 2 == 1 and i // 2 < 18 else None

        munits = [(h, d) for h in range(C_HEADS) for d in range(2)]
        blocks = {0: ((0, 0, 0), (1, 1, P), (1, 2, 2 * P), (2, 2, 3 * P)),
                  1: ((0, 0, 0), (1, 1, P), (2, 1, 2 * P), (2, 2, 3 * P))}
        ALOG, WST, ENM, WS = 0, 3, 5, 8

        OUT_BASE = {0: 0, 2: 6}
        N_DOWN0 = (KF + 3) // 4
        SCATTER = ((1, 0), (1, 1), (2, 0), (0, 0), (0, 1), (2, 1))
        SCAT_BANK = (2, 3, 4, 0, 1, 5)
        ITEM_STEPS = 15
        sq_even = arena[:, SQ0:SQ0 + NT * 512]
        sq_odd = arena[:, SQ1:SQ1 + NT * 512]

        def released(i):
            (what, j) = panels[i][0]
            if what == "mod":
                return mod_done, j + 1
            if what == "up":
                return up_done, 2 * (j + 1)
            if what == "down":
                return down_done, j + 1
            if what in ("out0", "out1"):
                return out_done, OUT_BASE[2 * int(what[3])] + 3 * (j + 1)
            last = [("qa", 3), ("ka", 3), ("va", 2), ("qb", 3), ("kb", 3), ("vb", 2)] if what == "in0" else \
                   [("xd", 3), ("gd", 3), ("q", 3), ("k", 3), ("v", 2), ("o", 2)]
            return proj_done, index[last[j]] + 1

        block = ctx.enter_context(nc.Block())

        @block.sync
        def _(sp_):
            sp_.wait_ge(rows_in, 16 * len(row_dmas))
            for i, (_, parts) in enumerate(panels):
                if i >= RING:
                    sp_.wait_ge(*released(i - RING))
                if i == RING:
                    sp_.dma_start(x[:, 0, :], I["x_prompt"][0]).then_inc(x_in, 16)
                    sp_.dma_start(x[:, 1:3, :], I["x_sample"][0].rearrange("(t p) d -> p t d", p=P))\
                       .then_inc(x_in, 16)
                for where, src in parts:
                    sp_.dma_start(place(i, where, src.shape[1]), src).then_inc(panel_in[i % RING], 16)
            for i in range(NP0 - RING, NP0):
                sp_.wait_ge(*released(i))
            sp_.wait_ge(plan_ready, 1)
            n_work = sp_.value_load(ewi[0:1, MAX_ITEMS:MAX_ITEMS + 1], min_val=1, max_val=MAX_ITEMS)
            with sp_.Fori(0, n_work) as w:
                e = sp_.value_load(ewi[0:1, bass.ds(w, 1)], min_val=0, max_val=N_EXP - 1)
                for j in range(ITEM):
                    sp_.wait_ge(half_used, w * (2 * ITEM) + (USED0 + 2 * (j - E_RING + 1)))
                    if j < UP:
                        for c_, src in ((0, I["moe_w1"]), (256, I["moe_w3"])):
                            s_ = src[0, bass.ds(e, 1)].rearrange("o (k p) n -> p (o k) n", p=P)
                            dst = e_panel(j).rearrange("p (k n) -> p k n", k=KD)[:, :, c_:c_ + 256]
                            sp_.dma_start(dst, s_[:, :, 256 * j:256 * j + 256]).then_inc(e_panel_in[j % E_RING], 16)
                    else:
                        s_ = I["moe_w2"][0, bass.ds(e, 1)].rearrange("o (k p) n -> p (o k) n", p=P)
                        dst = e_panel(j).rearrange("p (k n) -> p k n", k=4)
                        sp_.dma_start(dst, s_[:, 4 * (j - UP):4 * (j - UP) + 4, :]).then_inc(e_panel_in[j % E_RING], 16)
            sp_.wait_ge(x_ready, 10)
            sp_.dma_start(O[0][0], x[:, 0, :]).then_inc(stored, 16)
            sp_.wait_ge(x_ready, 12)
            sp_.dma_start(O[1][0].rearrange("(t p) d -> p t d", p=P), x[:, 1:3, :]).then_inc(stored, 16)
            sp_.wait_ge(stored, 16 * (4 + 2 + 2 + 2))
            for c_ in c_stored:
                sp_.wait_ge(c_, 4 * 16)

        @block.gpsimd
        def _(pool):
            n = [0]

            def then(ins):
                n[0] += 1
                ins.then_inc(pool_step, 1)
                pool.wait_ge(pool_step, n[0])

            pool.memset(epsc[:, :], EPS).then_inc(zeroed, 1)
            pool.wait_ge(zeroed, 1)
            pool.memset(bias[:, :, :, 256:384], 0.0).then_inc(zeroed, 1)
            pool.wait_ge(zeroed, 2)
            pool.memset(wgp[:, :, :, :], 0.0).then_inc(zeroed, 1)
            pool.wait_ge(zeroed, 3)
            pool.memset(gbias[:, :], 0.0).then_inc(zeroed, 1)
            pool.wait_ge(zeroed, 4)
            pool.memset(m0[:, :], 0.0).then_inc(zeroed, 1)
            pool.wait_ge(zeroed, 5)
            pool.wait_ge(bias_in, 16 * 4)
            for half in range(2):
                v = bias[64 * half:64 * half + 64, :, :, 0:256].rearrange("p q h (r c) -> p (q h) r c", r=4)
                lo = v[:, :, :, 0:48]
                hi = v[:, :, :, 16:64]
                for qh in range(16):
                    then(pool.affine_select(out=lo[:, qh], in_=lo[:, qh], compare_op=ALU.is_ge, fill=NEG,
                                            base=8, pattern=[[0, 4], [1, 48]], channel_multiplier=-1))
                    ins = pool.affine_select(out=hi[:, qh], in_=hi[:, qh], compare_op=ALU.is_gt, fill=NEG,
                                             base=8 - 16, pattern=[[0, 4], [-1, 48]], channel_multiplier=1)
                    if qh < 15 or half == 0:
                        then(ins)
            ins.then_inc(masked, 1)
            pool.wait_ge(masked, 1)
            pool.wait_ge(cst_rest_in, 16)
            for j in range(8):
                src = qat if j < 4 else kat
                wait_kept(pool, index[("qa" if j < 4 else "ka", j % 4)])
                if j >= 2:
                    pool.wait_ge(roped, j - 1)
                pool.tensor_tensor(ropec[j % 2], src[:, j % 4, P:3 * P], cst[:, C_COS:C_COS + 256], ALU.mult)\
                    .then_inc(cos_part, 1)
                pool.wait_ge(cos_part, j + 1)
            pool.wait_ge(x_ready, 6)
            pool.memset(xdin[:, :, :], 0.0).then_inc(zeroed, 1)
            pool.wait_ge(zeroed, 6)
            pool.memset(qkin[:, :, :], 0.0).then_inc(zeroed, 1)
            pool.wait_ge(zeroed, 7)
            pool.memset(wrg[:, :, :, :, :], 0.0).then_inc(zeroed, 1)
            pool.wait_ge(zeroed, 8)
            pool.wait_ge(rg_free, 1)
            pool.memset(rowsall, 0.0).then_inc(zeroed, 1)
            pool.wait_ge(zeroed, 9)
            pool.memset(vaug[:, :, :, 128:129], 1.0).then_inc(zeroed, 1)
            pool.wait_ge(zeroed, 10)
            pool.wait_ge(x_ready, 9)
            pool.memset(yacc[:, :, :], 0.0).then_inc(zeroed, 1)
            pool.wait_ge(zeroed, 11)

        @block.scalar
        def _(act):
            n = [0]

            def then(ins):
                n[0] += 1
                ins.then_inc(act_step, 1)
                act.wait_ge(act_step, n[0])

            act.dma_start(ident, I["shape_constants"][:, C_ID:C_ID + P]).then_inc(cst_in, 16)
            for t_, p_, m_, src in row_dmas:
                act.dma_start(rowt[p_:p_ + m_, t_, :], src).then_inc(rows_in, 16)
            act.wait_ge(cols_ready, 1)
            act.wait_ge(sc_clear, 1)
            act.activation(sc[:, :, 0], cols[:, col["c_ctx"]:col["c_ctx"] + 8], ACT.Silu).then_inc(sc_ready, 1)
            act.activation(sc[:, :, 1], cols[:, col["c"]:col["c"] + 8], ACT.Silu).then_inc(sc_ready, 1)
            act.dma_start(cst[:, P:C_N], I["shape_constants"][:, P:C_N]).then_inc(cst_rest_in, 16)
            act.dma_start(alam[:, :], bass.AP(tensor=I["a_lam"].tensor, offset=0, ap=[[0, P], [1, 256]]))\
               .then_inc(small_in, 16)
            act.dma_start(subg[:, 0, :], bass.AP(tensor=I["a_subln_g"].tensor, offset=0, ap=[[0, P], [1, P]]))\
               .then_inc(small_in, 16)
            act.dma_start(subg[:, 1, :], bass.AP(tensor=I["c_norm_g"].tensor, offset=0, ap=[[0, P], [1, P]]))\
               .then_inc(small_in, 16)
            act.dma_start(kcache[:, 0, :], I["cache_a_k"][0, 0].rearrange("s h e -> s (h e)")).then_inc(even_in, 16)
            act.dma_start(kcache[:, 1, :], I["cache_b_k"][0, 0].rearrange("s h e -> s (h e)")).then_inc(even_in, 16)
            act.dma_start(va[:, 3, :], I["cache_a_v"][0, 0].rearrange("s h e -> s (h e)")).then_inc(even_in, 16)
            act.dma_start(vb[:, 3, :], I["cache_b_v"][0, 0].rearrange("s h e -> s (h e)")).then_inc(even_in, 16)
            for k_ in range(7):
                act.dma_start(shear[:, :, k_, :],
                              bass.AP(tensor=I["b_rpb"].tensor, offset=(k_ + 4) * 31 + 15,
                                      ap=[[465, B_HEADS], [-1, GRID_W], [1, GRID_W]])).then_inc(shear_in, 16)
            act.wait_ge(shear_in, 16 * 7)
            for q in range(2):
                for half in range(2):
                    k_ = 3 - (2 * q + half)
                    act.dma_start(
                        bias[64 * half:64 * half + 64, q, :, 0:256].rearrange("p h (r c) -> p h r c", r=4),
                        shear[:, :, k_:k_ + 4, :].rearrange("h c r k -> c h r k")).then_inc(bias_in, 16)
            act.dma_start(wg[:, :, :], cut(I["w_in_odd"][0], 2048, 16)).then_inc(odd_in, 16)
            act.dma_start(rw[:, :, :], I["router_w"][0].rearrange("(k p) e -> p k e", p=P)).then_inc(router_in, 16)
            act.dma_start(rb[:, :], bass.AP(tensor=I["router_b"].tensor, offset=0, ap=[[0, P], [1, N_EXP]]))\
               .then_inc(router_in, 16)
            act.wait_ge(zeroed, 5)
            for d in range(2):
                for g in range(2):
                    act.dma_start(gbias[32 * d:32 * d + 4, g:g + 1],
                                  bass.AP(tensor=I["c_gate_b"].tensor, offset=8 * d + 4 * g, ap=[[1, 4], [1, 1]]))\
                       .then_inc(odd_in, 16)
                act.dma_start(m0[32 * d:32 * d + 4, :],
                              bass.AP(tensor=I["state_c_m"].tensor, offset=4 * d, ap=[[1, 4], [1, 1]]))\
                   .then_inc(odd_in, 16)

            def split_up(j):
                i = number[("up", j)]
                act.wait_ge(panel_in[i % RING], need[i])
                if j >= 2:
                    act.wait_ge(up_done, 2 * (j - 1))
                for h in range(2):
                    act.activation(whi_dense[(2 * i + h) % WHI], panel_half(i, h), ACT.Copy).then_inc(whi_ready, 1)

            def norm_in(s):
                for t in range(NT):
                    if s == 0:
                        act.wait_ge(x_in, 32)
                    else:
                        act.wait_ge(x_ready, 3 * (s - 1) + t + 1)
                    ins = act.activation(xn[:, t, :], x[:, t, :], ACT.Square, accum_out=ss[:, s, t:t + 1])
                then(ins)
                act.activation(sd[:, s, :], ss[:, s, :], ACT.Sqrt, scale=1.0 / D, bias=epsc[:, :])\
                   .then_inc(roots_ready, 1)
                act.wait_ge(gains_ready, s + 1)
                for k in range(0, KD, 2):
                    act.wait_ge(xn_turned, 8 * s + k + 1)
                    for c_, (lo, hi) in enumerate(((0, P), (P, T))):
                        ins = act.activation(ht[:, k, lo:hi], bank[k % 4][:, lo:hi], ACT.Identity,
                                             scale=acol[:, s, k, c_:c_ + 1],
                                             bias=modc[:, s // 2, 24 * (s % 2) + k, c_:c_ + 1])
                    ins.then_inc(ht_act, 1)
                for c_ in range(CONDS):
                    act.wait_ge(gb_made, 2 * s + c_ + 1)
                    act.activation(gb[:, c_, 0:512], bank[4][:, :], ACT.Copy)
                    act.activation(gb[:, c_, 512:1024], bank[5][:, :], ACT.Copy).then_inc(gb_kept, 1)

            def norm_out(s):
                for n_ in range(2):
                    for t in range(NT):
                        if s in (0, 2):
                            act.wait_ge(out_done, OUT_BASE[s] + 3 * n_ + t + 1)
                        elif s == 1:
                            act.wait_ge(down_done, N_DOWN0)
                        src = yacc[:, t, 512 * n_:512 * n_ + 512] if s == 3 else bank[2 * t + n_][:, :]
                        ins = act.activation(xn[:, t, 512 * n_:512 * n_ + 512], src, ACT.Square,
                                             accum_out=ss2[:, s, 2 * t + n_:2 * t + n_ + 1])
                ins.then_inc(sq2_ready, 1)
                act.wait_ge(sum2_ready, s + 1)
                act.activation(sd2[:, s, :], ssum[:, s, :], ACT.Sqrt, scale=1.0 / D, bias=epsc[:, :])\
                   .then_inc(root2_ready, 1)

            def head_norm(m):
                for t in range(NT):
                    sq = (sq_even, sq_odd)[m]
                    ins = act.activation(sq[:, 512 * t:512 * t + 512], heads[:, t, 0:512], ACT.Square)
                ins.then_inc(hsq_ready, 1)
                act.wait_ge(hsum_ready, m + 1)
                act.activation(hn[:, m, 1, :], hn[:, m, 0, :], ACT.Sqrt, scale=1.0 / P, bias=epsc[:, :])\
                   .then_inc(hroot_ready, 1)

            def turned_heads(m):
                for k in range(0, 8 if m == 0 else 4, 2):
                    act.wait_ge(o_turned, (0 if m == 0 else 8) + k + 1)
                    act.activation(ht[:, k, :], bank[k % 4][:, 0:T], ACT.Copy).then_inc(ot_act, 1)

            def keep_mod(m):
                act.wait_ge(mod_done, m + 1)
                if m >= 2:
                    act.wait_ge(mod_turned, m - 1)
                act.activation(mod_row(m), bank[mod_bank(m)][:, :], ACT.Copy).then_inc(mod_kept, 1)

            for m in range(6):
                keep_mod(m)
            act.wait_ge(zeroed, 1)
            norm_in(0)
            act.wait_ge(lam_sums, 1)
            act.activation(lamc[:, 2:4], lamc[:, 0:2], ACT.Exp).then_inc(lam_exps, 1)

            def keep_aux(i, dst, n_):
                act.wait_ge(aux_done, i + 1)
                act.activation(dst, bank[6][:, 0:n_].rearrange("p (h t) -> p h t", h=4), ACT.Copy)\
                   .then_inc(aux_kept, 1)

            keep_aux(0, kat[:, :, 3 * P:4 * P], 512)
            keep_aux(1, kbt[:, :, 3 * P:4 * P], 512)
            for i, (what, t, _) in enumerate(even_items):
                if "A" not in even_items[i][2]:
                    continue
                act.wait_ge(proj_done, i + 1)
                src = bank[i % 4]
                if what in ("qa", "qb"):
                    dst = (qat if what == "qa" else qbt)[:, t, :]
                    act.activation(dst, src[:, 0:T], ACT.Copy, scale=HD ** -0.5).then_inc(proj_act, 1)
                else:
                    act.activation((va if what == "va" else vb)[:, t, :], src[:, :], ACT.Copy).then_inc(proj_act, 1)
            act.wait_ge(aux_done, 3)
            keep_aux(2, knew[:, 0, :].rearrange("p (h t) -> p h t", h=4), 512)
            keep_aux(3, knew[:, 1, :].rearrange("p (h t) -> p h t", h=4), 512)
            act.wait_ge(aux_kept, 4)
            act.dma_start(O[2][0, 0].rearrange("s h e -> s (h e)"), knew[:, 0, :]).then_inc(stored, 16)
            act.dma_start(O[4][0, 0].rearrange("s h e -> s (h e)"), knew[:, 1, :]).then_inc(stored, 16)
            wait_kept(act, index[("vb", 2)])
            act.dma_start(O[3][0, 0].rearrange("s h e -> s (h e)"), va[:, 0, :]).then_inc(stored, 16)
            act.dma_start(O[5][0, 0].rearrange("s h e -> s (h e)"), vb[:, 0, :]).then_inc(stored, 16)

            for i in range(NU + 1):
                if i < NU:
                    kind, h, t, _ = units[i]
                    nk = keys(t)[1] - keys(t)[0]
                    if i >= 2:
                        act.wait_ge(probs_turned, i - 1)
                    for j in slots(i):
                        act.wait_ge(max_ready, j + 1)
                        src = prob[:, j % 4, 0:nk] if kind == "b" and t > 0 else bank[j % 4][:, 0:nk]
                        act.activation(prob[:, j % 4, 0:nk], src, ACT.Exp, bias=nmx[:, j:j + 1],
                                       accum_out=lsum[:, j:j + 1]).then_inc(exp_done, 1)
                if mod_at(i) is not None:
                    if i == 0:
                        act.wait_ge(roped, 8)
                    keep_mod(mod_at(i))
                if i >= 1:
                    u = i - 1
                    nk = keys(units[u][2])[1] - keys(units[u][2])[0]
                    act.wait_ge(probs_turned, u + 1)
                    if u >= 2:
                        act.wait_ge(pv_done, u - 1)
                    act.activation(pts[:, u % 2, 0:nk], bank[4 + u % 2][:, 0:nk], ACT.Copy).then_inc(pts_ready, 1)
            act.wait_ge(o_kept, NU)
            head_norm(0)
            act.wait_ge(stored, 16 * 4)
            turned_heads(0)
            for j in range(2):
                split_up(j)
            norm_out(0)

            norm_in(1)
            act.wait_ge(ht_dve, 8)
            act.wait_ge(ht_act, 8)
            for b in range(2):
                act.activation(hth[:, 4 * b:4 * b + 4, :], ht[:, 4 * b:4 * b + 4, :], ACT.Copy).then_inc(hth_ready, 1)
            for f in range(KF):
                if f % 2 == 1 and f // 2 >= 1 and f // 2 + 1 < KF // 2:
                    split_up(f // 2 + 1)
                act.wait_ge(gate_done, f + 1)
                if f >= 2:
                    act.wait_ge(prod_ready, f - 1)
                act.activation(silt[:, f % 2, :], bank[6][:, 0:T], ACT.Silu).then_inc(silu_ready, 1)
            norm_out(1)

            norm_in(2)
            act.wait_ge(sp_abs, 1)
            act.activation(sp[:, 1, :], sp[:, 0, :], ACT.Exp, scale=-1.0).then_inc(sp_exp, 1)
            act.wait_ge(zeroed, 8)
            for d in range(2):
                for g, w_ in enumerate((I["rg_wa"], I["rg_wx"])):
                    for b in range(2):
                        act.dma_start(wrg[64 * b:64 * b + 64, d, g, :, 64 * b:64 * b + 64],
                                      w_[0, d].rearrange("(n b) i o -> b i n o", b=2)[b]).then_inc(wrg_in, 16)
            act.dma_start(c0[:, :, 0:P], I["state_c_C"][0, 0].rearrange("d h k e -> k (d h) e")).then_inc(c0_in, 16)

            def odd_item(i):
                what, m, engine = items[i]
                if engine != "A":
                    return
                act.wait_ge(proj_done, i + 1)
                src = bank[i % 4]
                if what in ("xd", "q", "k"):
                    dst = xdin[:, m, :] if what == "xd" else qkin[:, m + (4 if what == "k" else 0), :]
                    act.activation(dst[:, 1:1 + P], src[:, 0:P], ACT.Copy)
                    act.activation(dst[:, SEG[1]:SEG[1] + 256], src[:, P:T], ACT.Copy).then_inc(proj_act, 1)
                elif what == "gd":
                    act.activation(gd[:, m, :], src[:, 0:T], ACT.Gelu_apprx_tanh).then_inc(proj_act, 1)
                elif what in ("rg0", "rg1"):
                    d = int(what[2])
                    if d == 1 and m == 0:
                        act.wait_ge(rg_done, 1)
                    bc = col["rg_ba" if m < 4 else "rg_bx"] + 4 * d + m % 4
                    act.activation(rgb[m // 4][:, m % 4, 1:1 + NPAD], src[:, 0:NPAD], ACT.Sigmoid,
                                   bias=cols[:, bc:bc + 1]).then_inc(proj_act, 1)
                elif what == "v":
                    if m == 0:
                        act.wait_ge(rg_free, 1)
                    act.activation(vaug[:, m, :, 0:P], src[:, :].rearrange("p (h e) -> p h e", h=4), ACT.Copy)\
                       .then_inc(proj_act, 1)
                else:
                    act.activation(sigo[:, m, :], src[:, :], ACT.Sigmoid).then_inc(proj_act, 1)

            def rg_chain(d):
                act.wait_ge(rates_ready, 2)
                wait_kept(act, index[(f"rg{d}", 7)])
                for n_ in range(4):
                    c_ = 4 * d + n_
                    act.activation(rgb[2][:, n_, 1:1 + NPAD], rgb[0][:, n_, 1:1 + NPAD], ACT.Exp,
                                   scale=sp[:, 4, c_:c_ + 1]).then_inc(rg_exps, 1)
                act.wait_ge(rg_exps, 8 * d + 4)
                for n_ in range(4):
                    c_ = 4 * d + n_
                    act.activation(rgb[0][:, n_, 1:1 + NPAD], rgb[0][:, n_, 1:1 + NPAD], ACT.Tanh,
                                   scale=sp[:, 5, c_:c_ + 1]).then_inc(rg_exps, 1)
                act.wait_ge(rg_ratio, d + 1)
                act.activation(rgb[0][:, :, 1:1 + NPAD], rgb[0][:, :, 1:1 + NPAD], ACT.Sqrt, scale=2.0)\
                   .then_inc(rg_root, 1)

            act.wait_ge(zeroed, 8)
            for i in range(len(even_items), index[("rg0", 7)] + 1):
                odd_item(i)
            rg_chain(0)
            for i in range(index[("q", 0)], index[("rg1", 7)] + 1):
                odd_item(i)
            rg_chain(1)
            for i in range(index[("k", 0)], index[("k", 3)] + 1):
                odd_item(i)
            for n_ in range(8):
                act.wait_ge(conv_ready, n_ + 1)
                act.activation(qkc[:, n_, 1:1 + NPAD], qkc[:, n_, 1:1 + NPAD], ACT.Silu).then_inc(qk_ready, 1)
            for i in range(index[("v", 0)], index[("o", 0)]):
                odd_item(i)
            act.wait_ge(row_abs, 1)
            act.activation(rwork[:, 2, :], rwork[:, 1, :], ACT.Exp, scale=-1.0).then_inc(row_exp, 1)
            for i in range(index[("o", 0)], index[("o", 2)] + 1):
                odd_item(i)
            act.wait_ge(rows_m, 1)
            act.activation(rows[:, 2, :], rwork[:, 2, :], ACT.Exp, scale=-1.0).then_inc(rows_exp, 1)
            act.activation(rows[:, 1, P:T], rwork[:, 6, P:T], ACT.Exp, bias=m0[:, :]).then_inc(rows_exp, 1)
            for d, last in ((0, P - 1), (1, 0)):
                pp = slice(32 * d, 32 * d + 4)
                act.activation(rows[pp, 3, 0:P], rows[pp, 0, 0:P], ACT.Exp, bias=rwork[pp, 6, last:last + 1])\
                   .then_inc(rows_exp, 1)
                act.dma_start(O[8][0, 0, d].rearrange("(h o) -> h o", o=1), rwork[pp, 2, last:last + 1])\
                   .then_inc(stored, 16)
            act.wait_ge(ktok_done, 1)
            act.activation(ktok[:, :, :], bank[7][:, :].rearrange("p (h e) -> p h e", h=4), ACT.Copy)\
               .then_inc(ktok_kept, 1)
            def mlstm_exp(u):
                act.wait_ge(wlog_ready, u + 1)
                act.activation(wt[:, u % 2, :], wt[:, u % 2, :], ACT.Exp).then_inc(w_ready, 1)

            mlstm_exp(0)
            for u, (h, d) in enumerate(munits):
                q, r = u % 2, 32 * d + h
                if u + 1 < 8:
                    mlstm_exp(u + 1)
                act.wait_ge(mm_done, u + 1)
                if u >= 2:
                    act.wait_ge(h_ready, u - 1)
                    act.wait_ge(c_stored[q], 16 * (u // 2))
                for t in range(1, NT):
                    act.activation(inter[:, q, 129 * (t - 1):129 * t], bank[6 + q][:, 129 * (t - 1):129 * t],
                                   ACT.Copy, scale=colr[:, WST + t - 1, r:r + 1]).then_inc(inter_kept, 1)
                act.activation(cout[:, q, :], bank[6 + q][:, 258:387], ACT.Copy).then_inc(cout_kept, 1)
                act.wait_ge(cout_kept, u + 1)
                act.dma_start(O[6][0, 0, d, h], cout[:, q, 0:P]).then_inc(c_stored[q], 16)
            act.wait_ge(h_ready, 8)
            head_norm(1)
            act.wait_ge(fin_turned, 1)
            act.activation(finrows[:, :, :], bank[7][0:8, 0:256].rearrange("p (a e) -> p a e", a=2), ACT.Copy)\
               .then_inc(fin_kept, 1)
            act.wait_ge(fin_kept, 1)
            act.dma_start(O[7][0, 0].rearrange("d h k -> (d h) k"), finrows[:, 0, :]).then_inc(stored, 16)
            act.dma_start(O[9][0, 0].rearrange("d (n k) -> (d n) k", k=P), finrows[:, 1, :]).then_inc(stored, 16)
            turned_heads(1)
            norm_out(2)

            norm_in(3)
            for j in range(6):
                act.wait_ge(tok_turned, j + 1)
                act.activation(htok[:, j // 2, 512 * (j % 2):512 * (j % 2) + 512], bank[j % 4][:, :], ACT.Copy)\
                   .then_inc(htok_ready, 1)
            act.wait_ge(e1_in, 1)
            act.activation(tk[:, 5, :], tk[:, 4, :], ACT.Exp).then_inc(e1_ready, 1)
            act.wait_ge(plan_ready, 1)
            n_work = act.value_load(ewi[0:1, MAX_ITEMS:MAX_ITEMS + 1], min_val=1, max_val=MAX_ITEMS)
            with act.Fori(0, n_work) as w:
                def split_hi(j, h):
                    if h == 0:
                        act.wait_ge(e_panel_in[j % E_RING], w * slot_item[j % E_RING] + item_need[j])
                    act.wait_ge(half_used, w * (2 * ITEM) + (USED0 + 2 * j + h - WHI + 1))
                    act.activation(whi_moe[(2 * j + h) % WHI], e_half(j, h), ACT.Copy).then_inc(whi_ready, 1)

                def act_hi(j):
                    act.wait_ge(act_turned, w * UP + (j + 1))
                    act.activation(aeh[:, 2 * j:2 * j + 2, :],
                                   bank[2 + j % 2][:, 0:256].rearrange("p (f s) -> p f s", f=2), ACT.Copy)\
                       .then_inc(aeh_ready, 1)

                split_hi(0, 0)
                split_hi(0, 1)
                for b in range(2):
                    act.wait_ge(gath_done, w * 2 + (b + 1))
                    act.activation(xgh[:, 4 * b:4 * b + 4, :],
                                   bank[6 + b][:, :].rearrange("p (k s) -> p k s", k=4), ACT.Copy)\
                       .then_inc(xgh_ready, 1)
                split_hi(1, 0)
                split_hi(1, 1)
                for j in range(UP):
                    split_hi(j + 2, 0)
                    act.wait_ge(half_used, w * (2 * ITEM) + (USED0 + 2 * j + 2))
                    if j >= 2:
                        act.wait_ge(eprod_ready, w * UP + (j - 1))
                    act.activation(sil_e[:, j % 2, :], bank[j % 2][:, 0:256], ACT.Silu).then_inc(esilu_ready, 1)
                    split_hi(j + 2, 1)
                    if j:
                        act_hi(j - 1)
                act_hi(UP - 1)
                for j in range(UP + 2, ITEM):
                    split_hi(j, 0)
                    split_hi(j, 1)
                act.wait_ge(half_used, w * (2 * ITEM) + (USED0 + 2 * ITEM))
                for b in range(2):
                    act.activation(og[:, 512 * b:512 * b + 512], bank[6 + b][:, :], ACT.Copy).then_inc(og_ready, 1)
            act.wait_ge(yacc_ready, 1)
            norm_out(3)

        @block.tensor
        def _(pe):
            def panel(key):
                i = number[key]
                pe.wait_ge(panel_in[i % RING], need[i])
                return i

            def mod_mm(m):
                if m >= 2:
                    pe.wait_ge(mod_added, m - 1 if m < 6 else m)
                i = panel(("mod", m))
                w = place(i, "k512")
                for k in range(KD):
                    q = 32 * (k % 4)
                    ins = pe.matmul(bank[mod_bank(m)][q:q + 32, :], sc[:, k, :], w[:, k, :],
                                    start=(k < 4), stop=(k >= 4), skip_group_check=True)
                ins.then_inc(mod_done, 1)

            def mod_turn(m):
                pe.wait_ge(mod_kept, m + 1)
                if m and m < 6:
                    pe.wait_ge(mod_added, m)
                for n_ in range(4):
                    ins = pe.transpose(bank[turn_bank(m)][:, P * n_:P * n_ + P], mod_row(m)[:, P * n_:P * n_ + P],
                                       ident)
                ins.then_inc(mod_turned, 1)

            def norm_in(s):
                pe.wait_ge(xn_ready, 3 * (s + 1))
                for k in range(KD):
                    if k >= 4:
                        pe.wait_ge((ht_act, ht_dve)[k % 2], 4 * s + (k - 4) // 2 + 1)
                    for t in range(NT):
                        ins = pe.transpose(bank[k % 4][:, P * t:P * t + P], xn[:, t, P * k:P * k + P], ident)
                    ins.then_inc(xn_turned, 1)
                if s < 3:
                    gate_rows(s)
                pe.wait_ge(ht_act, 4 * (s + 1))
                pe.wait_ge(ht_dve, 4 * (s + 1))
                if s == 0:
                    pe.wait_ge(gb_kept, 2)

            def gate_rows(s):
                pe.wait_ge(gains_ready, s + 1)
                for c_ in range(CONDS):
                    if c_:
                        pe.wait_ge(gb_kept, 2 * s + 1)
                    for k in range(KD):
                        ins = pe.matmul(bank[4 + k // 4][:, P * (k % 4):P * (k % 4) + P],
                                        gcol[:, s, k, c_:c_ + 1].to_broadcast([P, P]), ident,
                                        start=True, stop=True)
                    ins.then_inc(gb_made, 1)

            def project(i, w, n0=None, t=None):
                if (i if i < len(even_items) else i - len(even_items)) >= 4:
                    wait_kept(pe, i - 4)
                for k in range(KD):
                    if t is None:
                        ins = pe.matmul(bank[i % 4][:, 0:T], w[:, k, n0:n0 + P], ht[:, k, :],
                                        start=(k == 0), stop=(k == KD - 1))
                    else:
                        ins = pe.matmul(bank[i % 4][:, :], ht[:, k, P * t:P * t + P], w[:, k, :],
                                        start=(k == 0), stop=(k == KD - 1))
                return ins

            def project_panel(key, what, by_token):
                i = panel(key)
                w = place(i, "k512")
                for m in range(3 if by_token else 4):
                    j = index[(what, m)]
                    ins = project(j, w, t=m) if by_token else project(j, w, n0=P * m)
                    ins.then_inc(proj_done, 1)

            def turn_heads(m):
                for k in range(8 if m == 0 else 4):
                    if k >= 4:
                        if k % 2 == 0:
                            pe.wait_ge(ot_act, k // 2 - 1)
                        else:
                            pe.wait_ge(ot_dve, k // 2 - 1)
                    for t in range(NT):
                        ins = pe.transpose(bank[k % 4][:, P * t:P * t + P], heads[:, t, P * k:P * k + P], ident)
                    ins.then_inc(o_turned, 1)
                pe.wait_ge(ot_act, 4 if m == 0 else 6)
                pe.wait_ge(ot_dve, 4 if m == 0 else 6)

            def out_proj(m):
                for j in range(2):
                    i = panel((f"out{m}", j))
                    w = place(i, "k512")
                    for t in range(NT):
                        for k in range(KD):
                            lhs = gd[:, k - 4, P * t:P * t + P] if m == 1 and k >= 4 else ht[:, k, P * t:P * t + P]
                            ins = pe.matmul(bank[2 * t + j][:, :], lhs, w[:, k, :], start=(k == 0), stop=(k == KD - 1))
                        ins.then_inc(out_done, 1)

            pe.wait_ge(cst_in, 16)
            pe.wait_ge(rows_in, 16 * len(row_dmas))
            for t_ in range(3):
                m_ = P if t_ < 2 else last_rows
                ins = pe.transpose(bank[6][:, P * t_:P * t_ + m_], rowt[0:m_, t_, :], ident[0:m_, 0:m_])
            ins.then_inc(rows_turned, 1)
            pe.wait_ge(sc_ready, 2)
            mod_mm(0)
            for m in range(6):
                if m < 5:
                    mod_mm(m + 1)
                mod_turn(m)
            norm_in(0)
            for a in range(2):
                pe.wait_ge(even_in, 64)
                if a:
                    pe.wait_ge(aux_kept, a)
                for h in range(4):
                    ins = pe.transpose(bank[6][:, P * h:P * h + P], kcache[:, a, P * h:P * h + P], ident)
                ins.then_inc(aux_done, 1)
            project_panel(("in0", 0), "qa", False)
            project_panel(("in0", 1), "ka", False)
            project_panel(("in0", 2), "va", True)
            pe.wait_ge(cst_rest_in, 16)
            for j in range(8):
                src = qat if j < 4 else kat
                if j == 0:
                    wait_kept(pe, index[("ka", 3)])
                    wait_kept(pe, index[("qa", 3)])
                if j >= 2:
                    pe.wait_ge(roped, j - 1)
                pe.matmul(bank[4 + j % 2][:, 0:256], cst[:, C_ROT:C_ROT + P], src[:, j % 4, P:3 * P],
                          start=True, stop=True).then_inc(rot_done, 1)
            project_panel(("in0", 3), "qb", False)
            project_panel(("in0", 4), "kb", False)
            project_panel(("in0", 5), "vb", True)
            for a in range(2):
                pe.wait_ge(aux_kept, a + 2)
                wait_kept(pe, index[("kb", 3)])
                for h in range(4):
                    ins = pe.transpose(bank[6][:, P * h:P * h + P], (kat, kbt)[a][:, h, 0:P], ident)
                ins.then_inc(aux_done, 1)
            wait_kept(pe, index[("vb", 2)])
            wait_kept(pe, index[("vb", 1)])
            pe.wait_ge(roped, 8)
            pe.wait_ge(aux_kept, 4)
            for i in range(NU + 2):
                if i < NU:
                    kind, h, t, _ = units[i]
                    k0, k1 = keys(t)
                    for j in slots(i):
                        if j >= 4:
                            pe.wait_ge(exp_done, j - 3)
                        if kind == "a":
                            pp = slice(64 * (j % 2), 64 * (j % 2) + 64)
                            q_, k_ = qat[pp, h, P * t:P * t + P], kat[pp, h, k0:k1]
                        else:
                            pp = slice(64 * (h % 2), 64 * (h % 2) + 64)
                            q_, k_ = qbt[pp, h // 2, P * t:P * t + P], kbt[pp, h // 2, k0:k1]
                        pe.matmul(bank[j % 4][:, 0:k1 - k0], q_, k_, start=True, stop=True).then_inc(scores_done, 1)
                m = mod_at(i)
                if m is not None:
                    mod_mm(m)
                if turn_at(i) is not None:
                    mod_turn(turn_at(i))
                if 1 <= i <= NU:
                    u = i - 1
                    k0, k1 = keys(units[u][2])
                    j = slots(u)[0]
                    if units[u][0] == "a":
                        pe.wait_ge(probs_ready, u + 1)
                    else:
                        pe.wait_ge(exp_done, j + 1)
                    if u >= 2:
                        pe.wait_ge(pts_ready, u - 1)
                    for b in range((k1 - k0) // P):
                        ins = pe.transpose(bank[4 + u % 2][:, P * b:P * b + P], prob[:, j % 4, P * b:P * b + P], ident)
                    ins.then_inc(probs_turned, 1)
                if i >= 2:
                    u = i - 2
                    kind, h, t, _ = units[u]
                    k0, k1 = keys(t)
                    nb_ = (k1 - k0) // P
                    e = P if kind == "a" else HD
                    pe.wait_ge(pts_ready, u + 1)
                    if u:
                        pe.wait_ge(o_kept, u)
                    for b in range(nb_):
                        v_ = (va if kind == "a" else vb)[:, k0 // P + b, e * h:e * h + e]
                        ins = pe.matmul(bank[6][:, 0:e], pts[:, u % 2, P * b:P * b + P], v_,
                                        start=(b == 0), stop=(b == nb_ - 1))
                    ins.then_inc(pv_done, 1)
            pe.wait_ge(heads_ready, 1)
            turn_heads(0)
            out_proj(0)

            norm_in(1)
            for f in range(KF):
                if f % 2 == 0:
                    i = panel(("up", f // 2))
                for g in range(2):
                    if f:
                        pe.wait_ge((silu_ready, prod_ready)[g], f)
                    for k in range(KD):
                        if k % 4 == 0:
                            wh, wl = parts_of(i, k // 4, whi_dense, 4)
                            pe.wait_ge(wlo_ready, 2 * (f // 2) + k // 4 + 1)
                            pe.wait_ge(htl_ready, k // 4 + 1)
                        c_ = slice(256 * g + P * (f % 2), 256 * g + P * (f % 2) + P)
                        for lhs, rhs in ((wh, hth), (wh, htl), (wl, hth)):
                            ins = pe.matmul(bank[6 + g][:, 0:T], lhs[:, k % 4, c_], rhs[:, k, :],
                                            start=(k == 0 and lhs is wh and rhs is hth),
                                            stop=(k == KD - 1 and lhs is wl))
                    ins.then_inc((gate_done, up_done)[g], 1)
            pe.wait_ge(gb_kept, 4)
            pe.wait_ge(prod_ready, KF)
            for f in range(KF):
                if f % 4 == 0:
                    i = panel(("down", f // 4))
                w = place(i, "rows")
                for t in range(NT):
                    for n_ in range(2):
                        ins = pe.matmul(bank[2 * t + n_][:, :], actt[:, f, P * t:P * t + P],
                                        w[:, f % 4, 512 * n_:512 * n_ + 512], start=(f == 0), stop=(f == KF - 1))
                if f == KF - 1 or f % 4 == 3:
                    ins.then_inc(down_done, 1)

            norm_in(2)
            project_panel(("in1", 0), "xd", False)
            project_panel(("in1", 1), "gd", False)

            def rg_mm(d):
                if d == 0:
                    pe.wait_ge(xc_ready, 4)
                    pe.wait_ge(wrg_in, 16 * 8)
                for m in range(8):
                    i = index[(f"rg{d}", m)]
                    wait_kept(pe, i - 4)
                    pe.matmul(bank[i % 4][:, 0:NPAD], wrg[:, d, m // 4, m % 4, :], xc[:, m % 4, 1:1 + NPAD],
                              start=True, stop=True).then_inc(proj_done, 1)

            rg_mm(0)
            project_panel(("in1", 2), "q", False)
            rg_mm(1)
            project_panel(("in1", 3), "k", False)
            pe.wait_ge(gb_kept, 6)
            pe.wait_ge(wgp_ready, 1)
            for g in range(2):
                for k in range(KD):
                    ins = pe.matmul(bank[4 + g][0:36, 0:T], wgp[:, k, g, :], ht[:, k, :],
                                    start=(k == 0), stop=(k == KD - 1))
            ins.then_inc(gates_done, 1)
            project_panel(("in1", 4), "v", True)
            project_panel(("in1", 5), "o", True)
            pe.wait_ge(qk_ready, 8)
            for h in range(4):
                ins = pe.transpose(bank[7][:, P * h:P * h + P], qkc[:, 4 + h, SEG[0]:SEG[0] + P], ident)
            ins.then_inc(ktok_done, 1)
            pe.wait_ge(rows_m, 1)
            pe.wait_ge(rows_exp, 4)
            turns = ([(0, t) for t in range(3)] + [(1, 1), (1, 2)] + [(2, t) for t in range(3)] + [(3, 0)])
            for j, (kind, t) in enumerate(turns):
                ins = pe.transpose(bank[6][:, 36 * j:36 * j + 36], rows[:, kind, P * t:P * t + P], ident[0:36, 0:36])
            ins.then_inc(rows_turned2, 1)
            pe.wait_ge(colr_ready, 1)
            pe.wait_ge(ktok_kept, 1)
            pe.wait_ge(c0_in, 16)
            wait_kept(pe, index[("o", 2)])
            wait_kept(pe, index[("o", 1)])
            pe.wait_ge(zeroed, 10)

            def mlstm_logs(u):
                h, d = munits[u]
                if d == 0:
                    if u:
                        pe.wait_ge(sw_ready, u)
                    for s_, dst in ((0, bank[0][:, 0:P]), (1, bank[0][:, P:T]), (2, bank[1][:, 0:256])):
                        q_ = qkc[:, h, SEG[0]:SEG[0] + P] if s_ == 0 else qkc[:, h, SEG[1]:SEG[1] + 256]
                        ins = pe.matmul(dst, qkc[:, 4 + h, SEG[s_]:SEG[s_] + P], q_, start=True, stop=True)
                    ins.then_inc(st_done, 1)
                if u >= 2:
                    pe.wait_ge(wlog_ready, u - 1)
                sel_ = C_SEL + (4 * d + h) * P
                pe.matmul(bank[2 + u % 2][:, 0:T], cst[0:36, sel_:sel_ + P], rwork[:, 6, :], start=True, stop=True)\
                  .then_inc(nm_done, 1)

            mlstm_logs(0)
            for u, (h, d) in enumerate(munits):
                q = u % 2
                pe.wait_ge(sw_ready, u + 1)
                if u + 1 < 8:
                    mlstm_logs(u + 1)
                pe.wait_ge(kws_ready, u + 1)
                if u >= 2:
                    pe.wait_ge(h_ready, u - 1)
                    pe.wait_ge(inter_kept, 2 * (u - 1))
                    pe.wait_ge(cout_kept, u - 1)
                for t in range(NT):
                    bl = [b for b in blocks[d] if b[1] == t]
                    for b, (s_, _, o_) in enumerate(bl):
                        pe.matmul(bank[4 + q][:, 129 * t:129 * t + 129], sw[:, q, o_:o_ + P], vaug[:, s_, h, :],
                                  start=(b == 0), stop=(b == len(bl) - 1))
                for t in range(1, NT):
                    pe.matmul(bank[6 + q][:, 129 * (t - 1):129 * t], qkc[:, h, SEG[t]:SEG[t] + P],
                              c0[:, 4 * d + h, :], start=True, stop=True)
                pe.matmul(bank[6 + q][:, 258:387], kws[:, q, :], vaug[:, 0, h, :], start=True, stop=True)\
                  .then_inc(mm_done, 1)
            pe.wait_ge(fin_ready, 8)
            pe.wait_ge(rg_free, 1)
            pe.wait_ge(cout_kept, 8)
            for a in range(2):
                ins = pe.transpose(bank[7][0:8, P * a:P * a + P], fincols[:, 8 * a:8 * a + 8], ident)
            ins.then_inc(fin_turned, 1)
            pe.wait_ge(heads_ready, 2)
            turn_heads(1)
            pe.wait_ge(rg_free, 1)
            out_proj(1)

            norm_in(3)
            pe.wait_ge(router_in, 32)
            for t in range(NT):
                for k in range(KD):
                    ins = pe.matmul(bank[6][:, 8 * t:8 * t + 8], ht[:, k, P * t:P * t + P], rw[:, k, :],
                                    start=(k == 0), stop=(k == KD - 1))
            ins.then_inc(logits_done, 1)
            gate_rows(3)
            for j in range(6):
                if j >= 4:
                    pe.wait_ge(htok_ready, j - 3)
                for k in range(4):
                    ins = pe.transpose(bank[j % 4][:, P * k:P * k + P],
                                       ht[:, 4 * (j % 2) + k, P * (j // 2):P * (j // 2) + P], ident)
                ins.then_inc(tok_turned, 1)
            pe.wait_ge(sel_ready, 1)
            for t in range(NT):
                for t2 in range(t + 1):
                    m_ = cst[:, C_CUM:C_CUM + P] if t2 == t else ones
                    ins = pe.matmul(bank[7][:, 8 * t:8 * t + 8], m_, oh[:, 2, t2, :], start=(t2 == 0), stop=(t2 == t))
            ins.then_inc(half_used, USED0)
            for t in range(NT):
                ins = pe.matmul(bank[7][:, 24:32], ones, oh[:, 2, t, :], start=(t == 0), stop=(t == NT - 1))
            ins.then_inc(pos_done, 1)
            pe.wait_ge(htok_ready, 6)
            pe.wait_ge(gb_kept, 8)
            pe.wait_ge(plan_ready, 1)
            n_work = pe.value_load(ewi[0:1, MAX_ITEMS:MAX_ITEMS + 1], min_val=1, max_val=MAX_ITEMS)
            with pe.Fori(0, n_work) as w:
                pe.wait_ge(hot_ready, w + 1)
                for b in range(2):
                    for k in range(4):
                        for t in range(NT):
                            ins = pe.matmul(bank[6 + b][:, P * k:P * k + P],
                                            htok[:, t, 512 * b + P * k:512 * b + P * k + P], onehot[:, t, :],
                                            start=(t == 0), stop=(t == NT - 1))
                    ins.then_inc(gath_done, 1)
                pe.wait_ge(yadd, w * 6 + 1)
                for t in range(NT):
                    ins = pe.transpose(bank[4][:, P * t:P * t + P], gated[:, t, :], ident)
                ins.then_inc(gated_turned, 1)

                def turn_act(j):
                    pe.wait_ge(eprod_ready, w * UP + (j + 1))
                    if j >= 2:
                        pe.wait_ge(ael_ready, w * UP + (j - 1))
                    for f in range(2):
                        ins = pe.transpose(bank[2 + j % 2][:, P * f:P * f + P], a_tok[:, j % 2, P * f:P * f + P], ident)
                    ins.then_inc(act_turned, 1)

                for j in range(UP):
                    if j >= 2:
                        pe.wait_ge(eprod_ready, w * UP + (j - 1))
                    for h in range(2):
                        if j == 0:
                            pe.wait_ge(xgl_ready, w * 2 + (h + 1))
                        pe.wait_ge(wlo_ready, w * (2 * ITEM) + (KF + 2 * j + h + 1))
                        wh, wl = e_parts(j, h, 4)
                        for k in range(4):
                            for n_, (lhs, rhs) in enumerate(((xgh, wh), (xgh, wl), (xgl, wh))):
                                ins = pe.matmul(bank[j % 2][:, :], lhs[:, 4 * h + k, :], rhs[:, k, :],
                                                start=(h == 0 and k == 0 and n_ == 0),
                                                stop=(h == 1 and k == 3 and n_ == 2))
                        ins.then_inc(half_used, 1)
                    if j:
                        turn_act(j - 1)
                for jd in range(DOWN):
                    if jd == 1:
                        turn_act(UP - 1)
                    j = UP + jd
                    for h in range(2):
                        pe.wait_ge(ael_ready, w * UP + (2 * jd + h + 1))
                        pe.wait_ge(wlo_ready, w * (2 * ITEM) + (KF + 2 * j + h + 1))
                        wh, wl = e_parts(j, h, 2)
                        for k in range(2):
                            for n_, (lhs, rhs) in enumerate(((aeh, wh), (aeh, wl), (ael, wh))):
                                for b in range(2):
                                    ins = pe.matmul(bank[6 + b][:, :], lhs[:, 4 * jd + 2 * h + k, :],
                                                    rhs[:, k, 512 * b:512 * b + 512],
                                                    start=(jd == 0 and h == 0 and k == 0 and n_ == 0),
                                                    stop=(jd == DOWN - 1 and h == 1 and k == 1 and n_ == 2))
                        ins.then_inc(half_used, 1)
                pe.wait_ge(scat_ready, w + 1)
                pe.wait_ge(og_ready, w * 2 + 2)
                for j, (t, b) in enumerate(SCATTER):
                    pe.matmul(bank[SCAT_BANK[j]][:, :], scat[:, t, :], og[:, 512 * b:512 * b + 512],
                              start=True, stop=True).then_inc(scat_done, 1)

        @block.vector
        def _(dve):
            n = [0]

            def then(ins):
                n[0] += 1
                ins.then_inc(dve_step, 1)
                dve.wait_ge(dve_step, n[0])

            def add_mod(m):
                dve.wait_ge(mod_turned, m + 1)
                l, j = m // 12, m % 12
                b = cols[:, col["mod_b"] + 48 * l + 4 * j:col["mod_b"] + 48 * l + 4 * j + 4]
                v = modc[:, l, 4 * j:4 * j + 4, :]
                turned = bank[turn_bank(m)][:, :].rearrange("p (n q r) -> p n r q", n=4, q=4)
                then(dve.tensor_reduce(v, turned[:, :, 0:2, :], AX.X, ALU.add))
                dve.tensor_tensor(v, v, b.unsqueeze(2).to_broadcast([P, 4, 2]), ALU.add).then_inc(mod_added, 1)
                if m % 6 == 5:
                    gains(m // 6)

            def gains(s):
                l, h = s // 2, 24 * (s % 2)
                dve.wait_ge(mod_added, 6 * (s + 1))

                def g(r):
                    o = col["norm_g"] + 32 * l + 8 * (2 * (s % 2) + r)
                    return cols[:, o:o + 8].unsqueeze(2).to_broadcast([P, 8, 2])

                then(dve.scalar_tensor_tensor(out=acol[:, s, :, :], in0=modc[:, l, h + 8:h + 16, :], scalar=1.0,
                                              in1=g(0), op0=ALU.add, op1=ALU.mult))
                dve.tensor_tensor(gcol[:, s, :, :], modc[:, l, h + 16:h + 24, :], g(1), ALU.mult)\
                   .then_inc(gains_ready, 1)

            def split_up(j):
                i = number[("up", j)]
                for h in range(2):
                    dve.wait_ge(whi_ready, 2 * j + h + 1)
                    dve.tensor_tensor(low_half(i, h), panel_half(i, h), whi_dense[(2 * i + h) % WHI],
                                      ALU.subtract).then_inc(wlo_ready, 1)

            def norm_in(s):
                dve.wait_ge(roots_ready, s + 1)
                then(dve.reciprocal(rs[:, s, :], sd[:, s, :]))
                for t in range(NT):
                    dve.tensor_scalar(xn[:, t, :], x[:, t, :], rs[:, s, t:t + 1], None, ALU.mult)\
                       .then_inc(xn_ready, 1)
                for k in range(1, KD, 2):
                    dve.wait_ge(xn_turned, 8 * s + k + 1)
                    for c_, (lo, hi) in enumerate(((0, P), (P, T))):
                        ins = dve.tensor_scalar(ht[:, k, lo:hi], bank[k % 4][:, lo:hi], acol[:, s, k, c_:c_ + 1],
                                                modc[:, s // 2, 24 * (s % 2) + k, c_:c_ + 1], ALU.mult, ALU.add)
                    ins.then_inc(ht_dve, 1)

            def norm_out(s):
                dve.wait_ge(sq2_ready, s + 1)
                v = ss2[:, s, :].rearrange("p (t n) -> p n t", n=2)
                dve.tensor_tensor(ssum[:, s, :], v[:, 0, :], v[:, 1, :], ALU.add).then_inc(sum2_ready, 1)
                dve.wait_ge(root2_ready, s + 1)
                then(dve.reciprocal(rs2[:, s, :], sd2[:, s, :]))
                for t in range(NT):
                    if t:
                        dve.wait_ge(x_ready, 3 * s + t)
                    for n_ in range(2):
                        h = slice(512 * n_, 512 * n_ + 512)
                        src = yacc[:, t, h] if s == 3 else bank[2 * t + n_][:, :]
                        ins = dve.scalar_tensor_tensor(out=jk[:, n_, :], in0=src, scalar=rs2[:, s, t:t + 1],
                                                       in1=gb[:, min(t, 1), h], op0=ALU.mult, op1=ALU.mult)
                    then(ins)
                    for n_ in range(2):
                        h = slice(512 * n_, 512 * n_ + 512)
                        ins = dve.tensor_tensor(x[:, t, h], x[:, t, h], jk[:, n_, :], ALU.add)
                    ins.then_inc(x_ready, 1)

            def head_norm(m, sq, gate):
                dve.wait_ge(hsq_ready, m + 1)
                dve.tensor_reduce(hn[:, m, 0, :], sq.rearrange("p (u e) -> p u e", e=P), AX.X, ALU.add)\
                   .then_inc(hsum_ready, 1)
                dve.wait_ge(hroot_ready, m + 1)
                then(dve.reciprocal(hn[:, m, 2, :], hn[:, m, 1, :]))
                for t in range(NT):
                    for h in range(4):
                        v = heads[:, t, P * h:P * h + P]
                        ins = dve.scalar_tensor_tensor(out=v, in0=v, scalar=hn[:, m, 2, 4 * t + h:4 * t + h + 1],
                                                       in1=subg[:, m, :], op0=ALU.mult, op1=ALU.mult)
                if gate is not None:
                    then(ins)
                    for t in range(NT):
                        ins = dve.tensor_tensor(heads[:, t, 0:512], heads[:, t, 0:512], gate[:, t, :], ALU.mult)
                ins.then_inc(heads_ready, 1)

            def turned_heads(m):
                for k in range(1, 8 if m == 0 else 4, 2):
                    dve.wait_ge(o_turned, (0 if m == 0 else 8) + k + 1)
                    dve.tensor_copy(ht[:, k, :], bank[k % 4][:, 0:T]).then_inc(ot_dve, 1)

            dve.memset(sc[:, :, :], 0.0).then_inc(sc_clear, 1)
            dve.wait_ge(rows_turned, 1)
            dve.tensor_copy(cols[:, 0:n_rows], bank[6][:, 0:n_rows]).then_inc(cols_ready, 1)
            dve.wait_ge(cols_ready, 1)
            for m in range(6):
                add_mod(m)
            norm_in(0)

            dve.wait_ge(small_in, 48)
            dve.tensor_tensor_reduce(prob[:, 0, 0:64], alam[:, 0:64], alam[:, 64:128], 1.0, 0.0, ALU.mult, ALU.add,
                                     lamc[:, 0:1])
            dve.tensor_tensor_reduce(prob[:, 0, 64:128], alam[:, 128:192], alam[:, 192:256], 1.0, 0.0, ALU.mult,
                                     ALU.add, lamc[:, 1:2]).then_inc(lam_sums, 1)
            then(dve.tensor_scalar(subg[:, 0, :], subg[:, 0, :], 1.0 - LAM_INIT, None, ALU.mult))
            dve.wait_ge(lam_exps, 1)
            then(dve.tensor_tensor(lamc[:, 4:5], lamc[:, 3:4], lamc[:, 2:3], ALU.subtract))
            then(dve.tensor_scalar(lamc[:, 5:6], lamc[:, 4:5], -LAM_INIT, None, ALU.add))

            def even_item(i):
                what, t, _ = items[i]
                dve.wait_ge(proj_done, i + 1)
                dve.tensor_copy((kat if what == "ka" else kbt)[:, t, 0:T], bank[i % 4][:, 0:T]).then_inc(proj_dve, 1)

            for t in range(4):
                even_item(index[("ka", t)])
            dve.wait_ge(aux_done, 1)
            dve.wait_ge(cst_rest_in, 16)
            for j in range(8):
                dst = (qat if j < 4 else kat)[:, j % 4, P:3 * P]
                dve.wait_ge(rot_done, j + 1)
                if j >= 2:
                    dve.wait_ge(roped, j - 1)
                then(dve.tensor_tensor(ropes[j % 2], bank[4 + j % 2][:, 0:256], cst[:, C_SIN:C_SIN + 256], ALU.mult))
                dve.wait_ge(cos_part, j + 1)
                dve.tensor_tensor(dst, ropec[j % 2], ropes[j % 2], ALU.add).then_inc(roped, 1)
            for t in range(4):
                even_item(index[("kb", t)])

            for i in range(NU + 2):
                if i < NU:
                    kind, h, t, _ = units[i]
                    nk = keys(t)[1] - keys(t)[0]
                    for j in slots(i):
                        dve.wait_ge(scores_done, j + 1)
                        if kind == "b" and t > 0:
                            if h == 0 and t == 1:
                                dve.wait_ge(masked, 1)
                            dve.wait_ge(probs_turned, i - 1)
                            then(dve.tensor_tensor_reduce(prob[:, j % 4, 0:nk], bank[j % 4][:, 0:nk],
                                                          bias[:, t - 1, h, :], 1.0, -3.0e38, ALU.add, ALU.max,
                                                          rl[:, j:j + 1]))
                            dve.tensor_scalar(nmx[:, j:j + 1], rl[:, j:j + 1], -1.0, None, ALU.mult)\
                               .then_inc(max_ready, 1)
                        else:
                            dve.tensor_reduce(nmx[:, j:j + 1], bank[j % 4][:, 0:nk], AX.X, ALU.max, negate=True)\
                               .then_inc(max_ready, 1)
                if turn_at(i) is not None:
                    add_mod(turn_at(i))
                if 1 <= i <= NU:
                    u = i - 1
                    j = slots(u)[0]
                    nk = keys(units[u][2])[1] - keys(units[u][2])[0]
                    dve.wait_ge(exp_done, slots(u)[-1] + 1)
                    if units[u][0] == "a":
                        then(dve.reciprocal(rl[:, j:j + 2], lsum[:, j:j + 2]))
                        then(dve.tensor_scalar(rl[:, j + 1:j + 2], rl[:, j + 1:j + 2], lamc[:, 5:6], None, ALU.mult))
                        then(dve.tensor_scalar(prob[:, (j + 1) % 4, 0:nk], prob[:, (j + 1) % 4, 0:nk],
                                               rl[:, j + 1:j + 2], None, ALU.mult))
                        dve.scalar_tensor_tensor(out=prob[:, j % 4, 0:nk], in0=prob[:, j % 4, 0:nk],
                                                 scalar=rl[:, j:j + 1], in1=prob[:, (j + 1) % 4, 0:nk],
                                                 op0=ALU.mult, op1=ALU.add).then_inc(probs_ready, 1)
                    else:
                        then(dve.reciprocal(rl[:, j:j + 1], lsum[:, j:j + 1]))
                if i >= 2:
                    u = i - 2
                    kind, h, t, j = units[u]
                    dve.wait_ge(pv_done, u + 1)
                    if kind == "a":
                        dve.tensor_copy(heads[:, t, P * h:P * h + P], bank[6][:, 0:P])\
                           .then_inc(o_kept, 1)
                    else:
                        dve.tensor_scalar(heads[:, t, 512 + HD * h:512 + HD * h + HD],
                                          bank[6][:, 0:HD], rl[:, j:j + 1], None, ALU.mult)\
                           .then_inc(o_kept, 1)
            head_norm(0, sq_even, None)
            dve.wait_ge(stored, 16 * 4)
            turned_heads(0)
            for j in range(2):
                split_up(j)
            norm_out(0)

            norm_in(1)
            for b in range(2):
                dve.wait_ge(hth_ready, b + 1)
                v = slice(4 * b, 4 * b + 4)
                dve.tensor_tensor(htl[:, v, :], ht[:, v, :], hth[:, v, :], ALU.subtract).then_inc(htl_ready, 1)
            for f in range(KF):
                if f % 2 == 1 and f // 2 >= 1 and f // 2 + 1 < KF // 2:
                    split_up(f // 2 + 1)
                dve.wait_ge(up_done, f + 1)
                dve.wait_ge(silu_ready, f + 1)
                dve.tensor_tensor(actt[:, f, :], silt[:, f % 2, :], bank[7][:, 0:T], ALU.mult).then_inc(prod_ready, 1)
            norm_out(1)

            def log1p_of(e, z, z2, acc, out):
                then(dve.tensor_scalar(z, e, 2.0, None, ALU.add))
                then(dve.reciprocal(z, z))
                then(dve.tensor_tensor(z, z, e, ALU.mult))
                then(dve.tensor_tensor(z2, z, z, ALU.mult))
                then(dve.tensor_scalar(acc, z2, 1.0 / 15, None, ALU.mult))
                for c_ in (13, 11, 9, 7, 5, 3):
                    then(dve.scalar_tensor_tensor(out=acc, in0=acc, scalar=1.0 / c_, in1=z2, op0=ALU.add, op1=ALU.mult))
                then(dve.scalar_tensor_tensor(out=acc, in0=acc, scalar=1.0, in1=z, op0=ALU.add, op1=ALU.mult))
                then(dve.tensor_scalar(out, acc, 2.0, None, ALU.mult))

            norm_in(2)
            lam_ = cols[:, col["rg_lam"]:col["rg_lam"] + 8]
            dve.scalar_tensor_tensor(out=sp[:, 0, :], in0=lam_, scalar=-1.0, in1=lam_, op0=ALU.mult, op1=ALU.max)\
               .then_inc(sp_abs, 1)
            dve.wait_ge(sp_exp, 1)
            log1p_of(sp[:, 1, :], sp[:, 2, :], sp[:, 3, :], sp[:, 4, :], sp[:, 0, :])
            then(dve.tensor_scalar(sp[:, 2, :], lam_, -1.0, 0.0, ALU.mult, ALU.max))
            then(dve.tensor_tensor(sp[:, 3, :], sp[:, 0, :], sp[:, 2, :], ALU.add))
            dve.tensor_scalar(sp[:, 4, :], sp[:, 3, :], -8.0, None, ALU.mult).then_inc(rates_ready, 1)
            dve.tensor_scalar(sp[:, 5, :], sp[:, 3, :], 8.0, None, ALU.mult).then_inc(rates_ready, 1)
            dve.wait_ge(odd_in, 16 * 7)
            dve.wait_ge(zeroed, 5)
            for d in range(2):
                for g in range(2):
                    o = 8 * d + 4 * g
                    dve.tensor_copy(wgp[:, :, g, 32 * d:32 * d + 4], wg[:, :, o:o + 4]).then_inc(wgp_ready, 1)
            dve.tensor_copy(c0[:, :, P:P + 1], cols[:, col["state_c_n"]:col["state_c_n"] + 8].unsqueeze(2))\
               .then_inc(wgp_ready, 1)
            dve.wait_ge(zeroed, 8)

            def odd_item(i):
                what, m, engine = items[i]
                if engine != "D":
                    return
                dve.wait_ge(proj_done, i + 1)
                dst = xdin[:, m, :] if what == "xd" else qkin[:, m + (4 if what == "k" else 0), :]
                dve.tensor_copy(dst[:, 1:1 + P], bank[i % 4][:, 0:P])
                dve.tensor_copy(dst[:, SEG[1]:SEG[1] + 256], bank[i % 4][:, P:T]).then_inc(proj_dve, 1)

            def conv(dst, src, w0, step, b):
                def tap(j):
                    return cols[:, w0 + step * j:w0 + step * j + 1]
                then(dve.tensor_scalar(dst[:, 1:1 + NPAD], src[:, 0:NPAD], tap(0), b, ALU.mult, ALU.add))
                for j in range(1, 4):
                    ins = dve.scalar_tensor_tensor(out=dst[:, 1:1 + NPAD - (j > 2)], in0=src[:, j:j + NPAD - (j > 2)],
                                                   scalar=tap(j), in1=dst[:, 1:1 + NPAD - (j > 2)],
                                                   op0=ALU.mult, op1=ALU.add)
                    if j < 3:
                        then(ins)
                return ins

            for m in range(4):
                odd_item(index[("xd", m)])
            for m in range(4):
                wait_kept(dve, index[("xd", m)])
                conv(xc[:, m, :], xdin[:, m, :], col["conv_d"] + m, 4,
                     cols[:, col["conv_d_b"] + m:col["conv_d_b"] + m + 1]).then_inc(xc_ready, 1)

            def rg_chain(d):
                a_, u_, tmp = rgb[2][:, :, 1:1 + NPAD], rgb[1][:, :, 1:1 + NPAD], rgb[3][:, :, 1:1 + NPAD]
                th = rgb[0][:, :, 1:1 + NPAD]
                dve.wait_ge(xc_ready, 4)
                wait_kept(dve, index[(f"rg{d}", 7)])
                then(dve.tensor_tensor(u_, u_, xc[:, :, 1:1 + NPAD], ALU.mult))
                dve.wait_ge(rg_exps, 8 * (d + 1))
                then(dve.tensor_scalar(tmp, th, 1.0, None, ALU.add))
                then(dve.reciprocal(tmp, tmp))
                dve.tensor_tensor(th, th, tmp, ALU.mult).then_inc(rg_ratio, 1)
                dve.wait_ge(rg_root, d + 1)
                then(dve.tensor_tensor(u_, u_, th, ALU.mult))
                out = hfw if d == 0 else rgb[3]
                for m in range(4):
                    for c_, w in ((SEG[0], P), (SEG[1], 256)):
                        init = cols[:, col["state_d_h"] + 4 * d + m:col["state_d_h"] + 4 * d + m + 1] if w == 256 else 0.0
                        fwd = slice(c_, c_ + w)
                        sl = fwd if d == 0 else slice(c_ + w - 1, c_ - 1, -1)
                        ins = dve.tensor_tensor_scan(out[:, m, sl], rgb[2][:, m, sl], rgb[1][:, m, sl], init,
                                                     ALU.mult, ALU.add)
                then(ins)
                last = SEG[0] + P - 1 if d == 0 else SEG[0]
                ins = dve.tensor_copy(fincols[:, 8 + 4 * d:12 + 4 * d].unsqueeze(2), out[:, :, last:last + 1])
                if d == 0:
                    ins.then_inc(rg_done, 1)
                    return
                then(ins)
                for c_, w, o in ((SEG[0], P, 0), (SEG[1], 256, P)):
                    then(dve.tensor_tensor(rgb[0][:, :, c_:c_ + w], hfw[:, :, c_:c_ + w], rgb[3][:, :, c_:c_ + w],
                                           ALU.add))
                    ins = dve.tensor_tensor(gd[:, :, o:o + w], gd[:, :, o:o + w], rgb[0][:, :, c_:c_ + w], ALU.mult)
                    if o == 0:
                        then(ins)
                ins.then_inc(rg_free, 1)

            wait_kept(dve, index[("gd", 3)])
            rg_chain(0)
            for m in range(4):
                odd_item(index[("q", m)])
            rg_chain(1)
            for m in range(4):
                odd_item(index[("k", m)])
            for m in range(8):
                i = index[("q" if m < 4 else "k", m % 4)]
                wait_kept(dve, i)
                conv(qkc[:, m, :], qkin[:, m, :], col["conv_c"] + m, 8, 0.0).then_inc(conv_ready, 1)

            dve.wait_ge(zeroed, 10)
            dve.wait_ge(gates_done, 1)
            ig, ff, t2, t3, lf, b_, nm = (rwork[:, k, :] for k in range(7))
            then(dve.tensor_scalar(ig, bank[4][0:36, 0:T], gbias[:, 0:1], None, ALU.add))
            then(dve.tensor_scalar(t3, bank[5][0:36, 0:T], gbias[:, 1:2], None, ALU.add))
            dve.scalar_tensor_tensor(out=ff, in0=t3, scalar=-1.0, in1=t3, op0=ALU.mult, op1=ALU.max)\
               .then_inc(row_abs, 1)
            dve.wait_ge(row_exp, 1)
            log1p_of(t2, ff, b_, nm, lf)
            then(dve.tensor_scalar(t3, t3, 0.0, None, ALU.min))
            then(dve.tensor_tensor(lf, t3, lf, ALU.subtract))

            def scan(out, src, op0, op1, first, init):
                for d in range(2):
                    pp = slice(32 * d, 32 * d + 4)
                    for lo, hi in ((0, P), (P, T)):
                        sl = slice(lo, hi) if d == 0 else slice(hi - 1, lo - 1 if lo else None, -1)
                        i0 = m0[pp, :] if init and lo else 0.0
                        f_ = cst[pp, C_ONE:C_ONE + hi - lo] if first is None else first[pp, sl]
                        ins = dve.tensor_tensor_scan(out[pp, sl], f_, src[pp, sl], i0, op0, op1)
                then(ins)

            then(dve.memset(b_, 0.0))
            scan(b_, lf, ALU.mult, ALU.add, None, False)
            then(dve.tensor_tensor(rows[:, 0, :], ig, b_, ALU.subtract))
            scan(nm, rows[:, 0, :], ALU.max, ALU.max, rows[:, 0, :], True)
            then(dve.tensor_tensor(t2, b_, nm, ALU.add))
            dve.tensor_scalar(nm, nm, -1.0, None, ALU.mult).then_inc(rows_m, 1)
            dve.wait_ge(rows_turned2, 1)
            then(dve.tensor_copy(colr[:, :, :], bank[6][:, 0:324].rearrange("p (k r) -> p k r", k=9)))
            dve.tensor_scalar(colr[:, WST:WST + 2, :], colr[:, WST:WST + 2, :], C_SCALE, None, ALU.mult)\
               .then_inc(colr_ready, 1)

            def mlstm_logs(u):
                h, d = munits[u]
                q, r = u % 2, 32 * d + h
                dve.wait_ge(nm_done, u + 1)
                for b, (s_, t, o_) in enumerate(blocks[d]):
                    src = bank[2 + q][:, P * t:P * t + P]
                    a_ = colr[:, ALOG + s_, r:r + 1]
                    mk = C_MF if d == 0 else C_MB
                    if s_ == t:
                        ins = dve.scalar_tensor_tensor(out=wt[:, q, o_:o_ + P], in0=src, scalar=a_,
                                                       in1=cst[:, mk:mk + P], op0=ALU.add, op1=ALU.min)
                    else:
                        ins = dve.tensor_scalar(wt[:, q, o_:o_ + P], src, a_, 0.0, ALU.add, ALU.min)
                ins.then_inc(wlog_ready, 1)

            dve.wait_ge(colr_ready, 1)
            dve.wait_ge(ktok_kept, 1)
            wait_kept(dve, index[("o", 2)])

            def mlstm_weigh(u):
                h, d = munits[u]
                q, r = u % 2, 32 * d + h
                dve.wait_ge(st_done, h + 1)
                dve.wait_ge(w_ready, u + 1)
                cut_ = 3 * P if d == 0 else 2 * P
                lo2 = P if d == 0 else 0
                dve.scalar_tensor_tensor(out=sw[:, q, 0:cut_], in0=bank[0][:, 0:cut_], scalar=C_SCALE,
                                         in1=wt[:, q, 0:cut_], op0=ALU.mult, op1=ALU.mult)
                dve.scalar_tensor_tensor(out=sw[:, q, cut_:512], in0=bank[1][:, lo2:256], scalar=C_SCALE,
                                         in1=wt[:, q, cut_:512], op0=ALU.mult, op1=ALU.mult).then_inc(sw_ready, 1)
                dve.tensor_scalar(kws[:, q, :], ktok[:, h, :], colr[:, WS, r:r + 1], None, ALU.mult)\
                   .then_inc(kws_ready, 1)

            mlstm_logs(0)
            mlstm_weigh(0)
            mlstm_logs(1)
            for u, (h, d) in enumerate(munits):
                q, r = u % 2, 32 * d + h
                if u + 1 < 8:
                    mlstm_weigh(u + 1)
                dve.wait_ge(inter_kept, 2 * (u + 1))
                dve.wait_ge(cout_kept, u + 1)
                dve.tensor_copy(fincols[:, 4 * d + h:4 * d + h + 1], cout[:, q, P:P + 1]).then_inc(fin_ready, 1)
                then(dve.tensor_tensor(num[:, :], bank[4 + q][:, 129:387], inter[:, q, :], ALU.add))

                def row(t):
                    return bank[4 + q][:, 0:129] if t == 0 else num[:, 129 * (t - 1):129 * t]

                for t in range(NT):
                    ins = dve.tensor_scalar(den[:, 0, t:t + 1], row(t)[:, P:P + 1], -1.0, colr[:, ENM + t, r:r + 1],
                                            ALU.mult, ALU.max)
                then(ins)
                for t in range(NT):
                    ins = dve.tensor_tensor(den[:, 0, t:t + 1], den[:, 0, t:t + 1], row(t)[:, P:P + 1], ALU.max)
                then(ins)
                then(dve.reciprocal(den[:, 1, :], den[:, 0, :]))
                for t in range(NT):
                    dst = heads[:, t, P * h:P * h + P]
                    if d == 0:
                        ins = dve.tensor_scalar(dst, row(t)[:, 0:P], den[:, 1, t:t + 1], None, ALU.mult)
                    else:
                        ins = dve.scalar_tensor_tensor(out=dst, in0=row(t)[:, 0:P], scalar=den[:, 1, t:t + 1],
                                                       in1=dst, op0=ALU.mult, op1=ALU.add)
                ins.then_inc(h_ready, 1)
                if u < 7:
                    dve.wait_ge(h_ready, u + 1)
                if u < 6:
                    mlstm_logs(u + 2)
            dve.wait_ge(h_ready, 8)
            head_norm(1, sq_odd, sigo)
            turned_heads(1)
            norm_out(2)

            norm_in(3)
            dve.wait_ge(logits_done, 1)
            dve.wait_ge(router_in, 32)
            then(dve.tensor_tensor(lg[:, :, :], bank[6][:, 0:24].rearrange("p (t e) -> p t e", t=NT),
                                   rb[:, :].unsqueeze(1).to_broadcast([P, NT, N_EXP]), ALU.add))
            tie = cst[:, C_TIE:C_TIE + 64].rearrange("p (e j) -> p e j", e=N_EXP)
            for t in range(NT):
                lj = lg[:, t, :].unsqueeze(1).to_broadcast([P, N_EXP, N_EXP])
                le = lg[:, t, :].unsqueeze(2).to_broadcast([P, N_EXP, N_EXP])
                gt_, eq_ = (cmp[:, k, :].rearrange("p (e j) -> p e j", e=N_EXP) for k in range(2))
                then(dve.tensor_tensor(gt_, lj, le, ALU.is_gt))
                then(dve.tensor_tensor(eq_, lj, le, ALU.is_equal))
                then(dve.tensor_tensor(eq_, eq_, tie, ALU.mult))
                then(dve.tensor_tensor(gt_, gt_, eq_, ALU.add))
                then(dve.tensor_reduce(rank[:, t, :], gt_, AX.X, ALU.add))
            then(dve.tensor_scalar(oh[:, 0, :, :], rank[:, :, :], 0.0, None, ALU.is_equal))
            then(dve.tensor_scalar(oh[:, 1, :, :], rank[:, :, :], 1.0, None, ALU.is_equal))
            dve.tensor_tensor(oh[:, 2, :, :], oh[:, 0, :, :], oh[:, 1, :, :], ALU.add).then_inc(sel_ready, 1)

            def pick(dst, which, src):
                then(dve.tensor_tensor(rank[:, :, :], oh[:, which, :, :], src, ALU.mult))
                return dve.tensor_reduce(tk[:, dst, :], rank[:, :, :], AX.X, ALU.add)

            then(pick(0, 0, lg[:, :, :]))
            then(pick(1, 1, lg[:, :, :]))
            dve.tensor_tensor(tk[:, 4, :], tk[:, 1, :], tk[:, 0, :], ALU.subtract).then_inc(e1_in, 1)
            dve.wait_ge(e1_ready, 1)
            then(dve.tensor_scalar(tk[:, 7, :], tk[:, 5, :], 1.0, None, ALU.add))
            then(dve.reciprocal(tk[:, 6, :], tk[:, 7, :]))
            then(dve.tensor_tensor(tk[:, 7, :], tk[:, 5, :], tk[:, 6, :], ALU.mult))
            dve.wait_ge(pos_done, 1)
            cnt = bank[7][:, 24:32]
            then(dve.tensor_scalar(nb[:, 0, :], cnt, 0.0, None, ALU.is_gt))
            for j in range(1, NT):
                then(dve.scalar_tensor_tensor(out=nb[:, 0, :], in0=cnt, scalar=float(P * j), in1=nb[:, 0, :],
                                              op0=ALU.is_gt, op1=ALU.add))
            then(dve.tensor_tensor_scan(nb[:, 1, :], cst[:, C_ONE:C_ONE + N_EXP], nb[:, 0, :], 0.0, ALU.mult, ALU.add))
            then(dve.tensor_tensor(nb[:, 2, :], nb[:, 1, :], nb[:, 0, :], ALU.subtract))
            then(dve.tensor_scalar(nb[:, 3, :], nb[:, 2, :], float(P), None, ALU.mult))
            then(dve.tensor_tensor(gp[:, :, :], bank[7][:, 0:24].rearrange("p (t e) -> p t e", t=NT),
                                   nb[:, 3, :].unsqueeze(1).to_broadcast([P, NT, N_EXP]), ALU.add))
            then(pick(2, 0, gp[:, :, :]))
            then(pick(3, 1, gp[:, :, :]))
            wv = ewf[:, :].rearrange("p (w e) -> p w e", e=N_EXP)
            then(dve.tensor_tensor(wv, nb[0:1, 1, :].unsqueeze(1).to_broadcast([1, MAX_ITEMS, N_EXP]),
                                   cst[0:1, C_W:C_N].rearrange("p (w e) -> p w e", e=N_EXP), ALU.is_le))
            then(dve.tensor_reduce(ew1[:, 0:MAX_ITEMS], wv, AX.X, ALU.add))
            then(dve.tensor_scalar(ew1[:, 0:MAX_ITEMS], ew1[:, 0:MAX_ITEMS], float(N_EXP - 1), None, ALU.min))
            then(dve.tensor_copy(ew1[:, MAX_ITEMS:MAX_ITEMS + 1], nb[0:1, 1, N_EXP - 1:N_EXP]))
            dve.tensor_copy(ewi[:, :], ew1[:, :]).then_inc(plan_ready, 1)
            then(dve.tensor_copy(slot[:, :], cst[:, C_IOTA:C_IOTA + P]))

            def hot(step):
                for t in range(NT):
                    step(dve.tensor_scalar(onehot[:, t, :], slot[:, :], tk[:, 2, t:t + 1], None, ALU.is_equal), 0)
                    step(dve.tensor_scalar(gated[:, t, :], slot[:, :], tk[:, 2, t:t + 1], tk[:, 6, t:t + 1],
                                           ALU.is_equal, ALU.mult), 0)
                    step(dve.tensor_scalar(gtmp[:, t, :], slot[:, :], tk[:, 3, t:t + 1], tk[:, 7, t:t + 1],
                                           ALU.is_equal, ALU.mult), 1)
                for t in range(NT):
                    step(dve.scalar_tensor_tensor(out=onehot[:, t, :], in0=slot[:, :], scalar=tk[:, 3, t:t + 1],
                                                  in1=onehot[:, t, :], op0=ALU.is_equal, op1=ALU.add), 0)
                    ins = dve.tensor_tensor(gated[:, t, :], gated[:, t, :], gtmp[:, t, :], ALU.add)
                    if t < NT - 1:
                        step(ins, 0)
                ins.then_inc(hot_ready, 1)

            hot(lambda ins, w_: then(ins))
            dve.wait_ge(plan_ready, 1)
            n_work = dve.value_load(ewi[0:1, MAX_ITEMS:MAX_ITEMS + 1], min_val=1, max_val=MAX_ITEMS)
            dve.wait_ge(zeroed, 11)
            dve.memset(jk[:, 1, 0:1], 0.0).then_inc(yadd, 1)
            with dve.Fori(0, n_work) as w:
                c_ = [0]

                def chain(ins, w_=1):
                    c_[0] += 1
                    ins.then_inc(item_step, 1)
                    dve.wait_ge(item_step, w * ITEM_STEPS + c_[0])


                def split_lo(j, h):
                    dve.wait_ge(whi_ready, w * (2 * ITEM) + (KF + 2 * j + h + 1))
                    dve.tensor_tensor(e_half(j, h, low=True), e_half(j, h), whi_moe[(2 * j + h) % WHI],
                                      ALU.subtract).then_inc(wlo_ready, 1)

                def act_lo(j):
                    dve.wait_ge(aeh_ready, w * UP + (j + 1))
                    dve.tensor_tensor(ael[:, 2 * j:2 * j + 2, :],
                                      bank[2 + j % 2][:, 0:256].rearrange("p (f s) -> p f s", f=2),
                                      aeh[:, 2 * j:2 * j + 2, :], ALU.subtract).then_inc(ael_ready, 1)

                split_lo(0, 0)
                split_lo(0, 1)
                for b in range(2):
                    dve.wait_ge(xgh_ready, w * 2 + (b + 1))
                    dve.tensor_tensor(xgl[:, 4 * b:4 * b + 4, :],
                                      bank[6 + b][:, :].rearrange("p (k s) -> p k s", k=4),
                                      xgh[:, 4 * b:4 * b + 4, :], ALU.subtract).then_inc(xgl_ready, 1)
                split_lo(1, 0)
                split_lo(1, 1)
                dve.wait_ge(gated_turned, w + 1)
                dve.tensor_copy(scat[:, :, :], bank[4][:, 0:T].rearrange("p (t s) -> p t s", t=NT))\
                   .then_inc(scat_ready, 1)
                for j in range(UP):
                    split_lo(j + 2, 0)
                    dve.wait_ge(esilu_ready, w * UP + (j + 1))
                    if j >= 2:
                        dve.wait_ge(act_turned, w * UP + (j - 1))
                    dve.tensor_tensor(a_tok[:, j % 2, :], sil_e[:, j % 2, :], bank[j % 2][:, 256:512], ALU.mult)\
                       .then_inc(eprod_ready, 1)
                    split_lo(j + 2, 1)
                    if j:
                        act_lo(j - 1)
                act_lo(UP - 1)
                for j in range(UP + 2, ITEM):
                    split_lo(j, 0)
                    split_lo(j, 1)
                dve.wait_ge(hot_ready, w + 1)
                chain(dve.tensor_scalar(slot[:, :], slot[:, :], float(P), None, ALU.add))
                hot(chain)
                for j, (t, b) in enumerate(SCATTER):
                    dve.wait_ge(scat_done, w * 6 + (j + 1))
                    v = yacc[:, t, 512 * b:512 * b + 512]
                    dve.tensor_tensor(v, v, bank[SCAT_BANK[j]][:, :], ALU.add).then_inc(yadd, 1)
                assert c_[0] == ITEM_STEPS, c_[0]
            dve.memset(jk[:, 1, 0:1], 0.0).then_inc(yacc_ready, 1)
            norm_out(3)


_INS = ["x_prompt", "x_sample", "c", "cache_a_k", "cache_a_v", "cache_b_k", "cache_b_v", "state_c_C", "state_c_n",
        "state_c_m", "state_d_h", "c_ctx", "mod_w", "mod_b", "norm_g", "w_in_even", "w_out_even", "a_lam",
        "a_subln_g", "b_rpb", "ff_w1", "ff_w3", "ff_w2", "w_in_odd", "c_gate_b", "conv_c", "conv_d", "conv_d_b",
        "rg_wa", "rg_ba", "rg_wx", "rg_bx", "rg_lam", "c_norm_g", "w_out_odd", "router_w", "router_b",
        "moe_w1", "moe_w3", "moe_w2"]
_OUTS = [(1, 128, 1024), (1, 256, 1024), (1, 1, 128, 4, 128), (1, 1, 128, 4, 128), (1, 1, 128, 8, 64),
         (1, 1, 128, 8, 64), (1, 1, 2, 4, 128, 128), (1, 1, 2, 4, 128), (1, 1, 2, 4), (1, 1, 2, 512)]


def kernel(**inputs):
    import concourse.bacc as _bacc
    from concourse.bass_utils import run_bass_kernel_spmd as _run

    nc = _bacc.Bacc("TRN2", target_bir_lowering=False, num_devices=1)
    arrays, aps = {}, {}
    for name in _INS:
        a = np.ascontiguousarray(inputs[name])
        arrays[f"in_{name}_dram"] = a
        aps[name] = nc.dram_tensor(f"in_{name}_dram", a.shape, F32, kind="ExternalInput").ap()
    table = shape_constants()
    arrays["in_shape_constants_dram"] = table
    aps["shape_constants"] = nc.dram_tensor("in_shape_constants_dram", table.shape, F32, kind="ExternalInput").ap()
    outs = [nc.dram_tensor(f"out_{i}_dram", s, F32, kind="ExternalOutput").ap() for i, s in enumerate(_OUTS)]
    trunk_step(nc, aps, outs)
    r = _run(nc, [arrays], core_ids=[0])
    return tuple(r.results[0][f"out_{i}_dram"] for i in range(len(_OUTS)))
```
